# Optimizing a Trainium2 kernel written in Bass

```python
import math
import jax, jax.numpy as jnp
from jax import lax
import numpy as np

D_MODEL = 1024
BATCH = 1
SEQ = 128
DEPTH = 2
DEC_BATCH = 1
DEC_SEQ = 256
PAST_LEN = 128

GRID_W = 64
POOL_WIDTH = D_MODEL // 4
POOL_WINDOWS = (2, 4, 8, 16)
POOL_GROUPS = len(POOL_WINDOWS)
POOL_GC = POOL_WIDTH // POOL_GROUPS
ATTN_HEADS = 4
HEAD_DIM = 64
V_DIM = 2 * HEAD_DIM
ATTN_WIDTH = ATTN_HEADS * V_DIM
QK_WIDTH = ATTN_HEADS * 2 * HEAD_DIM
CONV_WIDTH = D_MODEL - POOL_WIDTH - ATTN_WIDTH
CONV_K = 31
MIX_WIDTH = POOL_WIDTH + ATTN_WIDTH + CONV_WIDTH
IN_WIDTH = POOL_WIDTH + 2 * QK_WIDTH + ATTN_WIDTH + 2 * CONV_WIDTH
AXIS_DIM = HEAD_DIM // 2
ROPE_THETA = 10000.0
N_GROUPS = 4
EXPERTS_PER_GROUP = 8
N_EXPERTS = N_GROUPS * EXPERTS_PER_GROUP
TOP_K = 2
EXPERT_FF = D_MODEL // 4
ALPHA = (2 * DEPTH) ** 0.25
BETA = (8 * DEPTH) ** -0.25
LN_EPS = 1e-5
Q_BLOCK = 128

kernel_name = "hybrid_pool_diffattn_conformer_hmoe_step"

def layer_norm(x, g, b):
    x32 = x.astype(jnp.float32)
    mu = jnp.mean(x32, axis=-1, keepdims=True)
    var = jnp.mean(jnp.square(x32 - mu), axis=-1, keepdims=True)
    return ((x32 - mu) * lax.rsqrt(var + LN_EPS) * g + b).astype(x.dtype)

def rope_tables(L):
    rows = L // GRID_W
    row_id = jnp.repeat(jnp.arange(rows), GRID_W).astype(jnp.float32)
    col_id = jnp.tile(jnp.arange(GRID_W), rows).astype(jnp.float32)
    inv = ROPE_THETA ** (-jnp.arange(0, AXIS_DIM, 2, dtype=jnp.float32) / AXIS_DIM)
    ang = jnp.stack([row_id[:, None] * inv, col_id[:, None] * inv], axis=1)
    ang = ang[None, :, None, None, :, None, :]
    return jnp.cos(ang), jnp.sin(ang)

def apply_rope(x, cos, sin):
    xs = x.reshape(x.shape[:-1] + (2, 2, AXIS_DIM // 2))
    rot = jnp.stack([-xs[..., 1, :], xs[..., 0, :]], axis=-2)
    return (xs * cos + rot * sin).astype(x.dtype).reshape(x.shape)

def multiscale_pool(a, w_pool, pool_scale):
    B, L, _ = a.shape
    a32 = a.astype(jnp.float32)
    cs = jnp.concatenate([jnp.zeros((B, 1, POOL_WIDTH), jnp.float32), jnp.cumsum(a32, axis=1)], axis=1)
    t = jnp.arange(L)
    means = []
    for g, w in enumerate(POOL_WINDOWS):
        lo = jnp.clip(t - w // 2, 0, L)
        hi = jnp.clip(t + w // 2, 0, L)
        sl = slice(g * POOL_GC, (g + 1) * POOL_GC)
        s = cs[:, hi, sl] - cs[:, lo, sl]
        means.append(s / (hi - lo).astype(jnp.float32)[None, :, None])
    pooled = jnp.stack(means, axis=2) - a32.reshape(B, L, POOL_GROUPS, POOL_GC)
    mixed = jnp.einsum('blgc,gcd->blgd', pooled.astype(a.dtype), w_pool)
    return mixed.reshape(B, L, POOL_WIDTH) * pool_scale

def diff_attention(q, k, v, lam):
    B, Lq = q.shape[:2]
    nb = Lq // Q_BLOCK
    qb = q.reshape(B, nb, Q_BLOCK, ATTN_HEADS, 2, HEAD_DIM).transpose(1, 0, 2, 3, 4, 5)
    scale = 1.0 / math.sqrt(HEAD_DIM)

    def one_block(qblk):
        s = jnp.einsum('bqhmd,bkhmd->bhmqk', qblk, k).astype(jnp.float32) * scale
        p = jax.nn.softmax(s, axis=-1)
        a = p[:, :, 0] - lam * p[:, :, 1]
        return jnp.einsum('bhqk,bkhe->bqhe', a.astype(v.dtype), v)

    out = lax.map(one_block, qb)
    return out.transpose(1, 0, 2, 3, 4).reshape(B, Lq, ATTN_HEADS, V_DIM)

def conformer_conv(c_in, dw, ln_g, ln_b, pw):
    a, b = jnp.split(c_in, 2, axis=-1)
    h = a * jax.nn.sigmoid(b)
    h = lax.conv_general_dilated(h, dw[:, None, :], window_strides=(1,),
                                 padding=[(CONV_K // 2, CONV_K // 2)],
                                 dimension_numbers=('NWC', 'WIO', 'NWC'),
                                 feature_group_count=CONV_WIDTH)
    h = jax.nn.silu(layer_norm(h, ln_g, ln_b))
    return h @ pw

def token_mixer(u, p, lam_init, rope, ctx_kv):
    B, L, _ = u.shape
    proj = u @ p['w_in']
    o1 = POOL_WIDTH
    o2 = o1 + QK_WIDTH
    o3 = o2 + QK_WIDTH
    o4 = o3 + ATTN_WIDTH
    a_in, q, k, v, c_in = jnp.split(proj, [o1, o2, o3, o4], axis=-1)
    y_pool = multiscale_pool(a_in, p['pool_w'], p['pool_scale'])
    q = q.reshape(B, L, ATTN_HEADS, 2, HEAD_DIM)
    k = k.reshape(B, L, ATTN_HEADS, 2, HEAD_DIM)
    v = v.reshape(B, L, ATTN_HEADS, V_DIM)
    if rope is not None:
        cos, sin = rope
        q = apply_rope(q, cos, sin)
        k_att = apply_rope(k, cos, sin)
    else:
        k_att = k
    if ctx_kv is not None:
        k_att = jnp.concatenate([k_att, ctx_kv[0]], axis=1)
        v_att = jnp.concatenate([v, ctx_kv[1]], axis=1)
    else:
        v_att = v
    lp = p['diff_lambda'].astype(jnp.float32)
    lam = jnp.exp(jnp.sum(lp[0] * lp[1])) - jnp.exp(jnp.sum(lp[2] * lp[3])) + lam_init
    o = diff_attention(q, k_att, v_att, lam).astype(jnp.float32)
    o = o * lax.rsqrt(jnp.mean(jnp.square(o), axis=-1, keepdims=True) + LN_EPS) * p['subln_g'] * (1.0 - lam_init)
    y_attn = o.astype(u.dtype).reshape(B, L, ATTN_WIDTH)
    y_conv = conformer_conv(c_in, p['conv_dw'], p['conv_ln_g'], p['conv_ln_b'], p['conv_pw'])
    y = jnp.concatenate([y_pool.astype(u.dtype), y_attn, y_conv.astype(u.dtype)], axis=-1) @ p['w_out']
    return y, k, v

def hier_moe(u, p):
    B, L, D = u.shape
    t = u.reshape(-1, D)
    g_logits = (t @ p['router_grp']).astype(jnp.float32) + p['router_grp_b']
    g_prob = jax.nn.softmax(g_logits, axis=-1)
    g_w, g_idx = lax.top_k(g_prob, 1)
    e_logits = ((t @ p['router_exp']).astype(jnp.float32) + p['router_exp_b']).reshape(-1, N_GROUPS, EXPERTS_PER_GROUP)
    e_sel = jnp.take_along_axis(e_logits, g_idx[:, :, None], axis=1)[:, 0]
    top_v, top_i = lax.top_k(e_sel, TOP_K)
    w = g_w * jax.nn.softmax(top_v, axis=-1)
    ids = g_idx * EXPERTS_PER_GROUP + top_i
    comb = jnp.einsum('nk,nke->ne', w, jax.nn.one_hot(ids, N_EXPERTS, dtype=jnp.float32))
    h = jax.nn.silu(jnp.einsum('nd,edf->nef', t, p['w_gate'])) * jnp.einsum('nd,edf->nef', t, p['w_up'])
    y = jnp.einsum('nef,efd->nd', h * comb[:, :, None].astype(h.dtype), p['w_down'])
    return y.reshape(B, L, D)

def trunk_layer(x, mod, p, lam_init, rope, ctx_kv):
    shift1, scale1, gate1, shift2, scale2, gate2 = jnp.split(mod[:, None, :].astype(x.dtype), 6, axis=-1)
    u = x * (1 + scale1) + shift1
    y, k, v = token_mixer(u, p, lam_init, rope, ctx_kv)
    x = layer_norm(ALPHA * x + gate1 * y, p['ln1_g'], p['ln1_b'])
    u = x * (1 + scale2) + shift2
    x = layer_norm(ALPHA * x + gate2 * hier_moe(u, p), p['ln2_g'], p['ln2_b'])
    return x, k, v

def setup_inputs(seed: int = 0) -> dict:
    key = jax.random.key(seed)
    ks = jax.random.split(key, 32)
    f = jnp.float32
    n = lambda i, shape, s: jax.random.normal(ks[i], shape, f) * s
    return {
        'x_prompt': n(0, (BATCH, SEQ, D_MODEL), 1.0),
        'x_sample': n(1, (DEC_BATCH, DEC_SEQ, D_MODEL), 1.0),
        'cache_k': n(2, (DEC_BATCH, DEPTH, PAST_LEN, ATTN_HEADS, 2, HEAD_DIM), 1.0),
        'cache_v': n(3, (DEC_BATCH, DEPTH, PAST_LEN, ATTN_HEADS, V_DIM), 1.0),
        'c': n(4, (DEC_BATCH, D_MODEL), 1.0),
        'c_ctx': n(5, (D_MODEL,), 1.0),
        'w_mod': n(6, (DEPTH, D_MODEL, 6 * D_MODEL), D_MODEL ** -0.5),
        'b_mod': n(7, (DEPTH, 6 * D_MODEL), 0.02),
        'w_in': n(8, (DEPTH, D_MODEL, IN_WIDTH), D_MODEL ** -0.5),
        'w_out': n(9, (DEPTH, MIX_WIDTH, D_MODEL), BETA * MIX_WIDTH ** -0.5),
        'pool_w': n(10, (DEPTH, POOL_GROUPS, POOL_GC, POOL_GC), POOL_GC ** -0.5),
        'pool_scale': 1.0 + n(11, (DEPTH, POOL_WIDTH), 0.1),
        'diff_lambda': n(12, (DEPTH, 4, HEAD_DIM), 0.1),
        'subln_g': 1.0 + n(13, (DEPTH, V_DIM), 0.1),
        'conv_dw': n(14, (DEPTH, CONV_K, CONV_WIDTH), CONV_K ** -0.5),
        'conv_ln_g': 1.0 + n(15, (DEPTH, CONV_WIDTH), 0.1),
        'conv_ln_b': n(16, (DEPTH, CONV_WIDTH), 0.02),
        'conv_pw': n(17, (DEPTH, CONV_WIDTH, CONV_WIDTH), CONV_WIDTH ** -0.5),
        'ln1_g': 1.0 + n(18, (DEPTH, D_MODEL), 0.1),
        'ln1_b': n(19, (DEPTH, D_MODEL), 0.02),
        'ln2_g': 1.0 + n(20, (DEPTH, D_MODEL), 0.1),
        'ln2_b': n(21, (DEPTH, D_MODEL), 0.02),
        'router_grp': n(22, (DEPTH, D_MODEL, N_GROUPS), D_MODEL ** -0.5),
        'router_grp_b': n(23, (DEPTH, N_GROUPS), 0.01),
        'router_exp': n(24, (DEPTH, D_MODEL, N_EXPERTS), D_MODEL ** -0.5),
        'router_exp_b': n(25, (DEPTH, N_EXPERTS), 0.01),
        'w_gate': n(26, (DEPTH, N_EXPERTS, D_MODEL, EXPERT_FF), D_MODEL ** -0.5),
        'w_up': n(27, (DEPTH, N_EXPERTS, D_MODEL, EXPERT_FF), D_MODEL ** -0.5),
        'w_down': n(28, (DEPTH, N_EXPERTS, EXPERT_FF, D_MODEL), BETA * EXPERT_FF ** -0.5),
    }

def reference(x_prompt, x_sample, cache_k, cache_v, c, c_ctx, w_mod, b_mod, w_in, w_out,
              pool_w, pool_scale, diff_lambda, subln_g, conv_dw, conv_ln_g, conv_ln_b, conv_pw,
              ln1_g, ln1_b, ln2_g, ln2_b, router_grp, router_grp_b, router_exp, router_exp_b,
              w_gate, w_up, w_down):
    rope = rope_tables(x_sample.shape[1])
    silu_ctx = jax.nn.silu(c_ctx)[None]
    silu_c = jax.nn.silu(c)
    xp, xs = x_prompt, x_sample
    new_k, new_v = [], []
    for l in range(DEPTH):
        p = {
            'w_in': w_in[l], 'w_out': w_out[l], 'pool_w': pool_w[l], 'pool_scale': pool_scale[l],
            'diff_lambda': diff_lambda[l], 'subln_g': subln_g[l], 'conv_dw': conv_dw[l],
            'conv_ln_g': conv_ln_g[l], 'conv_ln_b': conv_ln_b[l], 'conv_pw': conv_pw[l],
            'ln1_g': ln1_g[l], 'ln1_b': ln1_b[l], 'ln2_g': ln2_g[l], 'ln2_b': ln2_b[l],
            'router_grp': router_grp[l], 'router_grp_b': router_grp_b[l],
            'router_exp': router_exp[l], 'router_exp_b': router_exp_b[l],
            'w_gate': w_gate[l], 'w_up': w_up[l], 'w_down': w_down[l],
        }
        lam_init = 0.8 - 0.6 * math.exp(-0.3 * l)
        mod_ctx = silu_ctx @ w_mod[l] + b_mod[l]
        xp, k_l, v_l = trunk_layer(xp, mod_ctx, p, lam_init, None, None)
        new_k.append(k_l)
        new_v.append(v_l)
        mod_lat = silu_c @ w_mod[l] + b_mod[l]
        xs, _, _ = trunk_layer(xs, mod_lat, p, lam_init, rope, (cache_k[:, l], cache_v[:, l]))
    new_cache_k = jnp.stack(new_k, axis=1)
    new_cache_v = jnp.stack(new_v, axis=1)
    return (xp, xs, new_cache_k, new_cache_v)


_drawn_inputs = setup_inputs


def setup_inputs(seed=0):
    import zlib

    import numpy as np

    out = dict(_drawn_inputs(seed))
    spreads = {}
    factors = {'diff_lambda': 4.852,
     'conv_ln_b': 8.0,
     'router_grp_b': 6.839,
     'router_exp_b': 14.293,
     'conv_ln_g': 2.851}
    for name, (base, spread) in spreads.items():
        noise = np.random.default_rng([zlib.crc32(name.encode()), seed]).standard_normal(out[name].shape)
        drawn = base * np.exp(spread * noise) if base else spread * noise
        out[name] = __import__('jax').numpy.asarray(drawn.astype(out[name].dtype))
    for name, factor in factors.items():
        out[name] = (out[name] * factor).astype(out[name].dtype)
    return out
```

```python
from contextlib import ExitStack
import math

import numpy as np
import concourse.bass as bass
from concourse import mybir

F32 = mybir.dt.float32
I32 = mybir.dt.int32
ALU = mybir.AluOpType
ACT = mybir.ActivationFunctionType
AX = mybir.AxisListType.X
ds = bass.ds

P = 128
D = 1024
DEPTH = 2
SEQ = 128
LAT = 256
PAST = 128
T = SEQ + LAT
NT = T // P
KD = D // P
GRID_W = 64
POOL = D // 4
HEADS = 4
HD = 64
VD = 2 * HD
QK = HEADS * 2 * HD
AW = HEADS * VD
CONV = D - POOL - AW
TAPS = 31
AXIS = HD // 2
NG = 4
EPG = 8
NE = NG * EPG
FF = D // 4
ALPHA = (2 * DEPTH) ** 0.25
EPS = 1e-5
PAIRS = 2 * T
ST = PAIRS // P
W = 96
PADDED = PAIRS + W
RING = 4
SLOT_COLS = 768
HALF = SLOT_COLS // 2
SLOT = KD * SLOT_COLS
NMOD = 6 * KD
MOD_LOADS = 6 * D // SLOT_COLS
MAX_CHUNKS = NE + (PAIRS - NE) // W
MAX_ROUNDS = -(-MAX_CHUNKS // RING)
BIG = 1e30

PP = 8
POOL_COLS = 2 * PP + SEQ + 2 * PP + LAT
POOL_LAT = 3 * PP + SEQ
POOL_N = POOL_COLS - 2 * PP
CP = TAPS // 2
GLU_COLS = 4 * CP + T
GLU_LAT = 3 * CP + SEQ
CONV_N = GLU_COLS - 2 * CP
CONV_LAT = 2 * CP + SEQ

VECS = [("b_mod", NMOD), ("pool_scale", POOL // P), ("subln_g", 1), ("conv_ln_g", CONV // P),
        ("conv_ln_b", CONV // P), ("ln1_g", KD), ("ln1_b", KD), ("ln2_g", KD), ("ln2_b", KD)]
VCOL, NVEC = {}, 0
for _name, _n in VECS:
    VCOL[_name] = NVEC
    NVEC += _n

CONST_COLS = [("ident", P), ("ones", P), ("rot", P), ("cos", LAT), ("sin", LAT),
              ("rank", NE), ("kk", 1), ("rounds", MAX_ROUNDS), ("inv", 2 * POOL_N)]


def shape_constants():
    c = {}
    c["ident"] = np.eye(P)
    c["tri"] = np.triu(np.ones((P, P)), 1)
    c["ones"] = np.ones((P, P))
    rot = np.zeros((P, P))
    half = AXIS // 2
    for j in range(P):
        if (j // half) % 2 == 0:
            rot[j + half, j] = -1.0
        else:
            rot[j - half, j] = 1.0
    c["rot"] = rot
    pos = np.arange(LAT)
    coord = np.stack([pos // GRID_W, pos % GRID_W]).astype(np.float32)
    inv = (np.float32(10000.0) ** (-np.arange(0, AXIS, 2, dtype=np.float32) / np.float32(AXIS))).astype(np.float32)
    p = np.arange(P)
    ang = coord[(p // AXIS) % 2, :] * inv[p % half][:, None]
    c["cos"] = np.cos(ang)
    c["sin"] = np.sin(ang)
    c["rank"] = np.tile(np.arange(NE, 0, -1), (P, 1))
    c["kk"] = np.arange(P)[:, None]
    c["rounds"] = np.tile(np.arange(MAX_ROUNDS) * RING, (P, 1))
    cnt = np.zeros((P, 2, POOL_N))
    for base, length in ((0, SEQ), (POOL_LAT - PP, LAT)):
        t = np.arange(length)
        for g, w in enumerate((2, 4, 8, 16)):
            n = np.clip(t + w // 2, 0, length) - np.clip(t - w // 2, 0, length)
            cnt[64 * (g % 2):64 * (g % 2) + 64, g // 2, base:base + length] = (1.0 / n)
    c["inv"] = cnt.reshape(P, 2 * POOL_N)
    table = np.concatenate([c[n].reshape(P, k) for n, k in CONST_COLS], axis=1).astype(np.float32)
    iota = np.concatenate([np.tile(np.arange(PAIRS), (P, 1)), c["tri"]], axis=1).astype(np.float32)
    lam = np.array([0.8 - 0.6 * math.exp(-0.3 * l) for l in range(DEPTH)])
    lam = np.stack([lam, 1.0 - lam], axis=-1)[:, None, :].repeat(P, axis=1).astype(np.float32)
    return table, iota, lam


class Signal:

    def __init__(self, sem, per_layer, step=1, credit=0):
        self.sem, self.per_layer, self.step, self.credit = sem, per_layer, step, credit

    def at(self, l, n):
        return (l * self.per_layer + n) * self.step + self.credit


class Steps:

    def __init__(self, signal):
        self.raised, self.n = signal, 0

    def add(self, ins):
        self.n += 1
        ins.then_inc(self.raised.sem, 1)
        return self.n

    def check(self):
        assert self.n == self.raised.per_layer, (self.raised.sem, self.n, self.raised.per_layer)


ACT_STEPS = 0
DVE_STEPS = 202


def build(nc, g, consts, iota_dram, lam_dram, y_prompt, y_sample, new_k, new_v):
    with ExitStack() as ctx:
        def sb(name, shape, dt=F32):
            return ctx.enter_context(nc.sbuf_tensor(name, shape, dt))

        def signal(name, per_layer, step=1, credit=0):
            return Signal(ctx.enter_context(nc.semaphore(name)), per_layer, step, credit)

        ring = sb("ring", [P, RING, SLOT])
        tail = sb("tail", [P, KD * 256])
        xT = sb("xT", [P, KD, T])
        uT = sb("uT", [P, KD, T])
        XS = max(KD * PADDED, NT * (D + PAIRS) + 2 * PAIRS)
        arena = sb("arena", [P, 2 * XS])
        PTw = sb("PTw", [P, ST, T])
        cst = sb("cst", [P, sum(n for _, n in CONST_COLS)])
        pool_blk = sb("pool_blk", [P, 2, P])
        conv_pw = sb("conv_pw", [P, 2, CONV])
        krow = sb("krow", [P, QK])
        vec_rows = sb("vec_rows", [NVEC, P])
        vec = sb("vec", [P, NVEC])
        dw = sb("dw", [P, 2, TAPS])
        router_w = sb("router_w", [P, KD, NG + NE])
        router_b = sb("router_b", [NG + NE, 1])
        modT = sb("modT", [P, NMOD, 2])
        sT = sb("sT", [P, KD, 2])
        lam_in = sb("lam_in", [1, 4, HD])
        lam_c = sb("lam_c", [P, 2])
        lam_s = sb("lam_s", [1, 4])
        nlam = sb("nlam", [P, 1])
        subg = sb("subg", [P, 1])
        epsc = sb("epsc", [P, 1])
        chunk_tab = sb("chunk_tab", [1, 2, MAX_ROUNDS * RING], I32)
        rounds_tab = sb("rounds_tab", [1, DEPTH], I32)
        before_f = sb("before_f", [1, DEPTH + 1])
        before_tab = sb("before_tab", [1, DEPTH + 1], I32)

        C, at = {}, 0
        for name, n in CONST_COLS:
            C[name] = cst[:, at:at + n]
            at += n
        ident = C["ident"]

        def place(base, *sizes):
            out, at = [], base
            for n in sizes:
                out.append(arena[:, at:at + n])
                at += n
            return out, at

        (mixT, qT, kT, ckT), end = place(0, KD * T, HEADS * T, HEADS * T, HEADS * PAST)
        assert end <= XS
        (vrow, cv, ck_rows, apad, glu, cacc, probs, dw_rows), end = place(
            XS, NT * AW, AW, QK, 2 * POOL_COLS, 2 * GLU_COLS, 2 * CONV_N, 4 * T, CONV)
        assert end <= 2 * XS
        mixT = mixT.rearrange("p (m t) -> p m t", m=KD)
        qT = qT.rearrange("p (h t) -> p h t", h=HEADS)
        kT = kT.rearrange("p (h t) -> p h t", h=HEADS)
        ckT = ckT.rearrange("p (h t) -> p h t", h=HEADS)
        vrow = vrow.rearrange("p (t n) -> p t n", t=NT)
        apad = apad.rearrange("p (c n) -> p c n", c=2)
        glu = glu.rearrange("p (c n) -> p c n", c=2)
        cacc = cacc.rearrange("p (c n) -> p c n", c=2)
        csil = arena[:, XS + NT * AW + AW + QK + 2 * POOL_COLS:][:, 0:2 * T].rearrange("p (c n) -> p c n", c=2)
        probs = probs.rearrange("p (b m n) -> p b m n", b=2, m=2)
        rope_t = probs.rearrange("p b m n -> p (b m n)")[:, 0:4 * LAT].rearrange("p (b n) -> p b n", b=4)
        uflat = uT[:].rearrange("p m t -> p (m t)")
        aT = uflat[:, 0:2 * T].rearrange("p (b k q) -> p b k q", b=2, k=NT)
        orow = uflat[:, 2 * T:2 * T + NT * AW].rearrange("p (t h e) -> p t h e", t=NT, h=HEADS)
        crow = uflat[:, 2 * T + NT * AW:2 * T + NT * AW + NT * CONV].rearrange("p (t n) -> p t n", t=NT)
        ptflat = PTw[:].rearrange("p s t -> p (s t)")
        sumX = ptflat[:, 0:2 * POOL_COLS].rearrange("p (c n) -> p c n", c=2)
        sumY = ptflat[:, 2 * POOL_COLS:4 * POOL_COLS].rearrange("p (c n) -> p c n", c=2)
        mrow = arena[0:2, 0:2 * HALF].rearrange("p (b n) -> p b n", b=2)
        XsT = arena[:, 0:KD * PADDED].rearrange("p (k n) -> p k n", k=KD)
        YsT = arena[:, XS:XS + KD * PADDED].rearrange("p (k n) -> p k n", k=KD)
        Ysr = arena[:, 0:ST * D].rearrange("p (s n) -> p s n", s=ST)
        urow = arena[:, XS:XS + NT * D].rearrange("p (t n) -> p t n", t=NT)
        Pm = arena[:, XS + NT * D:XS + NT * D + NT * PAIRS].rearrange("p (t n) -> p t n", t=NT)
        Pw = arena[:, XS + NT * (D + PAIRS):XS + NT * (D + PAIRS) + 2 * PAIRS].rearrange("p (t n) -> p t n", t=2)
        assert XS + NT * (D + PAIRS) + 2 * PAIRS <= 2 * XS
        sg = tail[:, 0:4 * W].rearrange("p (b f n) -> p b f n", b=2, f=2)
        assert 8 * W <= PAIRS
        hT = tail[:, 4 * W:8 * W].rearrange("p (b f n) -> p b f n", b=2, f=2)
        iota_tri = tail[:, PAIRS:2 * PAIRS + P]
        iota, tri = iota_tri[:, 0:PAIRS], iota_tri[:, PAIRS:]
        ln_t = arena[:, XS + NT * AW:XS + NT * AW + 4 * T].rearrange("p (b n) -> p b n", b=4)
        xrow = arena[:, 0:NT * D].rearrange("p (t n) -> p t n", t=NT)
        RT_COLS = NT * (NG + NE) + 2 * NT * NG + 4 * NT * NE
        at = [0]

        def rts(*shape):
            n = int(np.prod(shape))
            v = arena[:, at[0]:at[0] + n]
            at[0] += n
            return v if len(shape) == 1 else v.rearrange("p (a b) -> p a b", a=shape[0])
        lg = rts(NT, NG + NE)
        og, gtmp = rts(NT, NG), rts(NT, NG)
        o1, o2 = rts(NT, NE), rts(NT, NE)
        etmp, asg = rts(NT, NE), rts(NT, NE)
        r3 = sb("r3", [P, 15, NT])
        gmax, gsum, gw, m1, m2, cm, q, s1, s2, w1, w2, rq, gcm, c1, c2 = [r3[:, i, :] for i in range(15)]
        assert at[0] == RT_COLS
        tot, start, cb, le, dd, ce = [arena[:, RT_COLS + 33 * i:RT_COLS + 33 * (i + 1)] for i in range(6)]
        lgT = arena[0:NG + NE, RT_COLS + 198:RT_COLS + 198 + T]
        chk = sb("chk", [P, 4])
        small = sb("small", [P, 2, 2, 4])
        rnd = sb("rnd", [P, MAX_ROUNDS + 1])
        bstat = sb("bstat", [P, NT, 6])
        cstat = sb("cstat", [P, NT, 4])
        rms = sb("rms", [P, 2, NT * HEADS])

        ps = ctx.enter_context(nc.psum_tensor("ps", [P, 8, 512], F32))

        s_cst = signal("const_loaded", 0, 16)
        s_xin = signal("x_rows_loaded", 0, 16)
        s_cin = signal("cond_loaded", 0, 16)
        s_xt = signal("x_turned", 0)
        s_ctl = signal("tables_zeroed", 0)
        s_crow = signal("cond_rows_silu", 0)
        s_cT = signal("cond_transposed", 0)
        s_sT = signal("cond_ready", 0)
        s_zero = signal("zeros_written", 0)
        vec_loaded = signal("vec_loaded", len(VECS) + 2, 16)
        vec_ready = signal("vec_transposed", 1, credit=1)
        dw_ready = signal("taps_transposed", 1)
        vec_copied = signal("vec_copied", 1)
        lam_dot = signal("lambda_dots", 1)
        lam_exp = signal("lambda_exps", 1)
        lam_ready = signal("lambda_ready", 1, credit=1)
        lam_done = signal("lambda_copied", 1)
        mix_loaded = signal("mixer_params_loaded", 8, 16)
        rt_loaded = signal("router_loaded", 4, 16)
        iota_loaded = signal("iota_loaded", 1, 16)
        layer_x = signal("x_ready", KD)
        slot_done = [signal(f"slot_done{s}", 3, credit=1) for s in range(RING)]
        slot_loaded = [signal(f"slot_loaded{s}", 3, 32) for s in range(RING)]
        exp_loaded = [signal(f"expert_loaded{s}", 0, 16) for s in range(RING)]
        tail_loaded = signal("tail_loaded", 1, 16)
        tail_used = signal("tail_used", 1)
        mod_rows = signal("mod_rows", MOD_LOADS)
        mod_rows_copied = signal("mod_rows_copied", 2 * MOD_LOADS)
        mod_turned = signal("mod_turned", 2 * MOD_LOADS)
        mod_done = signal("mod_done", 1)
        u_act = signal("u_tiles_act", KD // 2)
        u_dve = signal("u_tiles_dve", KD // 2)
        proj_ready = signal("proj_ready", 14)
        proj_act = signal("proj_taken_act", 15)
        proj_dve = signal("proj_taken_dve", 2)
        rot_ready = signal("rot_ready", 8)
        roped = signal("roped", 8)
        ck_turned = signal("ck_turned", 2)
        ck_copied = signal("ck_copied", 2)
        lam_bc = signal("lambda_broadcast", 1)
        scores_ready = signal("scores_ready", 12)
        scores_used = signal("scores_used", 12)
        neg_max = signal("neg_max", 12)
        prob_ready = signal("prob_ready", 12)
        prob_turned = signal("prob_turned", 12)
        prob_copied = signal("prob_copied", 12)
        o_ready = signal("o_ready", 12)
        o_copied = signal("o_copied", 12)
        pads_zero = signal("pads_zero", 1)
        logits_T = signal("logits_columns", 1)
        logits_copied = signal("logits_columns_copied", 1)
        conv_done = signal("conv_done", 1)
        pool_done = signal("pool_sums_done", 1)
        pool_ready = signal("pool_mixed", 2)
        rms_var = signal("rms_mean_square", 1)
        rms_sd = signal("rms_root", 1)
        o_normed = signal("o_normed", 1)
        o_turned = signal("o_turned", HEADS)
        crow_ready = signal("conv_rows_turned", NT)
        cln_var = signal("conv_var", 1)
        cln_sd = signal("conv_root", 1)
        cln_done = signal("conv_rows_normed", 1)
        cback = signal("conv_turned_back", 2)
        csil_ready = signal("conv_silu", 2)
        cpw_ready = signal("conv_pointwise", 2)
        mix_ready = signal("mix_tiles", KD)
        y1_ready = signal("y1_ready", KD - 2)
        y2_ready = signal("y2_ready", KD)
        gated = signal("y_gated", 2 * KD)
        z_ready = signal("z_ready", 2 * KD)
        mean_ready = signal("mean_ready", 2)
        centred = signal("centred", 2 * KD)
        squared = signal("squared", 2 * KD)
        sq_used = signal("squares_used", 2 * KD)
        root_ready = signal("root_ready", 2)
        normed = signal("normed", 2 * KD)
        x_mid = signal("x_mid", KD)
        u2_ready = signal("u2_ready", KD)
        logits_ready = signal("logits_ready", 1)
        urow_turned = signal("urow_turned", 6)
        urow_ready = signal("urow_ready", 6)
        gdiff = signal("group_diff", 1)
        gexp = signal("group_exp", 1)
        ediff = signal("expert_diff", 1)
        eexp = signal("expert_exp", 1)
        assign_ready = signal("assignment", 1)
        ranks_ready = signal("ranks", 1)
        chunk_cols = signal("chunk_columns", 1)
        chunk_turned = signal("chunk_turned", 1)
        chunks_ready = signal("chunk_list", 1)
        P_ready = signal("gather_matrix", NT)
        Pw_ready = signal("weighted_matrix", NT)
        Pw_turned = signal("weighted_turned", 2 * NT)
        PT_ready = signal("unsort_matrix", 2 * NT)
        gath_ready = signal("gathered", 2 * KD)
        xs_act = signal("sorted_x_act", KD)
        xs_dve = signal("sorted_x_dve", KD)
        gu_ready = signal("gate_up_ready", 0)
        silu_ready = signal("silu_ready", 0)
        h_ready = signal("h_ready", 0)
        down_ready = signal("down_half_ready", 0)
        down_act = signal("down_taken_act", 0, credit=2)
        down_dve = signal("down_taken_dve", 0, credit=2)
        ys_turned = signal("ys_turned", 12, credit=1)
        ys_act = signal("ys_rows_act", 6)
        ys_dve = signal("ys_rows_dve", 6)
        out_k = signal("new_kv_stored", 2, 16)
        kv_free = signal("kv_rows_free", 1, credit=1)
        out_turned = signal("out_turned", 0)
        out_rows = signal("out_rows", 0)
        s_out = signal("y_stored", 0, 16)
        dve_self = signal("dve_step", DVE_STEPS)
        act_self = signal("act_step", ACT_STEPS)

        def engine_wait(eng):
            def wait(sig, l, n, alone=False):
                eng.wait_ge(sig.sem, sig.at(l, n))
                if alone:
                    eng.nop(nofuse=True)
            return wait

        w_mod, w_in, w_out = g["w_mod"], g["w_in"], g["w_out"]
        q0, k0, v0, c0 = POOL, POOL + QK, POOL + 2 * QK, POOL + 2 * QK + AW
        slot = [ring[:, s, :].rearrange("p (k n) -> p k n", k=KD) for s in range(RING)]
        gate_w = [ring[:, s, 0:KD * FF].rearrange("p (k f) -> p k f", k=KD) for s in range(RING)]
        up_w = [ring[:, s, KD * FF:2 * KD * FF].rearrange("p (k f) -> p k f", k=KD) for s in range(RING)]
        down_w = [ring[:, s, 2 * KD * FF:3 * KD * FF].rearrange("p (k n) -> p k n", k=2) for s in range(RING)]
        tail_w = tail[:].rearrange("p (k n) -> p k n", k=KD)
        SEGS = ((0, SEQ, 1), (SEQ, T, 0))
        SH1, SC1, GA1, SH2, SC2, GA2 = [i * KD for i in range(6)]

        def mod(i, v):
            return modT[:, i, v:v + 1]

        def vcol(name, i=0):
            return vec[:, VCOL[name] + i:VCOL[name] + i + 1]

        block = ctx.enter_context(nc.Block())

        @block.sync
        def _(sp):
            wait = engine_wait(sp)
            sp.dma_start(cst[:], consts).then_inc(s_cst.sem, 16)
            sp.dma_start(xrow[:, 0, :], g["x_prompt"][0]).then_inc(s_xin.sem, 16)
            sp.dma_start(xrow[:, 1:NT, :], g["x_sample"][0].rearrange("(t p) d -> p t d", p=P)).then_inc(s_xin.sem, 16)

            sp.wait_ge(s_ctl.sem, 1)
            with sp.Fori(0, DEPTH) as l:
                before = sp.value_load(before_tab[0:1, ds(l, 1)], min_val=0, max_val=DEPTH * MAX_ROUNDS)

                def load_slot(s, use, parts):
                    sp.wait_ge(slot_done[s].sem, before + l * 3 + (use + 1))
                    sp.nop(nofuse=True)
                    for dst, src in parts:
                        sp.dma_start(dst, src).then_inc(slot_loaded[s].sem, 16)

                def cols(w, a, b, k0_, k1_):
                    return w[ds(l, 1), k0_ * P:k1_ * P, a:b].rearrange("o (k p) n -> p (o k) n", p=P)

                h2 = KD // 2
                for j in range(MOD_LOADS):
                    s = j % RING
                    a = j * SLOT_COLS
                    load_slot(s, j // RING, [(slot[s][:, 0:h2, :], cols(w_mod, a, a + SLOT_COLS, 0, h2)),
                                             (slot[s][:, h2:KD, :], cols(w_mod, a, a + SLOT_COLS, h2, KD))])
                load_slot(0, 2, [(slot[0][:, :, POOL:SLOT_COLS], cols(w_in, c0, c0 + 2 * CONV, 0, KD)),
                                 (slot[0][:, :, 0:POOL], cols(w_in, 0, POOL, 0, KD))])
                for s in (1, 2):
                    a = q0 + (s - 1) * SLOT_COLS
                    load_slot(s, 2, [(slot[s][:, 0:h2, :], cols(w_in, a, a + SLOT_COLS, 0, h2)),
                                     (slot[s][:, h2:KD, :], cols(w_in, a, a + SLOT_COLS, h2, KD))])
                load_slot(3, 2, [(slot[3][:, 0:h2, :], cols(w_out, 0, SLOT_COLS, 0, h2)),
                                 (slot[3][:, h2:KD, :], cols(w_out, 0, SLOT_COLS, h2, KD))])
                wait(ys_turned, l, 0, alone=True)
                sp.dma_start(tail_w, cols(w_out, SLOT_COLS, D, 0, KD)).then_inc(tail_loaded.sem, 16)

                wait(chunks_ready, l, 1, alone=True)
                rounds = sp.value_load(rounds_tab[0:1, ds(l, 1)], min_val=1, max_val=MAX_ROUNDS)
                with sp.Fori(0, rounds) as r:
                    for i in range(RING):
                        e = sp.value_load(chunk_tab[0:1, 0, ds(r * RING + i, 1)], min_val=0, max_val=NE - 1)
                        sp.wait_ge(slot_done[i].sem, before + r + l * 3 + (3 + 1))
                        sp.nop(nofuse=True)
                        sp.dma_start(gate_w[i], g["w_gate"][ds(l, 1), ds(e, 1)].rearrange(
                            "o a (p k) f -> p (o a k) f", k=KD)).then_inc(exp_loaded[i].sem, 16)
                        sp.dma_start(up_w[i], g["w_up"][ds(l, 1), ds(e, 1)].rearrange(
                            "o a (p k) f -> p (o a k) f", k=KD)).then_inc(exp_loaded[i].sem, 16)
                        sp.dma_start(down_w[i], g["w_down"][ds(l, 1), ds(e, 1)].rearrange(
                            "o a (k p) n -> p (o a k) n", p=P)).then_inc(exp_loaded[i].sem, 16)

        @block.gpsimd
        def _(pool):
            wait = engine_wait(pool)
            nc.gpsimd.memset(pool_blk[:], 0.0).then_inc(s_zero.sem, 1)
            for sig in slot_done + [vec_ready, lam_ready, ys_turned, down_act, down_dve, kv_free]:
                pool.sem_inc(sig.sem, sig.credit)
            pool.dma_start(krow[0:8, 0:P], g["c"][0].rearrange("(k p) -> k p", p=P)).then_inc(s_cin.sem, 16)
            pool.dma_start(krow[0:8, P:2 * P], g["c_ctx"].rearrange("(k p) -> k p", p=P)).then_inc(s_cin.sem, 16)
            pool.wait_ge(s_zero.sem, 1)
            with pool.Fori(0, DEPTH) as l:
                def row(name, n):
                    return g[name][ds(l, 1)].rearrange("o (k p) -> (o k) p", p=P)

                wait(vec_ready, l, 0, alone=True)
                for name, n in VECS:
                    pool.dma_start(vec_rows[VCOL[name]:VCOL[name] + n, :], row(name, n)).then_inc(vec_loaded.sem, 16)
                wait(lam_ready, l, 0, alone=True)
                pool.dma_start(lam_in[:], g["diff_lambda"][ds(l, 1)]).then_inc(vec_loaded.sem, 16)
                pool.dma_start(lam_c[:], lam_dram[ds(l, 1)].rearrange("o p c -> (o p) c")).then_inc(vec_loaded.sem, 16)
                wait(layer_x, l, KD, alone=True)
                pool.dma_start(ck_rows, g["cache_k"][0, ds(l, 1)].rearrange("o t h m d -> (o t) (h m d)")).then_inc(mix_loaded.sem, 16)
                pool.dma_start(dw_rows[0:TAPS, :], g["conv_dw"][ds(l, 1)].rearrange("o k n -> (o k) n")).then_inc(mix_loaded.sem, 16)
                pool.dma_start(cv, g["cache_v"][0, ds(l, 1)].rearrange("o t h e -> (o t) (h e)")).then_inc(mix_loaded.sem, 16)
                pool.dma_start(conv_pw[:], g["conv_pw"][ds(l, 1)].rearrange("o (k p) n -> p (o k) n", p=P)).then_inc(mix_loaded.sem, 16)
                for b in range(4):
                    q = 64 * (b % 2)
                    pool.dma_start(pool_blk[q:q + 64, b // 2, q:q + 64], g["pool_w"][ds(l, 1), b].rearrange(
                        "o c d -> (o c) d")).then_inc(mix_loaded.sem, 16)
                pool.dma_start(router_w[:, :, 0:NG], g["router_grp"][ds(l, 1)].rearrange(
                    "o (k p) n -> p (o k) n", p=P)).then_inc(rt_loaded.sem, 16)
                pool.dma_start(router_w[:, :, NG:], g["router_exp"][ds(l, 1)].rearrange(
                    "o (k p) n -> p (o k) n", p=P)).then_inc(rt_loaded.sem, 16)
                pool.dma_start(router_b[0:NG, :], g["router_grp_b"][ds(l, 1)].rearrange("o n -> n o")).then_inc(rt_loaded.sem, 16)
                pool.dma_start(router_b[NG:, :], g["router_exp_b"][ds(l, 1)].rearrange("o n -> n o")).then_inc(rt_loaded.sem, 16)
                wait(ck_copied, l, 2, alone=True)
                pool.dma_start(new_k[0, ds(l, 1)].rearrange("o t h m d -> (o t) (h m d)"), krow[:]).then_inc(out_k.sem, 16)
                wait(proj_act, l, 13, alone=True)
                pool.dma_start(new_v[0, ds(l, 1)].rearrange("o t h e -> (o t) (h e)"), vrow[:, 0, :]).then_inc(out_k.sem, 16)
                wait(tail_used, l, 1, alone=True)
                pool.dma_start(iota_tri, iota_dram).then_inc(iota_loaded.sem, 16)
                wait(out_k, l, 2, alone=True)
                pool.sem_inc(kv_free.sem, 1)
            for t in range(NT):
                pool.wait_ge(out_rows.sem, 2 * t + 2)
                dst = y_prompt[0] if t == 0 else y_sample[0, (t - 1) * P:t * P, :]
                pool.dma_start(dst, xrow[:, t, :]).then_inc(s_out.sem, 16)
            pool.wait_ge(s_out.sem, 16 * NT)

        @block.tensor
        def _(pe):
            wait = engine_wait(pe)
            mm, tr = nc.tensor.matmul, nc.tensor.transpose

            pe.wait_ge(s_cst.sem, 16)
            pe.wait_ge(s_xin.sem, 32)
            for m in range(KD):
                for t in range(NT):
                    last = tr(ps[:, m, t * P:(t + 1) * P], xrow[:, t, m * P:(m + 1) * P], ident)
                last.then_inc(s_xt.sem, 1)
            pe.wait_ge(s_crow.sem, 1)
            pe.wait_ge(layer_x.sem, 1)
            for v in range(2):
                last = tr(ps[:, 0, 8 * v:8 * v + 8], krow[0:8, 256 + v * P:256 + (v + 1) * P], ident[0:8, 0:8])
            last.then_inc(s_cT.sem, 1)
            pe.wait_ge(s_sT.sem, 1)
            pe.wait_ge(s_ctl.sem, 1)

            with pe.Fori(0, DEPTH) as l:
                before = pe.value_load(before_tab[0:1, ds(l, 1)], min_val=0, max_val=DEPTH * MAX_ROUNDS)
                wait(layer_x, l, KD)

                def vectors():
                    wait(vec_loaded, l, len(VECS) + 2)
                    tr(ps[:, 6, 0:NVEC], vec_rows[:], ident[0:NVEC, 0:NVEC]).then_inc(vec_ready.sem, 1)
                    wait(mix_loaded, l, 8, alone=True)
                    for c in range(2):
                        last = tr(ps[:, 5, 32 * c:32 * c + TAPS], dw_rows[0:TAPS, c * P:(c + 1) * P],
                                  ident[0:TAPS, 0:TAPS])
                    last.then_inc(dw_ready.sem, 1)
                    wait(lam_ready, l, 1)
                    mm(ps[:, 4, 0:1], C["ones"][0:1, :], lam_s[0:1, 3:4], start=True, stop=True).then_inc(lam_bc.sem, 1)

                def mod_turn(n):
                    wait(mod_rows_copied, l, n + 1, alone=True)
                    for i in range(HALF // P):
                        o = (n * (HALF // P) + i) * 2
                        last = tr(ps[:, 7, o:o + 2], mrow[:, n % 2, i * P:(i + 1) * P], ident[0:2, 0:2])
                    last.then_inc(mod_turned.sem, 1)

                for n in range(2 * MOD_LOADS):
                    s = (n // 2) % RING
                    if n % 2 == 0:
                        pe.wait_ge(slot_loaded[s].sem, l * 96 + (n // (2 * RING)) * 32 + 32)
                    if n >= 2:
                        wait(mod_rows_copied, l, n - 1)
                    for k in range(KD):
                        last = mm(ps[0:2, n % 2, 0:HALF], sT[:, k, :], slot[s][:, k, (n % 2) * HALF:(n % 2 + 1) * HALF],
                                  start=(k == 0), stop=(k == KD - 1))
                    last.then_inc((slot_done[s] if n % 2 else mod_rows).sem, 1)
                    if n >= 1:
                        mod_turn(n - 1)
                    if n == 9:
                        vectors()
                mod_turn(2 * MOD_LOADS - 1)

                ACT_TAKES = [0, 2] + list(range(4, 17))

                def project(n, s, c, rows=None, sig=proj_ready):
                    if n >= 4:
                        if n - 4 in ACT_TAKES:
                            wait(proj_act, l, ACT_TAKES.index(n - 4) + 1)
                        else:
                            wait(proj_dve, l, (n - 4) // 2 + 1)
                    for k in range(KD):
                        if rows is None:
                            last = mm(ps[:, n % 4, 0:T], slot[s][:, k, c:c + P], uT[:, k, :],
                                      start=(k == 0), stop=(k == KD - 1))
                        else:
                            last = mm(ps[:, n % 4, 0:AW], uT[:, k, rows * P:(rows + 1) * P], slot[s][:, k, c:c + AW],
                                      start=(k == 0), stop=(k == KD - 1))
                    last.then_inc(sig.sem, 1)

                def rotate(n):
                    wait(proj_act, l, 4 + n + 1)
                    if n >= 2:
                        wait(roped, l, n - 1)
                    src = (qT if n < HEADS else kT)[:, n % HEADS, SEQ:T]
                    mm(ps[:, 4 + n % 2, 0:LAT], C["rot"], src, start=True, stop=True).then_inc(rot_ready.sem, 1)

                wait(u_act, l, KD // 2)
                wait(u_dve, l, KD // 2)
                wait(lam_done, l, 1)
                pe.wait_ge(slot_loaded[0].sem, l * 96 + 96)
                for n, c in ((0, 4), (1, 2), (2, 5), (3, 3)):
                    project(n, 0, c * P)
                project(4, 0, 0)
                project(5, 0, P, sig=slot_done[0])
                pe.wait_ge(slot_loaded[1].sem, l * 96 + 96)
                for n in range(8):
                    if n == 6:
                        pe.wait_ge(slot_loaded[2].sem, l * 96 + 96)
                    project(6 + n, 1 + n // 6, (n % 6) * P, sig=slot_done[1] if n == 5 else proj_ready)
                    if n >= 1:
                        rotate(n - 1)
                for t in range(NT):
                    project(14 + t, 2, 2 * P, rows=t, sig=slot_done[2] if t == NT - 1 else proj_ready)
                    if t == 0:
                        rotate(7)

                wait(proj_act, l, 13)
                for h in range(HEADS):
                    last = tr(ps[:, 2, h * P:(h + 1) * P], ck_rows[:, h * P:(h + 1) * P], ident)
                last.then_inc(ck_turned.sem, 1)
                wait(proj_act, l, 14)
                for h in range(HEADS):
                    last = tr(ps[:, 3, h * P:(h + 1) * P], kT[:, h, 0:SEQ], ident)
                last.then_inc(ck_turned.sem, 1)
                wait(conv_done, l, 1)
                wait(mod_done, l, 1)
                for t in range(NT):
                    a = 0 if t == 0 else CONV_LAT + (t - 1) * P
                    for c in range(2):
                        last = tr(ps[:, 6 + t // 2, (t % 2) * CONV + c * P:(t % 2) * CONV + (c + 1) * P],
                                  cacc[:, c, a:a + P], ident)
                    last.then_inc(crow_ready.sem, 1)

                wait(ck_copied, l, 2)
                wait(roped, l, 8)

                def scores(u):
                    h, t = u // NT, u % NT
                    if u >= 2:
                        wait(scores_used, l, u - 1)
                    for m in range(2):
                        r = slice(64 * m, 64 * m + 64)
                        b = 2 * (u % 2) + m
                        q = qT[r, h, t * P:(t + 1) * P]
                        if t == 0:
                            last = mm(ps[:, b, 0:SEQ], q, kT[r, h, 0:SEQ], start=True, stop=True)
                        else:
                            mm(ps[:, b, 0:LAT], q, kT[r, h, SEQ:T], start=True, stop=True)
                            last = mm(ps[:, b, LAT:LAT + PAST], q, ckT[r, h, :], start=True, stop=True)
                    last.then_inc(scores_ready.sem, 1)

                def turn(u):
                    wait(prob_ready, l, u + 1)
                    if u >= 2:
                        wait(prob_copied, l, u - 1)
                    for k in range(1 if u % NT == 0 else NT):
                        last = tr(ps[:, 4 + u % 2, k * P:(k + 1) * P], probs[:, u % 2, 0, k * P:(k + 1) * P], ident)
                    last.then_inc(prob_turned.sem, 1)

                def values(u):
                    h, t = u // NT, u % NT
                    wait(prob_copied, l, u + 1)
                    if u >= 2:
                        wait(o_copied, l, u - 1)
                    hs = slice(h * VD, (h + 1) * VD)
                    vs = [vrow[:, 0, hs]] if t == 0 else [vrow[:, 1, hs], vrow[:, 2, hs], cv[:, hs]]
                    for k, v in enumerate(vs):
                        last = mm(ps[:, 6 + u % 2, 0:VD], aT[:, u % 2, k, :], v, start=(k == 0), stop=(k == len(vs) - 1))
                    last.then_inc(o_ready.sem, 1)

                wait(proj_act, l, 15)
                NU = HEADS * NT
                for u in range(NU + 2):
                    if u < NU:
                        scores(u)
                    if u == 2:
                        wait(cln_done, l, 1)
                    if u >= 1 and u - 1 < NU:
                        turn(u - 1)
                    if u >= 2:
                        values(u - 2)

                wait(pool_done, l, 1)
                wait(scores_used, l, NU)
                for c in range(2):
                    mm(ps[:, c, 0:SEQ], pool_blk[:, c, :], sumX[:, c, PP:PP + SEQ], start=True, stop=True)
                    mm(ps[:, c, SEQ:T], pool_blk[:, c, :], sumX[:, c, POOL_LAT:POOL_LAT + LAT],
                       start=True, stop=True).then_inc(pool_ready.sem, 1)
                wait(prob_copied, l, NU)
                for c in range(2):
                    for t in range(NT):
                        last = tr(ps[:, 4 + c, t * P:(t + 1) * P], crow[:, t, c * P:(c + 1) * P], ident)
                    last.then_inc(cback.sem, 1)
                wait(o_normed, l, 1)
                for h in range(HEADS):
                    if h == 2:
                        wait(mix_ready, l, 2)
                    for t in range(NT):
                        last = tr(ps[:, (6 + h) % 8, t * P:(t + 1) * P], orow[:, t, h, :], ident)
                    last.then_inc(o_turned.sem, 1)
                wait(csil_ready, l, 2)
                for n in range(2):
                    for c in range(2):
                        last = mm(ps[:, 2 + n, 0:T], conv_pw[:, c, n * P:(n + 1) * P], csil[:, c, :],
                                  start=(c == 0), stop=(c == 1))
                    last.then_inc(cpw_ready.sem, 1)

                def layer_norm(which, n):
                    wait(z_ready, l, which * KD + n + 1)
                    last = mm(ps[:, 4, 0:T], C["ones"], uT[:, n, :], start=(n == 0), stop=(n == KD - 1))
                    if n == KD - 1:
                        last.then_inc(mean_ready.sem, 1)
                        for m in range(KD):
                            wait(squared, l, which * KD + m + 1)
                            last = mm(ps[:, 5, 0:T], C["ones"], ln_t[:, 2 + m % 2, :], start=(m == 0), stop=(m == KD - 1))
                            last.then_inc(sq_used.sem, 1)

                wait(mix_ready, l, KD)
                pe.wait_ge(slot_loaded[3].sem, l * 96 + 96)
                wait(tail_loaded, l, 1)
                for m in range(KD):
                    if m >= 4:
                        wait(gated, l, m - 3)
                    for k in range(KD):
                        wt = slot[3][:, k, m * P:(m + 1) * P] if m < 6 else tail_w[:, k, (m - 6) * P:(m - 5) * P]
                        last = mm(ps[:, m % 4, 0:T], wt, mixT[:, k, :], start=(k == 0), stop=(k == KD - 1))
                    last.then_inc({5: slot_done[3], 7: tail_used}.get(m, y1_ready).sem, 1)
                    if m >= 1:
                        layer_norm(0, m - 1)
                layer_norm(0, KD - 1)

                wait(rt_loaded, l, 4)
                for k in range(KD):
                    wait(u2_ready, l, k + 1)
                    last = mm(ps[0:NG + NE, 6, 0:T], router_w[:, k, :], uT[:, k, :], start=(k == 0), stop=(k == KD - 1))
                last.then_inc(logits_T.sem, 1)
                wait(logits_copied, l, 1, alone=True)
                for t in range(NT):
                    last = tr(ps[:, 5, t * (NG + NE):(t + 1) * (NG + NE)], lgT[:, t * P:(t + 1) * P],
                              ident[0:NG + NE, 0:NG + NE])
                last.then_inc(logits_ready.sem, 1)
                for n in range(6):
                    t, h = n // 2, n % 2
                    if n >= 4:
                        wait(urow_ready, l, n - 3)
                    for m in range(4):
                        last = tr(ps[:, n % 4, m * P:(m + 1) * P], uT[:, 4 * h + m, t * P:(t + 1) * P], ident)
                    last.then_inc(urow_turned.sem, 1)
                wait(assign_ready, l, 1)
                wait(iota_loaded, l, 1)
                for t in range(NT):
                    mm(ps[:, 7, 0:NE], C["ones"], asg[:, t, :], start=(t == 0), stop=(t == NT - 1))
                for t in range(NT):
                    o = ps[:, 7, NE * (t + 1):NE * (t + 2)]
                    for s in range(t):
                        mm(o, C["ones"], asg[:, s, :], start=(s == 0), stop=False)
                    last = mm(o, tri, asg[:, t, :], start=(t == 0), stop=True)
                last.then_inc(ranks_ready.sem, 1)
                wait(chunk_cols, l, 1)
                for i in range(2):
                    last = tr(ps[0:1, 6, i * P:(i + 1) * P], chk[:, i:i + 1], ident)
                last.then_inc(chunk_turned.sem, 1)
                wait(urow_ready, l, 6)
                wait(P_ready, l, NT)
                for n in range(2 * KD):
                    k, h = n // 2, n % 2
                    if n >= 4:
                        wait(xs_act if h == 0 else xs_dve, l, k - 1)
                    a, b = (0, 512) if h == 0 else (512, PAIRS)
                    for t in range(NT):
                        last = mm(ps[:, n % 4, 0:b - a], urow[:, t, k * P:(k + 1) * P], Pm[:, t, a:b],
                                  start=(t == 0), stop=(t == NT - 1))
                    last.then_inc(gath_ready.sem, 1)
                for n in range(2 * NT):
                    t, h = n // 2, n % 2
                    wait(Pw_ready, l, t + 1)
                    if n >= 2:
                        wait(PT_ready, l, n - 1)
                    for s in range(3):
                        last = tr(ps[:, 4 + n % 2, s * P:(s + 1) * P], Pw[:, t % 2, (3 * h + s) * P:(3 * h + s + 1) * P], ident)
                    last.then_inc(Pw_turned.sem, 1)

                wait(xs_act, l, KD)
                wait(xs_dve, l, KD)
                wait(PT_ready, l, 2 * NT)
                wait(chunks_ready, l, 1)
                rounds = pe.value_load(rounds_tab[0:1, ds(l, 1)], min_val=1, max_val=MAX_ROUNDS)
                with pe.Fori(0, rounds) as r:
                    done = (before + r) * RING

                    def gate_up(i):
                        off = pe.value_load(chunk_tab[0:1, 1, ds(r * RING + i, 1)], min_val=0, max_val=PAIRS)
                        pe.wait_ge(exp_loaded[i].sem, (before + r) * 48 + 48)
                        for half, wt in ((0, gate_w[i]), (1, up_w[i])):
                            for f in range(2):
                                o = (2 * half + f) * W
                                for k in range(KD):
                                    last = mm(ps[:, i % 2, o:o + W], wt[:, k, f * P:(f + 1) * P], XsT[:, k, ds(off, W)],
                                              start=(k == 0), stop=(k == KD - 1))
                        last.then_inc(gu_ready.sem, 1)

                    def down(i):
                        pe.wait_ge(h_ready.sem, done + (i + 1))
                        pe.wait_ge(down_act.sem, done + (i - 1 + 2))
                        pe.wait_ge(down_dve.sem, done + (i - 1 + 2))
                        for m in range(KD):
                            for f in range(2):
                                last = mm(ps[:, 2 + 2 * (i % 2) + m // 4, (m % 4) * W:(m % 4 + 1) * W],
                                          down_w[i][:, f, m * P:(m + 1) * P], hT[:, i % 2, f, :],
                                          start=(f == 0), stop=(f == 1))
                            if m == KD // 2 - 1:
                                last.then_inc(down_ready.sem, 1)
                        last.then_inc(slot_done[i].sem, 1)

                    for i in range(RING):
                        gate_up(i)
                        if i >= 1:
                            down(i - 1)
                    down(RING - 1)

                after = (before + rounds) * RING
                pe.wait_ge(down_act.sem, after + 2)
                pe.wait_ge(down_dve.sem, after + 2)
                for n in range(2 * ST):
                    s, h = n // 2, n % 2
                    if n >= 4:
                        wait(ys_act if h == 0 else ys_dve, l, s - 1)
                    for m in range(4):
                        last = tr(ps[:, n % 4, m * P:(m + 1) * P], YsT[:, 4 * h + m, s * P:(s + 1) * P], ident)
                    last.then_inc(ys_turned.sem, 1)
                wait(ys_act, l, ST)
                wait(ys_dve, l, ST)
                for m in range(KD):
                    if m >= 4:
                        wait(gated, l, KD + m - 3)
                    for s in range(ST):
                        last = mm(ps[:, m % 4, 0:T], Ysr[:, s, m * P:(m + 1) * P], PTw[:, s, :],
                                  start=(s == 0), stop=(s == ST - 1))
                    last.then_inc(y2_ready.sem, 1)
                    if m >= 1:
                        layer_norm(1, m - 1)
                layer_norm(1, KD - 1)

            wait(layer_x, DEPTH, KD)
            for n in range(2 * NT):
                t, h = n // 2, n % 2
                for m in range(4):
                    last = tr(ps[:, n, m * P:(m + 1) * P], xT[:, 4 * h + m, t * P:(t + 1) * P], ident)
                last.then_inc(out_turned.sem, 1)

        @block.scalar
        def _(act):
            wait = engine_wait(act)
            fn = nc.scalar.activation
            ID = ACT.Identity

            act.wait_ge(s_cin.sem, 32)
            fn(krow[0:8, 2 * P:4 * P], krow[0:8, 0:2 * P], ACT.Silu).then_inc(s_crow.sem, 1)
            for m in range(KD):
                act.wait_ge(s_xt.sem, m + 1)
                fn(xT[:, m, :], ps[:, m, 0:T], ID).then_inc(layer_x.sem, 1)
            act.wait_ge(s_cT.sem, 1)
            fn(sT[:].rearrange("p k v -> p v k"), ps[:, 0, 0:16].rearrange("p (v k) -> p v k", v=2), ID).then_inc(s_sT.sem, 1)
            act.wait_ge(s_ctl.sem, 2)

            with act.Fori(0, DEPTH) as l:
                before = act.value_load(before_tab[0:1, ds(l, 1)], min_val=0, max_val=DEPTH * MAX_ROUNDS)

                def modulate(m, shift, scale, sig):
                    for a, b, v in SEGS:
                        last = fn(uT[:, m, a:b], xT[:, m, a:b], ID, bias=mod(shift + m, v), scale=mod(scale + m, v))
                    last.then_inc(sig.sem, 1)

                wait(lam_dot, l, 1)
                fn(lam_s[:, 0:2], lam_s[:, 0:2], ACT.Exp).then_inc(lam_exp.sem, 1)
                wait(layer_x, l, KD)
                for n in range(2 * MOD_LOADS):
                    if n % 2:
                        act.wait_ge(slot_done[(n // 2) % RING].sem, before + l * 3 + (n // (2 * RING) + 1 + 1))
                    else:
                        wait(mod_rows, l, n // 2 + 1)
                    if n >= 2:
                        wait(mod_turned, l, n - 1)
                    fn(mrow[:, n % 2, :], ps[0:2, n % 2, 0:HALF], ID).then_inc(mod_rows_copied.sem, 1)
                wait(mod_done, l, 1)
                for m in range(0, KD, 2):
                    modulate(m, SH1, SC1, u_act)

                def proj_wait(n):
                    if n == 5:
                        act.wait_ge(slot_done[0].sem, before + l * 3 + (3 + 1))
                    elif n == 11:
                        act.wait_ge(slot_done[1].sem, before + l * 3 + (3 + 1))
                    elif n == 16:
                        act.wait_ge(slot_done[2].sem, before + l * 3 + (3 + 1))
                    else:
                        wait(proj_ready, l, n + 1 - (n > 5) - (n > 11))

                wait(pads_zero, l, 1)
                for n in (0, 2):
                    proj_wait(n)
                    c = n // 2
                    fn(glu[:, c, CP:CP + SEQ], ps[:, n % 4, 0:SEQ], ACT.Sigmoid)
                    fn(glu[:, c, GLU_LAT:GLU_LAT + LAT], ps[:, n % 4, SEQ:T], ACT.Sigmoid).then_inc(proj_act.sem, 1)
                for n in (4, 5):
                    proj_wait(n)
                    fn(apad[:, n - 4, PP:PP + SEQ], ps[:, n % 4, 0:SEQ], ID)
                    fn(apad[:, n - 4, POOL_LAT:POOL_LAT + LAT], ps[:, n % 4, SEQ:T], ID).then_inc(proj_act.sem, 1)
                for n in range(8):
                    proj_wait(6 + n)
                    fn((qT if n < HEADS else kT)[:, n % HEADS, :], ps[:, (6 + n) % 4, 0:T], ID,
                       scale=HD ** -0.5 if n < HEADS else 1.0).then_inc(proj_act.sem, 1)
                wait(kv_free, l, 0)
                for t in range(NT):
                    proj_wait(14 + t)
                    fn(vrow[:, t, :], ps[:, (14 + t) % 4, 0:AW], ID).then_inc(proj_act.sem, 1)
                wait(ck_turned, l, 1)
                fn(ckT, ps[:, 2, :].rearrange("p (h t) -> p h t", h=HEADS), ID).then_inc(ck_copied.sem, 1)
                wait(ck_turned, l, 2)
                fn(krow[:], ps[:, 3, :], ID).then_inc(ck_copied.sem, 1)
                wait(cln_var, l, 1)
                fn(cstat[:, :, 2], cstat[:, :, 1], ACT.Sqrt, bias=epsc[:]).then_inc(cln_sd.sem, 1)

                NU = HEADS * NT
                for u in range(NU + 2):
                    if u < NU:
                        n = SEQ if u % NT == 0 else LAT + PAST
                        wait(neg_max, l, u + 1)
                        if u >= 2:
                            wait(prob_turned, l, u - 1)
                        for m in range(2):
                            last = fn(probs[:, u % 2, m, 0:n], ps[:, 2 * (u % 2) + m, 0:n], ACT.Exp,
                                      bias=small[:, u % 2, m, 1:2], accum_out=small[:, u % 2, m, 2:3])
                        last.then_inc(scores_used.sem, 1)
                    if u >= 1 and u - 1 < NU:
                        n = P * (1 if (u - 1) % NT == 0 else NT)
                        wait(prob_turned, l, u)
                        if u >= 3:
                            wait(o_ready, l, u - 2)
                        fn(aT[:, (u - 1) % 2].rearrange("p k q -> p (k q)")[:, 0:n], ps[:, 4 + (u - 1) % 2, 0:n], ID).then_inc(prob_copied.sem, 1)
                    if u >= 2:
                        v = u - 2
                        wait(o_ready, l, v + 1)
                        fn(orow[:, v % NT, v // NT, :], ps[:, 6 + v % 2, 0:VD], ID).then_inc(o_copied.sem, 1)

                wait(vec_copied, l, 1)
                for c in range(2):
                    wait(pool_ready, l, c + 1)
                    fn(mixT[:, c, :], ps[:, c, 0:T], ID, scale=vcol("pool_scale", c)).then_inc(mix_ready.sem, 1)
                wait(rms_var, l, 1)
                fn(rms[:, 1, :], rms[:, 0, :], ACT.Sqrt, bias=epsc[:], scale=1.0 / VD).then_inc(rms_sd.sem, 1)
                for h in range(HEADS):
                    wait(o_turned, l, h + 1)
                    fn(mixT[:, 2 + h, :], ps[:, (6 + h) % 8, 0:T], ID, scale=subg[:]).then_inc(mix_ready.sem, 1)
                for c in range(2):
                    wait(cback, l, c + 1)
                    fn(csil[:, c, :], ps[:, 4 + c, 0:T], ACT.Silu, bias=vcol("conv_ln_b", c),
                       scale=vcol("conv_ln_g", c)).then_inc(csil_ready.sem, 1)
                for c in range(2):
                    wait(cpw_ready, l, c + 1)
                    fn(mixT[:, 6 + c, :], ps[:, 2 + c, 0:T], ID).then_inc(mix_ready.sem, 1)

                def gate_tile(m, gate):
                    for a, b, v in SEGS:
                        last = fn(uT[:, m, a:b], ps[:, m % 4, a:b], ID, scale=mod(gate + m, v))
                    last.then_inc(gated.sem, 1)

                def squares_root(which):
                    for m in range(KD):
                        wait(centred, l, which * KD + m + 1)
                        if m >= 2:
                            wait(sq_used, l, which * KD + m - 1)
                        fn(ln_t[:, 2 + m % 2, :], uT[:, m, :], ACT.Square).then_inc(squared.sem, 1)
                    wait(sq_used, l, which * KD + KD)
                    fn(ln_t[:, 1, :], ps[:, 5, 0:T], ACT.Sqrt, bias=epsc[:], scale=1.0 / D).then_inc(root_ready.sem, 1)

                for m in range(KD):
                    if m == 5:
                        act.wait_ge(slot_done[3].sem, before + l * 3 + (3 + 1))
                    elif m == 7:
                        wait(tail_used, l, 1)
                    else:
                        wait(y1_ready, l, m + 1 - (m > 5))
                    gate_tile(m, GA1)
                squares_root(0)
                for m in range(KD + 1):
                    if m < KD:
                        wait(normed, l, m + 1)
                        fn(xT[:, m, :], uT[:, m, :], ID, bias=vcol("ln1_b", m), scale=vcol("ln1_g", m)).then_inc(x_mid.sem, 1)
                    if m >= 1:
                        wait(x_mid, l, m)
                        modulate(m - 1, SH2, SC2, u2_ready)

                wait(logits_T, l, 1)
                fn(lgT, ps[0:NG + NE, 6, 0:T], ID, bias=router_b[:]).then_inc(logits_copied.sem, 1)
                wait(gdiff, l, 1)
                fn(gtmp, gtmp, ACT.Exp).then_inc(gexp.sem, 1)
                wait(out_k, l, 2)
                for n in range(6):
                    t, h = n // 2, n % 2
                    wait(urow_turned, l, n + 1)
                    dst = urow[:, t, :].rearrange("q (k p) -> q p k", k=KD)[:, h * 64:(h + 1) * 64, :]
                    fn(dst, ps[:, n % 4, :].rearrange("q (p k) -> q p k", k=KD), ID).then_inc(urow_ready.sem, 1)
                    if n == 0:
                        wait(ediff, l, 1)
                        fn(q, q, ACT.Exp).then_inc(eexp.sem, 1)
                for k in range(KD):
                    wait(gath_ready, l, 2 * k + 1)
                    fn(XsT[:, k, 0:512], ps[:, (2 * k) % 4, 0:512], ID).then_inc(xs_act.sem, 1)
                for n in range(2 * NT):
                    t, h = n // 2, n % 2
                    wait(Pw_turned, l, n + 1)
                    fn(PTw[:, 3 * h:3 * h + 3, t * P:(t + 1) * P],
                       ps[:, 4 + n % 2, 0:3 * P].rearrange("p (s q) -> p s q", s=3), ID).then_inc(PT_ready.sem, 1)

                wait(chunks_ready, l, 1)
                rounds = act.value_load(rounds_tab[0:1, ds(l, 1)], min_val=1, max_val=MAX_ROUNDS)
                with act.Fori(0, rounds) as r:
                    done = (before + r) * RING

                    def take(i):
                        off = act.value_load(chunk_tab[0:1, 1, ds(r * RING + i, 1)], min_val=0, max_val=PAIRS)
                        act.wait_ge(down_ready.sem, done + (i + 1))
                        act.wait_ge(down_act.sem, done + (i + 2))
                        fn(YsT[:, 0:4, ds(off, W)], ps[:, 2 + 2 * (i % 2), 0:4 * W].rearrange("p (m n) -> p m n", m=4),
                           ID).then_inc(down_act.sem, 1)

                    for i in range(RING):
                        act.wait_ge(gu_ready.sem, done + (i + 1))
                        fn(sg[:, i % 2], ps[:, i % 2, 0:2 * W].rearrange("p (f n) -> p f n", f=2), ACT.Silu).then_inc(silu_ready.sem, 1)
                        if i >= 1:
                            take(i - 1)
                    take(RING - 1)

                for s in range(ST):
                    wait(ys_turned, l, 2 * s + 1)
                    fn(Ysr[:, s, 0:512], ps[:, (2 * s) % 4, :], ID).then_inc(ys_act.sem, 1)
                for m in range(KD):
                    wait(y2_ready, l, m + 1)
                    gate_tile(m, GA2)
                squares_root(1)
                for m in range(KD):
                    wait(normed, l, KD + m + 1)
                    fn(xT[:, m, :], uT[:, m, :], ID, bias=vcol("ln2_b", m), scale=vcol("ln2_g", m)).then_inc(layer_x.sem, 1)

            for n in range(2 * NT):
                t, h = n // 2, n % 2
                act.wait_ge(out_turned.sem, n + 1)
                fn(xrow[:, t, 512 * h:512 * h + 512], ps[:, n, :], ID).then_inc(out_rows.sem, 1)

        @block.vector
        def _(dve):
            wait = engine_wait(dve)
            v = nc.vector
            before_z = v.memset(before_tab[:], 0)
            before_z.then_inc(s_ctl.sem, 1)
            v.memset(before_f[:], 0.0)
            v.memset(epsc[:], EPS).then_inc(s_ctl.sem, 1)
            dve.wait_ge(s_ctl.sem, 2)

            with dve.Fori(0, DEPTH) as l:
                before = dve.value_load(before_tab[0:1, ds(l, 1)], min_val=0, max_val=DEPTH * MAX_ROUNDS)
                own = Steps(dve_self)

                def after(n, alone=False):
                    wait(dve_self, l, n, alone)

                wait(vec_loaded, l, len(VECS) + 2)
                pairs = lam_in[:].rearrange("o (a b) d -> o a b d", b=2)
                own.add(v.tensor_tensor(pairs[:, :, 0, :], pairs[:, :, 0, :], pairs[:, :, 1, :], ALU.mult))
                after(own.n)
                v.tensor_reduce(lam_s[:, 0:2], pairs[:, :, 0, :], AX, ALU.add).then_inc(lam_dot.sem, 1)
                wait(layer_x, l, KD)
                v.memset(arena[:, XS + NT * AW + AW + QK:XS + NT * AW + AW + QK + 2 * (POOL_COLS + GLU_COLS)],
                         0.0).then_inc(pads_zero.sem, 1)
                wait(vec_ready, l, 1)
                own.add(v.tensor_copy(vec[:], ps[:, 6, 0:NVEC]))
                after(own.n)
                own.add(v.tensor_scalar(subg[:], vcol("subln_g"), lam_c[:, 1:2], None, ALU.mult))
                wait(lam_exp, l, 1)
                own.add(v.tensor_tensor(lam_s[:, 2:3], lam_s[:, 1:2], lam_s[:, 0:1], ALU.subtract))
                after(own.n)
                v.tensor_tensor(lam_s[:, 3:4], lam_s[:, 2:3], lam_c[0:1, 0:1], ALU.subtract).then_inc(lam_ready.sem, 1)
                wait(dw_ready, l, 1)
                v.tensor_copy(dw[:], ps[:, 5, 0:64].rearrange("p (c k) -> p c k", c=2)[:, :, 0:TAPS]).then_inc(vec_copied.sem, 1)
                wait(lam_bc, l, 1)
                v.tensor_copy(nlam[:], ps[:, 4, 0:1]).then_inc(lam_done.sem, 1)
                wait(mod_turned, l, 2 * MOD_LOADS)
                own.add(v.tensor_tensor(modT[:], ps[:, 7, 0:2 * NMOD].rearrange("p (i v) -> p i v", v=2),
                                        vec[:, VCOL["b_mod"]:VCOL["b_mod"] + NMOD].unsqueeze(2).to_broadcast([P, NMOD, 2]),
                                        ALU.add))
                after(own.n)
                own.add(v.tensor_scalar(modT[:, SC1:SC1 + KD, :], modT[:, SC1:SC1 + KD, :], 1.0, None, ALU.add))
                v.tensor_scalar(modT[:, SC2:SC2 + KD, :], modT[:, SC2:SC2 + KD, :], 1.0, None, ALU.add).then_inc(mod_done.sem, 1)
                wait(mod_done, l, 1)
                for m in range(1, KD, 2):
                    for a, b, w_ in SEGS:
                        last = v.tensor_scalar(uT[:, m, a:b], xT[:, m, a:b], mod(SC1 + m, w_), mod(SH1 + m, w_),
                                               ALU.mult, ALU.add)
                    last.then_inc(u_dve.sem, 1)
                for c in range(2):
                    wait(proj_act, l, c + 1)
                    wait(proj_ready, l, 2 * c + 2)
                    bank = 1 + 2 * c
                    v.tensor_tensor(glu[:, c, CP:CP + SEQ], glu[:, c, CP:CP + SEQ], ps[:, bank, 0:SEQ], ALU.mult)
                    v.tensor_tensor(glu[:, c, GLU_LAT:GLU_LAT + LAT], glu[:, c, GLU_LAT:GLU_LAT + LAT], ps[:, bank, SEQ:T],
                                    ALU.mult).then_inc(proj_dve.sem, 1)
                wait(proj_dve, l, 2)

                conv_steps = [(tap, c) for tap in range(TAPS) for c in range(2)]
                conv_own = []

                def conv_step():
                    tap, c = conv_steps[len(conv_own)]
                    src, wt = glu[:, c, tap:tap + CONV_N], dw[:, c, tap:tap + 1]
                    if tap == 0:
                        conv_own.append(own.add(v.tensor_scalar(cacc[:, c, :], src, wt, None, ALU.mult)))
                    elif len(conv_own) < len(conv_steps) - 1:
                        after(conv_own[-2])
                        conv_own.append(own.add(v.scalar_tensor_tensor(cacc[:, c, :], src, wt, cacc[:, c, :], ALU.mult, ALU.add)))
                    else:
                        after(conv_own[-1])
                        conv_own.append(0)
                        v.scalar_tensor_tensor(cacc[:, c, :], src, wt, cacc[:, c, :], ALU.mult, ALU.add).then_inc(conv_done.sem, 1)

                for _ in range(14):
                    conv_step()
                wait(proj_act, l, 4)
                n = POOL_COLS
                own.add(v.tensor_tensor(sumX[:, :, 1:n], apad[:, :, 0:n - 1], apad[:, :, 1:n], ALU.add))
                after(own.n)
                own.add(v.tensor_tensor(sumY[:, :, 2:n - 1], sumX[:, :, 1:n - 2], sumX[:, :, 3:n], ALU.add))
                inv = C["inv"].rearrange("p (c n) -> p c n", c=2)
                mid = slice(PP, PP + POOL_N)
                lo, hi = slice(0, 64), slice(64, P)
                after(own.n)
                own.add(v.tensor_tensor(sumX[lo, 0, mid], sumX[lo, 0, mid], inv[lo, 0, :], ALU.mult))
                own.add(v.tensor_tensor(sumX[hi, 0, mid], sumY[hi, 0, mid], inv[hi, 0, :], ALU.mult))
                own.add(v.tensor_tensor(sumX[:, 1, 4:n - 3], sumY[:, 1, 2:n - 5], sumY[:, 1, 6:n - 1], ALU.add))
                after(own.n)
                own.add(v.tensor_tensor(sumY[:, 1, mid], sumX[:, 1, PP - 4:PP - 4 + POOL_N], sumX[:, 1, PP + 4:PP + 4 + POOL_N], ALU.add))
                after(own.n)
                own.add(v.tensor_tensor(sumX[lo, 1, mid], sumX[lo, 1, mid], inv[lo, 1, :], ALU.mult))
                own.add(v.tensor_tensor(sumX[hi, 1, mid], sumY[hi, 1, mid], inv[hi, 1, :], ALU.mult))
                after(own.n)
                v.tensor_tensor(sumX[:, :, mid], sumX[:, :, mid], apad[:, :, mid], ALU.subtract).then_inc(pool_done.sem, 1)
                for n in range(8):
                    x = (qT if n < HEADS else kT)[:, n % HEADS, SEQ:T]
                    b = 2 * (n % 2)
                    wait(proj_act, l, 4 + n + 1)
                    if n >= 2:
                        wait(roped, l, n - 1)
                    own.add(v.tensor_tensor(rope_t[:, b, :], x, C["cos"], ALU.mult))
                    wait(rot_ready, l, n + 1)
                    own.add(v.tensor_tensor(rope_t[:, b + 1, :], ps[:, 4 + n % 2, 0:LAT], C["sin"], ALU.mult))
                    after(own.n)
                    v.tensor_tensor(x, rope_t[:, b, :], rope_t[:, b + 1, :], ALU.add).then_inc(roped.sem, 1)
                    for _ in range(6):
                        conv_step()
                for t in range(NT):
                    src = ps[:, 6 + t // 2, (t % 2) * CONV:(t % 2 + 1) * CONV]
                    wait(crow_ready, l, max(t + 1, 2))
                    own.add(v.bn_stats(bstat[:, t, :], src))
                after(own.n, alone=True)
                for t in range(NT):
                    last = v.bn_aggr(cstat[:, t, 0:2], bstat[:, t, :])
                    if t < NT - 1:
                        own.add(last)
                last.then_inc(cln_var.sem, 1)

                def conv_norm():
                    wait(cln_sd, l, 1)
                    own.add(v.reciprocal(cstat[:, :, 3], cstat[:, :, 2]))
                    after(own.n)
                    for t in range(NT):
                        src = ps[:, 6 + t // 2, (t % 2) * CONV:(t % 2 + 1) * CONV]
                        last = v.tensor_scalar(crow[:, t, :], src, cstat[:, t, 0:1], cstat[:, t, 3:4], ALU.subtract, ALU.mult)
                        if t < NT - 1:
                            own.add(last)
                    last.then_inc(cln_done.sem, 1)

                NU = HEADS * NT
                for u in range(NU + 1):
                    if u < NU:
                        n = SEQ if u % NT == 0 else LAT + PAST
                        b = u % 2
                        wait(scores_ready, l, u + 1)
                        v.tensor_reduce(small[:, b, :, 1], ps[:, 2 * b:2 * b + 2, 0:n], AX, ALU.max,
                                        negate=True).then_inc(neg_max.sem, 1)
                    if u == 0:
                        conv_norm()
                    if u >= 1:
                        b = (u - 1) % 2
                        n = SEQ if (u - 1) % NT == 0 else LAT + PAST
                        wait(scores_used, l, u)
                        own.add(v.reciprocal(small[:, b, :, 3], small[:, b, :, 2]))
                        after(own.n)
                        own.add(v.tensor_tensor(small[:, b, 1, 0:1], small[:, b, 1, 3:4], nlam[:], ALU.mult))
                        own.add(v.tensor_scalar(probs[:, b, 0, 0:n], probs[:, b, 0, 0:n], small[:, b, 0, 3:4], None, ALU.mult))
                        after(own.n)
                        v.scalar_tensor_tensor(probs[:, b, 0, 0:n], probs[:, b, 1, 0:n], small[:, b, 1, 0:1],
                                               probs[:, b, 0, 0:n], ALU.mult, ALU.add).then_inc(prob_ready.sem, 1)

                wait(o_copied, l, NU)
                wait(prob_turned, l, NU)
                sq = probs.rearrange("p b m n -> p (b m n)").rearrange("p (u e) -> p u e", e=VD)
                o3 = orow.rearrange("p t h e -> p (t h) e")
                own.add(v.tensor_tensor(sq, o3, o3, ALU.mult))
                after(own.n)
                v.tensor_reduce(rms[:, 0, :], sq, AX, ALU.add).then_inc(rms_var.sem, 1)
                wait(rms_sd, l, 1)
                own.add(v.reciprocal(rms[:, 0, :], rms[:, 1, :]))
                after(own.n)
                v.tensor_tensor(o3, o3, rms[:, 0, :].unsqueeze(2).to_broadcast([P, NT * HEADS, VD]), ALU.mult).then_inc(o_normed.sem, 1)
                def residual_norm(which):
                    o = which * KD
                    for m in range(KD):
                        wait(gated, l, o + m + 1)
                        v.scalar_tensor_tensor(uT[:, m, :], xT[:, m, :], ALPHA, uT[:, m, :], ALU.mult, ALU.add).then_inc(z_ready.sem, 1)
                    wait(mean_ready, l, which + 1)
                    wait(z_ready, l, o + KD)
                    for m in range(KD):
                        v.scalar_tensor_tensor(uT[:, m, :], ps[:, 4, 0:T], -1.0 / D, uT[:, m, :], ALU.mult, ALU.add).then_inc(centred.sem, 1)
                    wait(root_ready, l, which + 1)
                    own.add(v.reciprocal(ln_t[:, 0, :], ln_t[:, 1, :]))
                    after(own.n)
                    wait(centred, l, o + KD)
                    for m in range(KD):
                        v.tensor_tensor(uT[:, m, :], uT[:, m, :], ln_t[:, 0, :], ALU.mult).then_inc(normed.sem, 1)

                residual_norm(0)

                def bc(x, n):
                    return x.unsqueeze(2).to_broadcast([P, NT, n])

                def bt(x, n):
                    return x.unsqueeze(1).to_broadcast([P, NT, n])

                def step(ins):
                    own.add(ins)
                    after(own.n)

                def first_max(vals, n, mx, cmx, onehot):
                    rank = bt(C["rank"][:, NE - n:NE], n)
                    step(v.tensor_reduce(mx, vals, AX, ALU.max))
                    step(v.tensor_tensor(onehot, vals, bc(mx, n), ALU.is_equal))
                    step(v.tensor_tensor(onehot, onehot, rank, ALU.mult))
                    step(v.tensor_reduce(cmx, onehot, AX, ALU.max))
                    step(v.tensor_tensor(onehot, onehot, bc(cmx, n), ALU.is_equal))

                wait(logits_ready, l, 1)
                step(v.tensor_copy(lg, ps[:, 5, 0:NT * (NG + NE)].rearrange("p (t n) -> p t n", t=NT)))
                first_max(lg[:, :, 0:NG], NG, gmax, gcm, og)
                v.tensor_tensor(gtmp, lg[:, :, 0:NG], bc(gmax, NG), ALU.subtract).then_inc(gdiff.sem, 1)
                step(v.tensor_scalar(og, og, BIG, -BIG, ALU.mult, ALU.add))
                e4 = lg[:, :, NG:].rearrange("p t (g e) -> p t g e", g=NG)
                step(v.tensor_tensor(e4, e4, og.unsqueeze(3).to_broadcast([P, NT, NG, EPG]), ALU.add))
                el = lg[:, :, NG:]
                first_max(el, NE, m1, c1, o1)
                step(v.scalar_tensor_tensor(etmp, o1, -3 * BIG, el, ALU.mult, ALU.add))
                first_max(etmp, NE, m2, c2, o2)
                v.tensor_tensor(asg, o1, o2, ALU.add).then_inc(assign_ready.sem, 1)
                v.tensor_tensor(q, m2, m1, ALU.subtract).then_inc(ediff.sem, 1)
                wait(gexp, l, 1)
                step(v.tensor_reduce(gsum, gtmp, AX, ALU.add))
                step(v.reciprocal(gw, gsum))
                wait(eexp, l, 1)
                step(v.tensor_scalar(rq, q, 1.0, None, ALU.add))
                step(v.reciprocal(cm, rq))
                step(v.tensor_tensor(w1, gw, cm, ALU.mult))
                step(v.tensor_tensor(w2, w1, q, ALU.mult))
                wait(ranks_ready, l, 1)
                step(v.tensor_copy(tot[:, 0:NE], ps[:, 7, 0:NE]))
                own.add(v.memset(le[:, NE:NE + 1], 0.0))
                ones32 = C["ones"][:, 0:NE]
                step(v.tensor_tensor_scan(start[:, 0:NE], ones32, tot[:, 0:NE], 0.0, ALU.mult, ALU.add))
                step(v.tensor_tensor(start[:, 0:NE], start[:, 0:NE], tot[:, 0:NE], ALU.subtract))
                step(v.tensor_scalar(ce[:, 0:NE], tot[:, 0:NE], 0.0, None, ALU.is_gt))
                for j in range(1, -(-T // W)):
                    step(v.scalar_tensor_tensor(ce[:, 0:NE], tot[:, 0:NE], float(W * j), ce[:, 0:NE], ALU.is_gt, ALU.add))
                step(v.tensor_tensor_scan(cb[:, 0:NE], ones32, ce[:, 0:NE], 0.0, ALU.mult, ALU.add))
                step(v.tensor_scalar(rnd[:, 0:MAX_ROUNDS], C["rounds"], cb[:, NE - 1:NE], None, ALU.is_lt))
                step(v.tensor_reduce(rnd[:, MAX_ROUNDS:], rnd[:, 0:MAX_ROUNDS], AX, ALU.add))
                step(v.tensor_copy(rounds_tab[:, ds(l, 1)], rnd[0:1, MAX_ROUNDS:]))
                step(v.tensor_tensor(before_f[:, ds(l + 1, 1)], before_f[:, ds(l, 1)], rnd[0:1, MAX_ROUNDS:], ALU.add))
                step(v.tensor_copy(before_tab[:, ds(l + 1, 1)], before_f[:, ds(l + 1, 1)]))
                step(v.tensor_tensor(cb[:, 0:NE], cb[:, 0:NE], ce[:, 0:NE], ALU.subtract))
                step(v.tensor_scalar(le[:, 0:NE], cb[:, 0:NE], C["kk"], None, ALU.is_le))
                step(v.tensor_reduce(chk[:, 2:3], le[:, 0:NE], AX, ALU.add))
                step(v.tensor_scalar(chk[:, 0:1], chk[:, 2:3], -1.0, None, ALU.add))
                step(v.tensor_tensor(dd[:, 0:NE], le[:, 0:NE], le[:, 1:NE + 1], ALU.subtract))
                step(v.scalar_tensor_tensor(ce[:, 0:NE], cb[:, 0:NE], float(-W), start[:, 0:NE], ALU.mult, ALU.add))
                step(v.tensor_tensor(ce[:, 0:NE], ce[:, 0:NE], dd[:, 0:NE], ALU.mult))
                step(v.tensor_reduce(chk[:, 2:3], ce[:, 0:NE], AX, ALU.add))
                step(v.tensor_scalar(chk[:, 3:4], C["kk"], float(W), chk[:, 2:3], ALU.mult, ALU.add))
                v.tensor_scalar(chk[:, 1:2], chk[:, 3:4], float(PAIRS), None, ALU.min).then_inc(chunk_cols.sem, 1)
                step(v.tensor_tensor(etmp, ps[:, 7, NE:NE * (1 + NT)].rearrange("p (t n) -> p t n", t=NT),
                                     bt(start[:, 0:NE], NE), ALU.add))
                own.add(v.tensor_tensor(o1, o1, etmp, ALU.mult))
                step(v.tensor_tensor(o2, o2, etmp, ALU.mult))
                own.add(v.tensor_reduce(s1, o1, AX, ALU.add))
                step(v.tensor_reduce(s2, o2, AX, ALU.add))
                wait(chunk_turned, l, 1)
                v.tensor_copy(chunk_tab[:], ps[0:1, 6, 0:2 * P].rearrange("p (i n) -> p i n", i=2)[:, :, 0:MAX_ROUNDS * RING]).then_inc(chunks_ready.sem, 1)
                wait(iota_loaded, l, 1)
                for t in range(NT):
                    step(v.tensor_scalar(Pm[:, t, :], iota, s1[:, t:t + 1], None, ALU.is_equal))
                    v.scalar_tensor_tensor(Pm[:, t, :], iota, s2[:, t:t + 1], Pm[:, t, :], ALU.is_equal,
                                           ALU.add).then_inc(P_ready.sem, 1)

                def weighted(t):
                    if t >= 2:
                        wait(Pw_turned, l, 2 * (t - 1))
                    if t >= 1:
                        wait(Pw_ready, l, t)
                    tmp = tail[:, 0:PAIRS]
                    own.add(v.tensor_scalar(tmp, iota, s1[:, t:t + 1], w1[:, t:t + 1], ALU.is_equal, ALU.mult))
                    step(v.tensor_scalar(Pw[:, t % 2, :], iota, s2[:, t:t + 1], w2[:, t:t + 1], ALU.is_equal, ALU.mult))
                    v.tensor_tensor(Pw[:, t % 2, :], Pw[:, t % 2, :], tmp, ALU.add).then_inc(Pw_ready.sem, 1)

                own.add(v.memset(XsT[:, :, PAIRS:PADDED], 0.0))
                for k in range(KD):
                    wait(gath_ready, l, 2 * k + 2)
                    if k == 0:
                        after(own.n)
                    v.tensor_copy(XsT[:, k, 512:PAIRS], ps[:, (2 * k + 1) % 4, 0:PAIRS - 512]).then_inc(xs_dve.sem, 1)
                    if 1 <= k <= 2:
                        weighted(k - 1)
                weighted(2)

                rounds = dve.value_load(rounds_tab[0:1, ds(l, 1)], min_val=1, max_val=MAX_ROUNDS)
                with dve.Fori(0, rounds) as r:
                    done = (before + r) * RING

                    def take(i):
                        off = dve.value_load(chunk_tab[0:1, 1, ds(r * RING + i, 1)], min_val=0, max_val=PAIRS)
                        dve.wait_ge(slot_done[i].sem, before + r + l * 3 + (3 + 1 + 1))
                        dve.wait_ge(down_dve.sem, done + (i + 2))
                        v.tensor_copy(YsT[:, 4:8, ds(off, W)], ps[:, 3 + 2 * (i % 2), 0:4 * W].rearrange("p (m n) -> p m n", m=4)
                                      ).then_inc(down_dve.sem, 1)

                    for i in range(RING):
                        dve.wait_ge(silu_ready.sem, done + (i + 1))
                        v.tensor_tensor(hT[:, i % 2], sg[:, i % 2], ps[:, i % 2, 2 * W:4 * W].rearrange("p (f n) -> p f n", f=2),
                                        ALU.mult).then_inc(h_ready.sem, 1)
                        if i >= 1:
                            take(i - 1)
                    take(RING - 1)

                for s in range(ST):
                    wait(ys_turned, l, 2 * s + 2)
                    v.tensor_copy(Ysr[:, s, 512:1024], ps[:, (2 * s + 1) % 4, :]).then_inc(ys_dve.sem, 1)
                residual_norm(1)
                own.check()


_INPUTS = ["x_prompt", "x_sample", "cache_k", "cache_v", "c", "c_ctx", "w_mod", "b_mod", "w_in", "w_out", "pool_w",
           "pool_scale", "diff_lambda", "subln_g", "conv_dw", "conv_ln_g", "conv_ln_b", "conv_pw", "ln1_g", "ln1_b",
           "ln2_g", "ln2_b", "router_grp", "router_grp_b", "router_exp", "router_exp_b", "w_gate", "w_up", "w_down"]
_OUTPUTS = [(1, SEQ, D), (1, LAT, D), (1, DEPTH, SEQ, HEADS, 2, HD), (1, DEPTH, SEQ, HEADS, VD)]


def kernel(**inputs):
    import concourse.bacc as bacc
    from concourse.bass_utils import run_bass_kernel_spmd as run

    nc = bacc.Bacc("TRN2", target_bir_lowering=False, num_devices=1)
    arrays, aps = {}, {}

    def add(name, a):
        a = np.ascontiguousarray(a)
        arrays[f"in_{name}"] = a
        aps[name] = nc.dram_tensor(f"in_{name}", a.shape, mybir.dt.from_np(a.dtype), kind="ExternalInput").ap()

    for name in _INPUTS:
        add(name, inputs[name])
    table, iota, lam = shape_constants()
    add("consts", table)
    add("iota", iota)
    add("lam", lam)
    outs = [nc.dram_tensor(f"out_{i}", s, F32, kind="ExternalOutput").ap() for i, s in enumerate(_OUTPUTS)]
    build(nc, aps, aps["consts"], aps["iota"], aps["lam"], *outs)
    r = run(nc, [arrays], core_ids=[0])
    return tuple(r.results[0][f"out_{i}"] for i in range(len(_OUTPUTS)))
```

```python
from contextlib import ExitStack
import math

import numpy as np
import concourse.bass as bass
from concourse import mybir

F32 = mybir.dt.float32
I32 = mybir.dt.int32
ALU = mybir.AluOpType
ACT = mybir.ActivationFunctionType
AX = mybir.AxisListType.X
ds = bass.ds

P = 128
D = 1024
DEPTH = 2
SEQ = 128
LAT = 256
PAST = 128
T = SEQ + LAT
NT = T // P
KD = D // P
GRID_W = 64
POOL = D // 4
HEADS = 4
HD = 64
VD = 2 * HD
QK = HEADS * 2 * HD
AW = HEADS * VD
CONV = D - POOL - AW
TAPS = 31
AXIS = HD // 2
NG = 4
EPG = 8
NE = NG * EPG
FF = D // 4
ALPHA = (2 * DEPTH) ** 0.25
EPS = 1e-5
PAIRS = 2 * T
ST = PAIRS // P
W = 96
PADDED = PAIRS + W
RING = 4
SLOT_COLS = 768
HALF = SLOT_COLS // 2
SLOT = KD * SLOT_COLS
NMOD = 6 * KD
MOD_STEPS = 6 * D // (2 * SLOT_COLS)
STEP_TILES = 2 * SLOT_COLS // P
GROUP_TILES = STEP_TILES // 4
USES = (4, 3, 3, 2)
MAX_CHUNKS = NE + (PAIRS - NE) // W
MAX_ROUNDS = -(-MAX_CHUNKS // RING)
BIG = 1e30

PP = 8
POOL_COLS = 2 * PP + SEQ + 2 * PP + LAT
POOL_LAT = 3 * PP + SEQ
POOL_N = POOL_COLS - 2 * PP
CP = TAPS // 2
GLU_COLS = 4 * CP + T
GLU_LAT = 3 * CP + SEQ
CONV_N = GLU_COLS - 2 * CP
CONV_LAT = 2 * CP + SEQ

VECS = [("b_mod", NMOD), ("pool_scale", POOL // P), ("subln_g", 1), ("conv_ln_g", CONV // P),
        ("conv_ln_b", CONV // P), ("ln1_g", KD), ("ln1_b", KD), ("ln2_g", KD), ("ln2_b", KD)]
VCOL, NVEC = {}, 0
for _name, _n in VECS:
    VCOL[_name] = NVEC
    NVEC += _n

CONST_COLS = [("ident", P), ("ones", P), ("rot", P), ("cos", LAT), ("sin", LAT),
              ("rank", NE), ("kk", 1), ("rounds", MAX_ROUNDS), ("inv", 2 * POOL_N)]


def shape_constants():
    c = {}
    c["ident"] = np.eye(P)
    c["tri"] = np.triu(np.ones((P, P)), 1)
    c["ones"] = np.ones((P, P))
    rot = np.zeros((P, P))
    half = AXIS // 2
    for j in range(P):
        if (j // half) % 2 == 0:
            rot[j + half, j] = -1.0
        else:
            rot[j - half, j] = 1.0
    c["rot"] = rot
    pos = np.arange(LAT)
    coord = np.stack([pos // GRID_W, pos % GRID_W]).astype(np.float32)
    inv = (np.float32(10000.0) ** (-np.arange(0, AXIS, 2, dtype=np.float32) / np.float32(AXIS))).astype(np.float32)
    p = np.arange(P)
    ang = coord[(p // AXIS) % 2, :] * inv[p % half][:, None]
    c["cos"] = np.cos(ang)
    c["sin"] = np.sin(ang)
    c["rank"] = np.tile(np.arange(NE, 0, -1), (P, 1))
    c["kk"] = np.arange(P)[:, None]
    c["rounds"] = np.tile(np.arange(MAX_ROUNDS) * RING, (P, 1))
    cnt = np.zeros((P, 2, POOL_N))
    for base, length in ((0, SEQ), (POOL_LAT - PP, LAT)):
        t = np.arange(length)
        for g, w in enumerate((2, 4, 8, 16)):
            n = np.clip(t + w // 2, 0, length) - np.clip(t - w // 2, 0, length)
            cnt[64 * (g % 2):64 * (g % 2) + 64, g // 2, base:base + length] = (1.0 / n)
    c["inv"] = cnt.reshape(P, 2 * POOL_N)
    table = np.concatenate([c[n].reshape(P, k) for n, k in CONST_COLS], axis=1).astype(np.float32)
    iota = np.concatenate([np.tile(np.arange(PAIRS), (P, 1)), c["tri"]], axis=1).astype(np.float32)
    lam = np.array([0.8 - 0.6 * math.exp(-0.3 * l) for l in range(DEPTH)])
    lam = np.stack([lam, 1.0 - lam], axis=-1)[:, None, :].repeat(P, axis=1).astype(np.float32)
    return table, iota, lam


class Signal:

    def __init__(self, sem, per_layer, step=1, credit=0):
        self.sem, self.per_layer, self.step, self.credit = sem, per_layer, step, credit

    def at(self, l, n):
        return (l * self.per_layer + n) * self.step + self.credit


class Steps:

    def __init__(self, signal):
        self.raised, self.n = signal, 0

    def add(self, ins):
        self.n += 1
        ins.then_inc(self.raised.sem, 1)
        return self.n

    def check(self):
        assert self.n == self.raised.per_layer, (self.raised.sem, self.n, self.raised.per_layer)


ACT_STEPS = 0
DVE_STEPS = 199


def build(nc, g, consts, iota_dram, lam_dram, y_prompt, y_sample, new_k, new_v):
    with ExitStack() as ctx:
        def sb(name, shape, dt=F32):
            return ctx.enter_context(nc.sbuf_tensor(name, shape, dt))

        def signal(name, per_layer, step=1, credit=0):
            return Signal(ctx.enter_context(nc.semaphore(name)), per_layer, step, credit)

        ring = sb("ring", [P, RING, SLOT])
        tail = sb("tail", [P, KD * 256])
        xT = sb("xT", [P, KD, T])
        uT = sb("uT", [P, KD, T])
        XS = max(KD * PADDED, NT * (D + PAIRS) + 2 * PAIRS)
        arena = sb("arena", [P, 2 * XS])
        PTw = sb("PTw", [P, ST, T])
        cst = sb("cst", [P, sum(n for _, n in CONST_COLS)])
        pool_blk = sb("pool_blk", [P, 2, P])
        conv_pw = sb("conv_pw", [P, 2, CONV])
        krow = sb("krow", [P, QK])
        vec_rows = sb("vec_rows", [NVEC, P])
        vec = sb("vec", [P, NVEC])
        dw = sb("dw", [P, 2, TAPS])
        router_w = sb("router_w", [P, KD, NG + NE])
        router_b = sb("router_b", [NG + NE, 1])
        modT = sb("modT", [P, NMOD, 2])
        sT = sb("sT", [P, 2 * KD + 30])
        lam_in = sb("lam_in", [1, 4, HD])
        lam_c = sb("lam_c", [P, 2])
        lam_s = sb("lam_s", [1, 4])
        nlam = sb("nlam", [P, 1])
        subg = sb("subg", [P, 1])
        epsc = sb("epsc", [P, 1])
        chunk_tab = sb("chunk_tab", [1, 2, MAX_ROUNDS * RING], I32)
        rounds_tab = sb("rounds_tab", [1, DEPTH], I32)
        before_f = sb("before_f", [1, DEPTH + 1])
        before_tab = sb("before_tab", [1, DEPTH + 1], I32)

        C, at = {}, 0
        for name, n in CONST_COLS:
            C[name] = cst[:, at:at + n]
            at += n
        ident = C["ident"]

        def place(base, *sizes):
            out, at = [], base
            for n in sizes:
                out.append(arena[:, at:at + n])
                at += n
            return out, at

        (mixT, qT, kT, ckT), end = place(0, KD * T, HEADS * T, HEADS * T, HEADS * PAST)
        assert end <= XS
        (vrow, cv, ck_rows, apad, glu, cacc, probs, dw_rows), end = place(
            XS, NT * AW, AW, QK, 2 * POOL_COLS, 2 * GLU_COLS, 2 * CONV_N, 4 * T, CONV)
        assert end <= 2 * XS
        mixT = mixT.rearrange("p (m t) -> p m t", m=KD)
        qT = qT.rearrange("p (h t) -> p h t", h=HEADS)
        kT = kT.rearrange("p (h t) -> p h t", h=HEADS)
        ckT = ckT.rearrange("p (h t) -> p h t", h=HEADS)
        vrow = vrow.rearrange("p (t n) -> p t n", t=NT)
        apad = apad.rearrange("p (c n) -> p c n", c=2)
        glu = glu.rearrange("p (c n) -> p c n", c=2)
        cacc = cacc.rearrange("p (c n) -> p c n", c=2)
        csil = arena[:, XS + NT * AW + AW + QK + 2 * POOL_COLS:][:, 0:2 * T].rearrange("p (c n) -> p c n", c=2)
        sq_out = cacc.rearrange("p c n -> p (c n)")[:, 0:6 * VD].rearrange("p (b n) -> p b n", b=6)
        probs = probs.rearrange("p (b m n) -> p b m n", b=2, m=2)
        rope_t = probs.rearrange("p b m n -> p (b m n)")[:, 0:4 * LAT].rearrange("p (b n) -> p b n", b=4)
        uflat = uT[:].rearrange("p m t -> p (m t)")
        aT = uflat[:, 0:2 * T].rearrange("p (b k q) -> p b k q", b=2, k=NT)
        orow = uflat[:, 2 * T:2 * T + NT * AW].rearrange("p (t h e) -> p t h e", t=NT, h=HEADS)
        crow = uflat[:, 2 * T + NT * AW:2 * T + NT * AW + NT * CONV].rearrange("p (t n) -> p t n", t=NT)
        ptflat = PTw[:].rearrange("p s t -> p (s t)")
        sumX = ptflat[:, 0:2 * POOL_COLS].rearrange("p (c n) -> p c n", c=2)
        sumY = ptflat[:, 2 * POOL_COLS:4 * POOL_COLS].rearrange("p (c n) -> p c n", c=2)
        mrow = arena[:, 0:2 * HALF].rearrange("p (b n) -> p b n", b=2)
        XsT = arena[:, 0:KD * PADDED].rearrange("p (k n) -> p k n", k=KD)
        YsT = arena[:, XS:XS + KD * PADDED].rearrange("p (k n) -> p k n", k=KD)
        Ysr = arena[:, 0:ST * D].rearrange("p (s n) -> p s n", s=ST)
        urow = arena[:, XS:XS + NT * D].rearrange("p (t n) -> p t n", t=NT)
        Pm = arena[:, XS + NT * D:XS + NT * D + NT * PAIRS].rearrange("p (t n) -> p t n", t=NT)
        Pw = arena[:, XS + NT * (D + PAIRS):XS + NT * (D + PAIRS) + 2 * PAIRS].rearrange("p (t n) -> p t n", t=2)
        assert XS + NT * (D + PAIRS) + 2 * PAIRS <= 2 * XS
        sg = tail[:, 0:4 * W].rearrange("p (b f n) -> p b f n", b=2, f=2)
        assert 8 * W <= PAIRS
        hT = tail[:, 4 * W:8 * W].rearrange("p (b f n) -> p b f n", b=2, f=2)
        iota_tri = tail[:, PAIRS:2 * PAIRS + P]
        iota, tri = iota_tri[:, 0:PAIRS], iota_tri[:, PAIRS:]
        ln_t = arena[:, XS + NT * AW:XS + NT * AW + (2 + KD) * T].rearrange("p (b n) -> p b n", b=2 + KD)
        xrow = arena[:, 0:NT * D].rearrange("p (t n) -> p t n", t=NT)
        RT_COLS = NT * (NG + NE) + NT * NG + 4 * NT * NE
        at = [0]

        def rts(*shape):
            n = int(np.prod(shape))
            v = arena[:, at[0]:at[0] + n]
            at[0] += n
            return v if len(shape) == 1 else v.rearrange("p (a b) -> p a b", a=shape[0])
        lg = rts(NT, NG + NE)
        og = rts(NT, NG)
        o1, o2 = rts(NT, NE), rts(NT, NE)
        etmp, asg = rts(NT, NE), rts(NT, NE)
        r3 = sb("r3", [P, 15, NT])
        gmax, gsum, gw, m1, m2, cm, q, s1, s2, w1, w2, rq, gcm, c1, c2 = [r3[:, i, :] for i in range(15)]
        assert at[0] == RT_COLS
        asg_flat = asg.rearrange("p t n -> p (t n)")
        lgT = arena[0:NG + NE, RT_COLS:RT_COLS + T]
        tot, start, cb, le, dd, ce = [tail[:, 2 * PAIRS + P + (NE + 1) * i:2 * PAIRS + P + (NE + 1) * (i + 1)] for i in range(6)]
        gtmp = tail[:, 2 * PAIRS + P + 6 * (NE + 1):][:, 0:NT * NG].rearrange("p (a b) -> p a b", a=NT)
        chk = sb("chk", [P, 4])
        small = sb("small", [P, 2, 2, 4])
        rnd = sb("rnd", [P, MAX_ROUNDS + 1])
        bstat = sb("bstat", [P, NT, 6])
        cstat = sb("cstat", [P, NT, 4])
        rms = sb("rms", [P, 2, NT * HEADS])

        ps = ctx.enter_context(nc.psum_tensor("ps", [P, 8, 512], F32))

        s_cst = signal("const_loaded", 0, 16)
        s_xin = signal("x_rows_loaded", 0, 16)
        s_cin = signal("cond_loaded", 0, 16)
        s_xt = signal("x_turned", 0)
        s_ctl = signal("tables_zeroed", 0)
        s_crow = signal("cond_rows_silu", 0)
        s_cT = signal("cond_transposed", 0)
        s_sT = signal("cond_ready", 0)
        s_zero = signal("zeros_written", 0)
        vec_loaded = signal("vec_loaded", len(VECS) + 2, 16)
        vec_ready = signal("vec_transposed", 1, credit=1)
        dw_ready = signal("taps_transposed", 1)
        vec_copied = signal("vec_copied", 1)
        lam_dot = signal("lambda_dots", 1)
        lam_exp = signal("lambda_exps", 1)
        lam_ready = signal("lambda_ready", 1, credit=1)
        lam_done = signal("lambda_copied", 1)
        mix_loaded = signal("mixer_params_loaded", 8, 16)
        rt_loaded = signal("router_loaded", 4, 16)
        iota_loaded = signal("iota_loaded", 1, 16)
        layer_x = signal("x_ready", KD)
        slot_done = [signal(f"slot_done{s}", USES[s], credit=1) for s in range(RING)]
        slot_loaded = [signal(f"slot_loaded{s}", USES[s], 32) for s in range(RING)]
        exp_loaded = [signal(f"expert_loaded{s}", 0, 16) for s in range(RING)]
        tail_loaded = signal("tail_loaded", 1, 16)
        tail_used = signal("tail_used", 1)
        mod_rows = signal("mod_rows", 2 * MOD_STEPS)
        mod_rows_copied = signal("mod_rows_copied", MOD_STEPS)
        mod_turned = signal("mod_turned", MOD_STEPS)
        mod_added = signal("mod_bias_added", MOD_STEPS)
        mod_done = signal("mod_done", 2)
        u_act = signal("u_tiles_act", KD // 2)
        u_dve = signal("u_tiles_dve", KD // 2)
        proj_ready = signal("proj_ready", 14)
        proj_act = signal("proj_taken_act", 15)
        proj_dve = signal("proj_taken_dve", 2)
        rot_ready = signal("rot_ready", 8)
        roped = signal("roped", 8)
        ck_turned = signal("ck_turned", 2)
        ck_copied = signal("ck_copied", 2)
        lam_bc = signal("lambda_broadcast", 1)
        scores_ready = signal("scores_ready", 12)
        scores_used = signal("scores_used", 12)
        neg_max = signal("neg_max", 12)
        prob_ready = signal("prob_ready", 12)
        prob_turned = signal("prob_turned", 12)
        prob_copied = signal("prob_copied", 12)
        o_ready = signal("o_ready", 12)
        o_copied = signal("o_copied", 12)
        pads_zero = signal("pads_zero", 1)
        logits_T = signal("logits_columns", 1)
        logits_copied = signal("logits_columns_copied", 1)
        conv_done = signal("conv_done", 1)
        pool_done = signal("pool_sums_done", 1)
        pool_ready = signal("pool_mixed", 2)
        o_squared = signal("o_rows_squared", 12)
        rms_sd = signal("rms_root", 1)
        o_normed = signal("o_normed", 1)
        o_turned = signal("o_turned", HEADS)
        crow_ready = signal("conv_rows_turned", NT)
        cln_var = signal("conv_var", 1)
        cln_sd = signal("conv_root", 1)
        cln_done = signal("conv_rows_normed", 1)
        cback = signal("conv_turned_back", 2)
        csil_ready = signal("conv_silu", 2)
        cpw_ready = signal("conv_pointwise", 2)
        mix_ready = signal("mix_tiles", KD)
        y1_ready = signal("y1_ready", KD - 2)
        y2_ready = signal("y2_ready", KD)
        gated = signal("y_gated", 2 * KD)
        z_ready = signal("z_ready", 2 * KD)
        mean_ready = signal("mean_ready", 2)
        centred = signal("centred", 2 * KD)
        squared = signal("squared", 2 * KD)
        sq_used = signal("squares_summed", 2)
        root_ready = signal("root_ready", 2)
        normed = signal("normed", 2 * KD)
        x_mid = signal("x_mid", KD // 2)
        x_mid_dve = signal("x_mid_dve", KD // 2)
        u2_act = signal("u2_act", KD // 2)
        u2_dve = signal("u2_dve", KD // 2)
        logits_ready = signal("logits_ready", 1)
        urow_turned = signal("urow_turned", 6)
        urow_ready = signal("urow_ready", 6)
        gdiff = signal("group_diff", 1)
        gexp = signal("group_exp", 1)
        ediff = signal("expert_diff", 1)
        eexp = signal("expert_exp", 1)
        assign_ready = signal("assignment", 1)
        ranks_ready = signal("ranks", 1)
        chunk_cols = signal("chunk_columns", 1)
        chunk_turned = signal("chunk_turned", 1)
        chunks_ready = signal("chunk_list", 1)
        P_ready = signal("gather_matrix", NT)
        Pw_ready = signal("weighted_matrix", NT)
        Pw_turned = signal("weighted_turned", 2 * NT)
        PT_ready = signal("unsort_matrix", 2 * NT)
        gath_ready = signal("gathered", 2 * KD)
        xs_act = signal("sorted_x_act", KD)
        xs_dve = signal("sorted_x_dve", KD)
        gu_ready = signal("gate_up_ready", 0)
        silu_ready = signal("silu_ready", 0)
        h_ready = signal("h_ready", 0)
        down_ready = signal("down_half_ready", 0)
        down_act = signal("down_taken_act", 0, credit=2)
        down_dve = signal("down_taken_dve", 0, credit=2)
        ys_turned = signal("ys_turned", 12, credit=1)
        ys_act = signal("ys_rows_act", 6)
        ys_dve = signal("ys_rows_dve", 6)
        out_k = signal("new_kv_stored", 2, 16)
        kv_free = signal("kv_rows_free", 1, credit=1)
        out_turned = signal("out_turned", 0)
        out_rows = signal("out_rows", 0)
        s_out = signal("y_stored", 0, 16)
        dve_self = signal("dve_step", DVE_STEPS)
        act_self = signal("act_step", ACT_STEPS)

        def engine_wait(eng):
            def wait(sig, l, n, alone=False):
                eng.wait_ge(sig.sem, sig.at(l, n))
                if alone:
                    eng.nop(nofuse=True)
            return wait

        w_mod, w_in, w_out = g["w_mod"], g["w_in"], g["w_out"]
        q0, k0, v0, c0 = POOL, POOL + QK, POOL + 2 * QK, POOL + 2 * QK + AW
        slot = [ring[:, s, :].rearrange("p (k n) -> p k n", k=KD) for s in range(RING)]
        gate_w = [ring[:, s, 0:KD * FF].rearrange("p (k f) -> p k f", k=KD) for s in range(RING)]
        up_w = [ring[:, s, KD * FF:2 * KD * FF].rearrange("p (k f) -> p k f", k=KD) for s in range(RING)]
        down_w = [ring[:, s, 2 * KD * FF:3 * KD * FF].rearrange("p (k n) -> p k n", k=2) for s in range(RING)]
        tail_w = tail[:].rearrange("p (k n) -> p k n", k=KD)
        PW_TURNS = (8, 10, 14)
        MOD_SLOTS = ((0, 1), (2, 3), (0, 1), (0, 2))
        MOD_USE = ((0, 0), (0, 0), (2, 2), (3, 2))
        SEGS = ((0, SEQ, 1), (SEQ, T, 0))
        SH1, SC1, GA1, SH2, SC2, GA2 = [i * KD for i in range(6)]

        def mod(i, v):
            return modT[:, i, v:v + 1]

        def vcol(name, i=0):
            return vec[:, VCOL[name] + i:VCOL[name] + i + 1]

        block = ctx.enter_context(nc.Block())

        @block.sync
        def _(sp):
            wait = engine_wait(sp)
            sp.dma_start(cst[:], consts).then_inc(s_cst.sem, 16)
            sp.dma_start(xrow[:, 0, :], g["x_prompt"][0]).then_inc(s_xin.sem, 16)
            sp.dma_start(xrow[:, 1:NT, :], g["x_sample"][0].rearrange("(t p) d -> p t d", p=P)).then_inc(s_xin.sem, 16)

            sp.wait_ge(s_ctl.sem, 4)
            with sp.Fori(0, DEPTH) as l:
                before = sp.value_load(before_tab[0:1, ds(l, 1)], min_val=0, max_val=DEPTH * MAX_ROUNDS)

                def load_slot(s, use, parts):
                    sp.wait_ge(slot_done[s].sem, before + l * USES[s] + (use + 1))
                    sp.nop(nofuse=True)
                    for dst, src in parts:
                        sp.dma_start(dst, src).then_inc(slot_loaded[s].sem, 16)

                def cols(w, a, b, k0_, k1_):
                    return w[ds(l, 1), k0_ * P:k1_ * P, a:b].rearrange("o (k p) n -> p (o k) n", p=P)

                h2 = KD // 2
                def load_mod(j):
                    for i in range(2):
                        s = MOD_SLOTS[j][i]
                        a = (2 * j + i) * SLOT_COLS
                        load_slot(s, MOD_USE[j][i], [(slot[s][:, 0:h2, :], cols(w_mod, a, a + SLOT_COLS, 0, h2)),
                                           (slot[s][:, h2:KD, :], cols(w_mod, a, a + SLOT_COLS, h2, KD))])

                load_mod(0)
                load_mod(1)
                load_slot(0, 1, [(slot[0][:, :, POOL:SLOT_COLS], cols(w_in, c0, c0 + 2 * CONV, 0, KD)),
                                 (slot[0][:, :, 0:POOL], cols(w_in, 0, POOL, 0, KD))])
                for s in (1, 2):
                    a = q0 + (s - 1) * SLOT_COLS
                    load_slot(s, 1, [(slot[s][:, 0:h2, :], cols(w_in, a, a + SLOT_COLS, 0, h2)),
                                     (slot[s][:, h2:KD, :], cols(w_in, a, a + SLOT_COLS, h2, KD))])
                load_slot(3, 1, [(slot[3][:, 0:h2, :], cols(w_out, 0, SLOT_COLS, 0, h2)),
                                 (slot[3][:, h2:KD, :], cols(w_out, 0, SLOT_COLS, h2, KD))])
                wait(ys_turned, l, 0, alone=True)
                sp.dma_start(tail_w, cols(w_out, SLOT_COLS, D, 0, KD)).then_inc(tail_loaded.sem, 16)
                load_mod(2)
                load_mod(3)

                wait(chunks_ready, l, 1, alone=True)
                rounds = sp.value_load(rounds_tab[0:1, ds(l, 1)], min_val=1, max_val=MAX_ROUNDS)
                with sp.Fori(0, rounds) as r:
                    for i in range(RING):
                        e = sp.value_load(chunk_tab[0:1, 0, ds(r * RING + i, 1)], min_val=0, max_val=NE - 1)
                        sp.wait_ge(slot_done[i].sem, before + r + l * USES[i] + (USES[i] + 1))
                        sp.nop(nofuse=True)
                        sp.dma_start(gate_w[i], g["w_gate"][ds(l, 1), ds(e, 1)].rearrange(
                            "o a (p k) f -> p (o a k) f", k=KD)).then_inc(exp_loaded[i].sem, 16)
                        sp.dma_start(up_w[i], g["w_up"][ds(l, 1), ds(e, 1)].rearrange(
                            "o a (p k) f -> p (o a k) f", k=KD)).then_inc(exp_loaded[i].sem, 16)
                        sp.dma_start(down_w[i], g["w_down"][ds(l, 1), ds(e, 1)].rearrange(
                            "o a (k p) n -> p (o a k) n", p=P)).then_inc(exp_loaded[i].sem, 16)

        @block.gpsimd
        def _(pool):
            wait = engine_wait(pool)
            nc.gpsimd.memset(pool_blk[:], 0.0).then_inc(s_zero.sem, 1)
            for sig in slot_done + [vec_ready, lam_ready, ys_turned, down_act, down_dve, kv_free]:
                pool.sem_inc(sig.sem, sig.credit)
            pool.dma_start(krow[0:8, 0:P], g["c"][0].rearrange("(k p) -> k p", p=P)).then_inc(s_cin.sem, 16)
            pool.dma_start(krow[0:8, P:2 * P], g["c_ctx"].rearrange("(k p) -> k p", p=P)).then_inc(s_cin.sem, 16)
            pool.wait_ge(s_zero.sem, 1)
            with pool.Fori(0, DEPTH) as l:
                def row(name, n):
                    return g[name][ds(l, 1)].rearrange("o (k p) -> (o k) p", p=P)

                wait(vec_ready, l, 0, alone=True)
                for name, n in VECS:
                    pool.dma_start(vec_rows[VCOL[name]:VCOL[name] + n, :], row(name, n)).then_inc(vec_loaded.sem, 16)
                wait(lam_ready, l, 0, alone=True)
                pool.dma_start(lam_in[:], g["diff_lambda"][ds(l, 1)]).then_inc(vec_loaded.sem, 16)
                pool.dma_start(lam_c[:], lam_dram[ds(l, 1)].rearrange("o p c -> (o p) c")).then_inc(vec_loaded.sem, 16)
                wait(layer_x, l, KD, alone=True)
                pool.dma_start(ck_rows, g["cache_k"][0, ds(l, 1)].rearrange("o t h m d -> (o t) (h m d)")).then_inc(mix_loaded.sem, 16)
                pool.dma_start(dw_rows[0:TAPS, :], g["conv_dw"][ds(l, 1)].rearrange("o k n -> (o k) n")).then_inc(mix_loaded.sem, 16)
                pool.dma_start(cv, g["cache_v"][0, ds(l, 1)].rearrange("o t h e -> (o t) (h e)")).then_inc(mix_loaded.sem, 16)
                pool.dma_start(conv_pw[:], g["conv_pw"][ds(l, 1)].rearrange("o (k p) n -> p (o k) n", p=P)).then_inc(mix_loaded.sem, 16)
                for b in range(4):
                    q = 64 * (b % 2)
                    pool.dma_start(pool_blk[q:q + 64, b // 2, q:q + 64], g["pool_w"][ds(l, 1), b].rearrange(
                        "o c d -> (o c) d")).then_inc(mix_loaded.sem, 16)
                pool.dma_start(router_w[:, :, 0:NG], g["router_grp"][ds(l, 1)].rearrange(
                    "o (k p) n -> p (o k) n", p=P)).then_inc(rt_loaded.sem, 16)
                pool.dma_start(router_w[:, :, NG:], g["router_exp"][ds(l, 1)].rearrange(
                    "o (k p) n -> p (o k) n", p=P)).then_inc(rt_loaded.sem, 16)
                pool.dma_start(router_b[0:NG, :], g["router_grp_b"][ds(l, 1)].rearrange("o n -> n o")).then_inc(rt_loaded.sem, 16)
                pool.dma_start(router_b[NG:, :], g["router_exp_b"][ds(l, 1)].rearrange("o n -> n o")).then_inc(rt_loaded.sem, 16)
                wait(ck_copied, l, 2, alone=True)
                pool.dma_start(new_k[0, ds(l, 1)].rearrange("o t h m d -> (o t) (h m d)"), krow[:]).then_inc(out_k.sem, 16)
                wait(proj_act, l, 13, alone=True)
                pool.dma_start(new_v[0, ds(l, 1)].rearrange("o t h e -> (o t) (h e)"), vrow[:, 0, :]).then_inc(out_k.sem, 16)
                wait(tail_used, l, 1, alone=True)
                pool.dma_start(iota_tri, iota_dram).then_inc(iota_loaded.sem, 16)
                wait(out_k, l, 2, alone=True)
                pool.sem_inc(kv_free.sem, 1)
            for t in range(NT):
                pool.wait_ge(out_rows.sem, 2 * t + 2)
                dst = y_prompt[0] if t == 0 else y_sample[0, (t - 1) * P:t * P, :]
                pool.dma_start(dst, xrow[:, t, :]).then_inc(s_out.sem, 16)
            pool.wait_ge(s_out.sem, 16 * NT)

        @block.tensor
        def _(pe):
            wait = engine_wait(pe)
            mm, tr = nc.tensor.matmul, nc.tensor.transpose

            pe.wait_ge(s_cst.sem, 16)
            pe.wait_ge(s_xin.sem, 32)
            for m in range(KD):
                for t in range(NT):
                    last = tr(ps[:, m, t * P:(t + 1) * P], xrow[:, t, m * P:(m + 1) * P], ident)
                last.then_inc(s_xt.sem, 1)
            pe.wait_ge(s_crow.sem, 1)
            pe.wait_ge(layer_x.sem, 1)
            for v in range(2):
                last = tr(ps[:, 0, 8 * v:8 * v + 8], krow[0:8, 256 + v * P:256 + (v + 1) * P], ident[0:8, 0:8])
            last.then_inc(s_cT.sem, 1)
            pe.wait_ge(s_sT.sem, 1)
            pe.wait_ge(s_ctl.sem, 4)

            with pe.Fori(0, DEPTH) as l:
                before = pe.value_load(before_tab[0:1, ds(l, 1)], min_val=0, max_val=DEPTH * MAX_ROUNDS)
                wait(layer_x, l, KD)

                def vectors():
                    wait(vec_loaded, l, len(VECS) + 2)
                    tr(ps[:, 6, 0:NVEC], vec_rows[:], ident[0:NVEC, 0:NVEC]).then_inc(vec_ready.sem, 1)
                    wait(mix_loaded, l, 8, alone=True)
                    for c in range(2):
                        last = tr(ps[:, 5, 32 * c:32 * c + TAPS], dw_rows[0:TAPS, c * P:(c + 1) * P],
                                  ident[0:TAPS, 0:TAPS])
                    last.then_inc(dw_ready.sem, 1)
                    wait(lam_ready, l, 1)
                    mm(ps[:, 4, 0:1], C["ones"][0:1, :], lam_s[0:1, 3:4], start=True, stop=True).then_inc(lam_bc.sem, 1)

                def mod_product(j, bank, ks):
                    sa, sb_ = MOD_SLOTS[j]
                    if ks[0] == 0:
                        for s, use in zip(MOD_SLOTS[j], MOD_USE[j]):
                            pe.wait_ge(slot_loaded[s].sem, l * (32 * USES[s]) + 32 * (use + 1))
                    for k in ks:
                        both = sT[:, 2 * k:2 * k + 32]
                        for g_ in range(4):
                            s = (sa, sb_)[g_ // 2]
                            last = mm(ps[32 * g_:32 * (g_ + 1), bank, 0:HALF], both,
                                      slot[s][:, k, (g_ % 2) * HALF:(g_ % 2 + 1) * HALF],
                                      start=(k == 0), stop=(k == KD - 1), tile_position=(0, 32 * g_))
                            if k == KD - 1:
                                last.then_inc((slot_done[s] if g_ % 2 else mod_rows).sem, 1)

                def mod_turn(j, bank):
                    wait(mod_rows_copied, l, j + 1)
                    for i in range(GROUP_TILES):
                        last = tr(ps[:, bank, i * P:(i + 1) * P], mrow[:, j % 2, i * P:(i + 1) * P], ident)
                    last.then_inc(mod_turned.sem, 1)

                mod_product(0, 0, range(KD))
                mod_product(1, 1, range(KD))
                vectors()
                mod_turn(0, 2)
                mod_turn(1, 3)

                ACT_TAKES = [0, 2] + list(range(4, 17))

                def project(n, s, c, rows=None, sig=proj_ready):
                    if n >= 4:
                        if n - 4 in ACT_TAKES:
                            wait(proj_act, l, ACT_TAKES.index(n - 4) + 1)
                        else:
                            wait(proj_dve, l, (n - 4) // 2 + 1)
                    for k in range(KD):
                        if rows is None:
                            last = mm(ps[:, n % 4, 0:T], slot[s][:, k, c:c + P], uT[:, k, :],
                                      start=(k == 0), stop=(k == KD - 1))
                        else:
                            last = mm(ps[:, n % 4, 0:AW], uT[:, k, rows * P:(rows + 1) * P], slot[s][:, k, c:c + AW],
                                      start=(k == 0), stop=(k == KD - 1))
                    last.then_inc(sig.sem, 1)

                def rotate(n):
                    wait(proj_act, l, 4 + n + 1)
                    if n >= 2:
                        wait(roped, l, n - 1)
                    src = (qT if n < HEADS else kT)[:, n % HEADS, SEQ:T]
                    mm(ps[:, 4 + n % 2, 0:LAT], C["rot"], src, start=True, stop=True).then_inc(rot_ready.sem, 1)

                wait(u_act, l, KD // 2)
                wait(u_dve, l, KD // 2)
                wait(lam_done, l, 1)
                pe.wait_ge(slot_loaded[0].sem, l * (32 * USES[0]) + 64)
                for n, c in ((0, 4), (1, 2), (2, 5), (3, 3)):
                    project(n, 0, c * P)
                project(4, 0, 0)
                project(5, 0, P, sig=slot_done[0])
                pe.wait_ge(slot_loaded[1].sem, l * (32 * USES[1]) + 64)
                for n in range(8):
                    if n == 6:
                        pe.wait_ge(slot_loaded[2].sem, l * (32 * USES[2]) + 64)
                    project(6 + n, 1 + n // 6, (n % 6) * P, sig=slot_done[1] if n == 5 else proj_ready)
                    if n >= 1:
                        rotate(n - 1)
                for t in range(NT):
                    project(14 + t, 2, 2 * P, rows=t, sig=slot_done[2] if t == NT - 1 else proj_ready)
                    if t == 0:
                        rotate(7)
                        mod_product(2, 7, range(KD))
                mod_turn(2, 7)

                wait(proj_act, l, 13)
                for h in range(HEADS):
                    last = tr(ps[:, 2, h * P:(h + 1) * P], ck_rows[:, h * P:(h + 1) * P], ident)
                last.then_inc(ck_turned.sem, 1)
                wait(proj_act, l, 14)
                for h in range(HEADS):
                    last = tr(ps[:, 3, h * P:(h + 1) * P], kT[:, h, 0:SEQ], ident)
                last.then_inc(ck_turned.sem, 1)
                wait(conv_done, l, 1)
                for t in range(NT):
                    if t == 2:
                        wait(mod_added, l, 3)
                    a = 0 if t == 0 else CONV_LAT + (t - 1) * P
                    for c in range(2):
                        last = tr(ps[:, 6 + t // 2, (t % 2) * CONV + c * P:(t % 2) * CONV + (c + 1) * P],
                                  cacc[:, c, a:a + P], ident)
                    last.then_inc(crow_ready.sem, 1)

                wait(ck_copied, l, 2)
                wait(roped, l, 8)

                def scores(u):
                    h, t = u // NT, u % NT
                    if u >= 2:
                        wait(scores_used, l, u - 1)
                    for m in range(2):
                        r = slice(64 * m, 64 * m + 64)
                        b = 2 * (u % 2) + m
                        q = qT[r, h, t * P:(t + 1) * P]
                        if t == 0:
                            last = mm(ps[:, b, 0:SEQ], q, kT[r, h, 0:SEQ], start=True, stop=True)
                        else:
                            mm(ps[:, b, 0:LAT], q, kT[r, h, SEQ:T], start=True, stop=True)
                            last = mm(ps[:, b, LAT:LAT + PAST], q, ckT[r, h, :], start=True, stop=True)
                    last.then_inc(scores_ready.sem, 1)

                def turn(u):
                    wait(prob_ready, l, u + 1)
                    if u >= 2:
                        wait(prob_copied, l, u - 1)
                    for k in range(1 if u % NT == 0 else NT):
                        last = tr(ps[:, 4 + u % 2, k * P:(k + 1) * P], probs[:, u % 2, 0, k * P:(k + 1) * P], ident)
                    last.then_inc(prob_turned.sem, 1)

                def values(u):
                    h, t = u // NT, u % NT
                    wait(prob_copied, l, u + 1)
                    if u >= 1:
                        wait(o_copied, l, u)
                    hs = slice(h * VD, (h + 1) * VD)
                    vs = [vrow[:, 0, hs]] if t == 0 else [vrow[:, 1, hs], vrow[:, 2, hs], cv[:, hs]]
                    for k, v in enumerate(vs):
                        last = mm(ps[:, 6, 0:VD], aT[:, u % 2, k, :], v, start=(k == 0), stop=(k == len(vs) - 1))
                    last.then_inc(o_ready.sem, 1)

                wait(proj_act, l, 15)
                NU = HEADS * NT

                def pool_product():
                    wait(pool_done, l, 1)
                    wait(scores_used, l, NU - 1)
                    for c in range(2):
                        mm(ps[:, c, 0:SEQ], pool_blk[:, c, :], sumX[:, c, PP:PP + SEQ], start=True, stop=True)
                        mm(ps[:, c, SEQ:T], pool_blk[:, c, :], sumX[:, c, POOL_LAT:POOL_LAT + LAT],
                           start=True, stop=True).then_inc(pool_ready.sem, 1)

                def conv_back():
                    wait(scores_used, l, NU)
                    for c in range(2):
                        for t in range(NT):
                            last = tr(ps[:, 2 + c, t * P:(t + 1) * P], crow[:, t, c * P:(c + 1) * P], ident)
                        last.then_inc(cback.sem, 1)

                for u in range(NU + 3):
                    if u < NU:
                        scores(u)
                    if u == 3:
                        wait(cln_done, l, 1)
                    if u == NU:
                        pool_product()
                    if u == NU + 1:
                        conv_back()
                    if 2 <= u and u - 2 < NU:
                        turn(u - 2)
                    if u >= 3:
                        values(u - 3)
                    if u in (5, 6):
                        mod_product(3, 7, range(4 * (u - 5), 4 * (u - 5) + 4))
                    elif u == 9:
                        mod_turn(3, 7)
                wait(o_normed, l, 1)
                wait(mod_added, l, MOD_STEPS)
                wait(mix_ready, l, 2)
                for h in range(HEADS):
                    for t in range(NT):
                        last = tr(ps[:, (6 + h) % 8, t * P:(t + 1) * P], orow[:, t, h, :], ident)
                    last.then_inc(o_turned.sem, 1)
                wait(csil_ready, l, 2)
                for n in range(2):
                    for c in range(2):
                        last = mm(ps[:, 4 + n, 0:T], conv_pw[:, c, n * P:(n + 1) * P], csil[:, c, :],
                                  start=(c == 0), stop=(c == 1))
                    last.then_inc(cpw_ready.sem, 1)

                def layer_norm(which, n):
                    wait(z_ready, l, which * KD + n + 1)
                    last = mm(ps[:, 4, 0:T], C["ones"], uT[:, n, :], start=(n == 0), stop=(n == KD - 1))
                    if n == KD - 1:
                        last.then_inc(mean_ready.sem, 1)
                        for m in range(KD):
                            wait(squared, l, which * KD + m + 1)
                            last = mm(ps[:, 5, 0:T], C["ones"], ln_t[:, 2 + m, :], start=(m == 0), stop=(m == KD - 1))
                        last.then_inc(sq_used.sem, 1)

                pe.wait_ge(slot_loaded[3].sem, l * (32 * USES[3]) + 64)
                wait(tail_loaded, l, 1)
                for m in range(KD):
                    if m >= 4:
                        wait(gated, l, m - 3)
                    for k in range(KD):
                        if m == 0 and k in (0, 6, 7):
                            wait(mix_ready, l, max(k + 1, 6))
                        wt = slot[3][:, k, m * P:(m + 1) * P] if m < 6 else tail_w[:, k, (m - 6) * P:(m - 5) * P]
                        last = mm(ps[:, m % 4, 0:T], wt, mixT[:, k, :], start=(k == 0), stop=(k == KD - 1))
                    last.then_inc({5: slot_done[3], 7: tail_used}.get(m, y1_ready).sem, 1)
                    if m >= 1:
                        layer_norm(0, m - 1)
                layer_norm(0, KD - 1)

                wait(rt_loaded, l, 4)
                for k in range(KD):
                    wait(u2_dve if k % 2 else u2_act, l, k // 2 + 1)
                    last = mm(ps[0:NG + NE, 6, 0:T], router_w[:, k, :], uT[:, k, :], start=(k == 0), stop=(k == KD - 1))
                last.then_inc(logits_T.sem, 1)
                wait(logits_copied, l, 1, alone=True)
                for t in range(NT):
                    last = tr(ps[:, 5, t * (NG + NE):(t + 1) * (NG + NE)], lgT[:, t * P:(t + 1) * P],
                              ident[0:NG + NE, 0:NG + NE])
                last.then_inc(logits_ready.sem, 1)
                for n in range(6):
                    t, h = n // 2, n % 2
                    if n >= 4:
                        wait(urow_ready, l, n - 3)
                    for m in range(4):
                        last = tr(ps[:, n % 4, m * P:(m + 1) * P], uT[:, 4 * h + m, t * P:(t + 1) * P], ident)
                    last.then_inc(urow_turned.sem, 1)
                wait(assign_ready, l, 1)
                wait(iota_loaded, l, 1)
                mm(ps[:, 7, 0:NT * NE], tri, asg_flat, start=True, stop=False, skip_group_check=True)
                for n in range(NT, 0, -1):
                    last = mm(ps[:, 7, (NT + 1 - n) * NE:(NT + 1) * NE], C["ones"], asg_flat[:, 0:n * NE], start=False,
                              stop=(n == 1), skip_group_check=True)
                last.then_inc(ranks_ready.sem, 1)
                wait(urow_ready, l, 6)
                wait(P_ready, l, NT)

                def chunk_turn():
                    wait(chunk_cols, l, 1)
                    for i in range(2):
                        last = tr(ps[0:1, 6, i * P:(i + 1) * P], chk[:, i:i + 1], ident)
                    last.then_inc(chunk_turned.sem, 1)

                def weighted_turn(t):
                    wait(Pw_ready, l, t + 1)
                    if t >= 1:
                        wait(PT_ready, l, 2 * t)
                    for h in range(2):
                        for s in range(3):
                            last = tr(ps[:, 4 + h, s * P:(s + 1) * P], Pw[:, t % 2, (3 * h + s) * P:(3 * h + s + 1) * P], ident)
                        last.then_inc(Pw_turned.sem, 1)

                for n in range(2 * KD):
                    k, h = n // 2, n % 2
                    if n == 5:
                        chunk_turn()
                    if n in PW_TURNS:
                        weighted_turn(PW_TURNS.index(n))
                    if n >= 4:
                        wait(xs_act if h == 0 else xs_dve, l, k - 1)
                    a, b = (0, 512) if h == 0 else (512, PAIRS)
                    for t in range(NT):
                        last = mm(ps[:, n % 4, 0:b - a], urow[:, t, k * P:(k + 1) * P], Pm[:, t, a:b],
                                  start=(t == 0), stop=(t == NT - 1))
                    last.then_inc(gath_ready.sem, 1)
                wait(xs_act, l, KD)
                wait(xs_dve, l, KD)
                wait(PT_ready, l, 2 * NT)
                wait(chunks_ready, l, 1)
                rounds = pe.value_load(rounds_tab[0:1, ds(l, 1)], min_val=1, max_val=MAX_ROUNDS)
                with pe.Fori(0, rounds) as r:
                    done = (before + r) * RING

                    def gate_up(i):
                        off = pe.value_load(chunk_tab[0:1, 1, ds(r * RING + i, 1)], min_val=0, max_val=PAIRS)
                        pe.wait_ge(exp_loaded[i].sem, (before + r) * 48 + 48)
                        for half, wt in ((0, gate_w[i]), (1, up_w[i])):
                            for f in range(2):
                                o = (2 * half + f) * W
                                for k in range(KD):
                                    last = mm(ps[:, i % 2, o:o + W], wt[:, k, f * P:(f + 1) * P], XsT[:, k, ds(off, W)],
                                              start=(k == 0), stop=(k == KD - 1))
                        last.then_inc(gu_ready.sem, 1)

                    def down(i):
                        pe.wait_ge(h_ready.sem, done + (i + 1))
                        pe.wait_ge(down_act.sem, done + (i - 1 + 2))
                        pe.wait_ge(down_dve.sem, done + (i - 1 + 2))
                        for m in range(KD):
                            for f in range(2):
                                last = mm(ps[:, 2 + 2 * (i % 2) + m // 4, (m % 4) * W:(m % 4 + 1) * W],
                                          down_w[i][:, f, m * P:(m + 1) * P], hT[:, i % 2, f, :],
                                          start=(f == 0), stop=(f == 1))
                            if m == KD // 2 - 1:
                                last.then_inc(down_ready.sem, 1)
                        last.then_inc(slot_done[i].sem, 1)

                    for i in range(RING):
                        gate_up(i)
                        if i >= 1:
                            down(i - 1)
                    down(RING - 1)

                after = (before + rounds) * RING
                pe.wait_ge(down_act.sem, after + 2)
                pe.wait_ge(down_dve.sem, after + 2)
                for n in range(2 * ST):
                    s, h = n // 2, n % 2
                    if n >= 4:
                        wait(ys_act if h == 0 else ys_dve, l, s - 1)
                    for m in range(4):
                        last = tr(ps[:, n % 4, m * P:(m + 1) * P], YsT[:, 4 * h + m, s * P:(s + 1) * P], ident)
                    last.then_inc(ys_turned.sem, 1)
                wait(ys_act, l, ST)
                wait(ys_dve, l, ST)
                for m in range(KD):
                    if m >= 4:
                        wait(gated, l, KD + m - 3)
                    for s in range(ST):
                        last = mm(ps[:, m % 4, 0:T], Ysr[:, s, m * P:(m + 1) * P], PTw[:, s, :],
                                  start=(s == 0), stop=(s == ST - 1))
                    last.then_inc(y2_ready.sem, 1)
                    if m >= 1:
                        layer_norm(1, m - 1)
                layer_norm(1, KD - 1)

            wait(layer_x, DEPTH, KD)
            for n in range(2 * NT):
                t, h = n // 2, n % 2
                for m in range(4):
                    last = tr(ps[:, n, m * P:(m + 1) * P], xT[:, 4 * h + m, t * P:(t + 1) * P], ident)
                last.then_inc(out_turned.sem, 1)

        @block.scalar
        def _(act):
            wait = engine_wait(act)
            fn = nc.scalar.activation
            ID = ACT.Identity

            act.wait_ge(s_cin.sem, 32)
            fn(krow[0:8, 2 * P:4 * P], krow[0:8, 0:2 * P], ACT.Silu).then_inc(s_crow.sem, 1)
            for m in range(KD):
                act.wait_ge(s_xt.sem, m + 1)
                fn(xT[:, m, :], ps[:, m, 0:T], ID).then_inc(layer_x.sem, 1)
            act.wait_ge(s_cT.sem, 1)
            fn(sT[:, 0:2 * KD].rearrange("p (k v) -> p v k", v=2), ps[:, 0, 0:16].rearrange("p (v k) -> p v k", v=2), ID).then_inc(s_sT.sem, 1)
            act.wait_ge(s_ctl.sem, 4)

            with act.Fori(0, DEPTH) as l:
                before = act.value_load(before_tab[0:1, ds(l, 1)], min_val=0, max_val=DEPTH * MAX_ROUNDS)

                def modulate(m, shift, scale, sig):
                    for a, b, v in SEGS:
                        last = fn(uT[:, m, a:b], xT[:, m, a:b], ID, bias=mod(shift + m, v), scale=mod(scale + m, v))
                    last.then_inc(sig.sem, 1)

                def mod_rows_out(j, bank):
                    wait(mod_rows, l, 2 * j + 2)
                    for s, use in zip(MOD_SLOTS[j], MOD_USE[j]):
                        act.wait_ge(slot_done[s].sem, before + l * USES[s] + (use + 1 + 1))
                    if j >= 2:
                        wait(mod_turned, l, j - 1)
                    fn(mrow[:, j % 2, :], ps[:, bank, 0:HALF], ID).then_inc(mod_rows_copied.sem, 1)

                wait(layer_x, l, KD)
                mod_rows_out(0, 0)
                mod_rows_out(1, 1)
                wait(lam_dot, l, 1)
                fn(lam_s[:, 0:2], lam_s[:, 0:2], ACT.Exp).then_inc(lam_exp.sem, 1)
                wait(mod_done, l, 1)
                for m in range(0, KD, 2):
                    modulate(m, SH1, SC1, u_act)

                def proj_wait(n):
                    if n == 5:
                        act.wait_ge(slot_done[0].sem, before + l * USES[0] + (2 + 1))
                    elif n == 11:
                        act.wait_ge(slot_done[1].sem, before + l * USES[1] + (2 + 1))
                    elif n == 16:
                        act.wait_ge(slot_done[2].sem, before + l * USES[2] + (2 + 1))
                    else:
                        wait(proj_ready, l, n + 1 - (n > 5) - (n > 11))

                wait(pads_zero, l, 1)
                for n in (0, 2):
                    proj_wait(n)
                    c = n // 2
                    fn(glu[:, c, CP:CP + SEQ], ps[:, n % 4, 0:SEQ], ACT.Sigmoid)
                    fn(glu[:, c, GLU_LAT:GLU_LAT + LAT], ps[:, n % 4, SEQ:T], ACT.Sigmoid).then_inc(proj_act.sem, 1)
                for n in (4, 5):
                    proj_wait(n)
                    fn(apad[:, n - 4, PP:PP + SEQ], ps[:, n % 4, 0:SEQ], ID)
                    fn(apad[:, n - 4, POOL_LAT:POOL_LAT + LAT], ps[:, n % 4, SEQ:T], ID).then_inc(proj_act.sem, 1)
                for n in range(8):
                    proj_wait(6 + n)
                    fn((qT if n < HEADS else kT)[:, n % HEADS, :], ps[:, (6 + n) % 4, 0:T], ID,
                       scale=HD ** -0.5 if n < HEADS else 1.0).then_inc(proj_act.sem, 1)
                wait(kv_free, l, 0)
                for t in range(NT):
                    proj_wait(14 + t)
                    fn(vrow[:, t, :], ps[:, (14 + t) % 4, 0:AW], ID).then_inc(proj_act.sem, 1)
                    if t == 1:
                        mod_rows_out(2, 7)
                wait(ck_turned, l, 1)
                fn(ckT, ps[:, 2, :].rearrange("p (h t) -> p h t", h=HEADS), ID).then_inc(ck_copied.sem, 1)
                wait(ck_turned, l, 2)
                fn(krow[:], ps[:, 3, :], ID).then_inc(ck_copied.sem, 1)
                wait(cln_var, l, 1)
                fn(cstat[:, :, 2], cstat[:, :, 1], ACT.Sqrt, bias=epsc[:]).then_inc(cln_sd.sem, 1)

                NU = HEADS * NT
                for u in range(NU + 3):
                    if 2 <= u and u - 2 < NU:
                        w_ = u - 2
                        n = P * (1 if w_ % NT == 0 else NT)
                        wait(prob_turned, l, w_ + 1)
                        if w_ >= 2:
                            wait(o_ready, l, w_ - 1)
                        fn(aT[:, w_ % 2].rearrange("p k q -> p (k q)")[:, 0:n], ps[:, 4 + w_ % 2, 0:n], ID).then_inc(prob_copied.sem, 1)
                    if u < NU:
                        n = SEQ if u % NT == 0 else LAT + PAST
                        wait(neg_max, l, u + 1)
                        if u >= 2:
                            wait(prob_turned, l, u - 1)
                        for m in range(2):
                            last = fn(probs[:, u % 2, m, 0:n], ps[:, 2 * (u % 2) + m, 0:n], ACT.Exp,
                                      bias=small[:, u % 2, m, 1:2], accum_out=small[:, u % 2, m, 2:3])
                        last.then_inc(scores_used.sem, 1)
                    if u >= 3:
                        w_ = u - 3
                        wait(o_ready, l, w_ + 1)
                        h, t = w_ // NT, w_ % NT
                        if w_ >= 6:
                            wait(o_squared, l, w_ - 5)
                        fn(sq_out[:, w_ % 6, :], ps[:, 6, 0:VD], ACT.Square,
                           accum_out=rms[:, 0, t * HEADS + h:t * HEADS + h + 1]).then_inc(o_squared.sem, 1)
                        fn(orow[:, t, h, :], ps[:, 6, 0:VD], ID).then_inc(o_copied.sem, 1)
                    if u == 7:
                        mod_rows_out(3, 7)
                    if u == NU + 1:
                        wait(vec_copied, l, 1)
                        for c in range(2):
                            wait(pool_ready, l, c + 1)
                            fn(mixT[:, c, :], ps[:, c, 0:T], ID, scale=vcol("pool_scale", c)).then_inc(mix_ready.sem, 1)

                wait(o_squared, l, NU)
                fn(rms[:, 1, :], rms[:, 0, :], ACT.Sqrt, bias=epsc[:], scale=1.0 / VD).then_inc(rms_sd.sem, 1)
                for c in range(2):
                    wait(cback, l, c + 1)
                    fn(csil[:, c, :], ps[:, 2 + c, 0:T], ACT.Silu, bias=vcol("conv_ln_b", c),
                       scale=vcol("conv_ln_g", c)).then_inc(csil_ready.sem, 1)
                for h in range(HEADS):
                    wait(o_turned, l, h + 1)
                    fn(mixT[:, 2 + h, :], ps[:, (6 + h) % 8, 0:T], ID, scale=subg[:]).then_inc(mix_ready.sem, 1)
                for c in range(2):
                    wait(cpw_ready, l, c + 1)
                    fn(mixT[:, 6 + c, :], ps[:, 4 + c, 0:T], ID).then_inc(mix_ready.sem, 1)

                def gate_tile(m, gate):
                    for a, b, v in SEGS:
                        last = fn(uT[:, m, a:b], ps[:, m % 4, a:b], ID, scale=mod(gate + m, v))
                    last.then_inc(gated.sem, 1)

                def squares_root(which):
                    for m in range(KD):
                        wait(centred, l, which * KD + m + 1)
                        fn(ln_t[:, 2 + m, :], uT[:, m, :], ACT.Square).then_inc(squared.sem, 1)
                    wait(sq_used, l, which + 1)
                    fn(ln_t[:, 1, :], ps[:, 5, 0:T], ACT.Sqrt, bias=epsc[:], scale=1.0 / D).then_inc(root_ready.sem, 1)

                for m in range(KD):
                    if m == 5:
                        act.wait_ge(slot_done[3].sem, before + l * USES[3] + (2 + 1))
                    elif m == 7:
                        wait(tail_used, l, 1)
                    else:
                        wait(y1_ready, l, m + 1 - (m > 5))
                    gate_tile(m, GA1)
                squares_root(0)
                for i in range(KD // 2 + 1):
                    if i < KD // 2:
                        m = 2 * i
                        wait(normed, l, m + 1)
                        fn(xT[:, m, :], uT[:, m, :], ID, bias=vcol("ln1_b", m), scale=vcol("ln1_g", m)).then_inc(x_mid.sem, 1)
                    if i >= 1:
                        wait(x_mid, l, i)
                        modulate(m - 2 if i < KD // 2 else m, SH2, SC2, u2_act)

                wait(logits_T, l, 1)
                fn(lgT, ps[0:NG + NE, 6, 0:T], ID, bias=router_b[:]).then_inc(logits_copied.sem, 1)
                wait(gdiff, l, 1)
                fn(gtmp, gtmp, ACT.Exp).then_inc(gexp.sem, 1)
                wait(out_k, l, 2)
                for n in range(6):
                    t, h = n // 2, n % 2
                    wait(urow_turned, l, n + 1)
                    dst = urow[:, t, :].rearrange("q (k p) -> q p k", k=KD)[:, h * 64:(h + 1) * 64, :]
                    fn(dst, ps[:, n % 4, :].rearrange("q (p k) -> q p k", k=KD), ID).then_inc(urow_ready.sem, 1)
                wait(ediff, l, 1)
                fn(q, q, ACT.Exp).then_inc(eexp.sem, 1)
                for k in range(KD):
                    if 2 * k in PW_TURNS:
                        t = PW_TURNS.index(2 * k)
                        for h in range(2):
                            wait(Pw_turned, l, 2 * t + h + 1)
                            fn(PTw[:, 3 * h:3 * h + 3, t * P:(t + 1) * P],
                               ps[:, 4 + h, 0:3 * P].rearrange("p (s q) -> p s q", s=3), ID).then_inc(PT_ready.sem, 1)
                    wait(gath_ready, l, 2 * k + 1)
                    fn(XsT[:, k, 0:512], ps[:, (2 * k) % 4, 0:512], ID).then_inc(xs_act.sem, 1)

                wait(chunks_ready, l, 1)
                rounds = act.value_load(rounds_tab[0:1, ds(l, 1)], min_val=1, max_val=MAX_ROUNDS)
                with act.Fori(0, rounds) as r:
                    done = (before + r) * RING

                    def take(i):
                        off = act.value_load(chunk_tab[0:1, 1, ds(r * RING + i, 1)], min_val=0, max_val=PAIRS)
                        act.wait_ge(down_ready.sem, done + (i + 1))
                        act.wait_ge(down_act.sem, done + (i + 2))
                        fn(YsT[:, 0:4, ds(off, W)], ps[:, 2 + 2 * (i % 2), 0:4 * W].rearrange("p (m n) -> p m n", m=4),
                           ID).then_inc(down_act.sem, 1)

                    for i in range(RING):
                        act.wait_ge(gu_ready.sem, done + (i + 1))
                        fn(sg[:, i % 2], ps[:, i % 2, 0:2 * W].rearrange("p (f n) -> p f n", f=2), ACT.Silu).then_inc(silu_ready.sem, 1)
                        if i >= 1:
                            take(i - 1)
                    take(RING - 1)

                for s in range(ST):
                    wait(ys_turned, l, 2 * s + 1)
                    fn(Ysr[:, s, 0:512], ps[:, (2 * s) % 4, :], ID).then_inc(ys_act.sem, 1)
                for m in range(KD):
                    wait(y2_ready, l, m + 1)
                    gate_tile(m, GA2)
                squares_root(1)
                for m in range(KD):
                    wait(normed, l, KD + m + 1)
                    fn(xT[:, m, :], uT[:, m, :], ID, bias=vcol("ln2_b", m), scale=vcol("ln2_g", m)).then_inc(layer_x.sem, 1)

            for n in range(2 * NT):
                t, h = n // 2, n % 2
                act.wait_ge(out_turned.sem, n + 1)
                fn(xrow[:, t, 512 * h:512 * h + 512], ps[:, n, :], ID).then_inc(out_rows.sem, 1)

        @block.vector
        def _(dve):
            wait = engine_wait(dve)
            v = nc.vector
            before_z = v.memset(before_tab[:], 0)
            before_z.then_inc(s_ctl.sem, 1)
            v.memset(before_f[:], 0.0).then_inc(s_ctl.sem, 1)
            v.memset(sT[:, 2 * KD:], 0.0).then_inc(s_ctl.sem, 1)
            v.memset(epsc[:], EPS).then_inc(s_ctl.sem, 1)
            dve.wait_ge(s_ctl.sem, 4)

            with dve.Fori(0, DEPTH) as l:
                before = dve.value_load(before_tab[0:1, ds(l, 1)], min_val=0, max_val=DEPTH * MAX_ROUNDS)
                own = Steps(dve_self)

                def after(n, alone=False):
                    wait(dve_self, l, n, alone)

                wait(vec_loaded, l, len(VECS) + 2)
                pairs = lam_in[:].rearrange("o (a b) d -> o a b d", b=2)
                own.add(v.tensor_tensor(pairs[:, :, 0, :], pairs[:, :, 0, :], pairs[:, :, 1, :], ALU.mult))
                after(own.n)
                v.tensor_reduce(lam_s[:, 0:2], pairs[:, :, 0, :], AX, ALU.add).then_inc(lam_dot.sem, 1)
                wait(layer_x, l, KD)
                v.memset(arena[:, XS + NT * AW + AW + QK:XS + NT * AW + AW + QK + 2 * (POOL_COLS + GLU_COLS)],
                         0.0).then_inc(pads_zero.sem, 1)
                wait(vec_ready, l, 1)
                own.add(v.tensor_copy(vec[:], ps[:, 6, 0:NVEC]))
                after(own.n)
                own.add(v.tensor_scalar(subg[:], vcol("subln_g"), lam_c[:, 1:2], None, ALU.mult))
                wait(lam_exp, l, 1)
                own.add(v.tensor_tensor(lam_s[:, 2:3], lam_s[:, 1:2], lam_s[:, 0:1], ALU.subtract))
                after(own.n)
                v.tensor_tensor(lam_s[:, 3:4], lam_s[:, 2:3], lam_c[0:1, 0:1], ALU.subtract).then_inc(lam_ready.sem, 1)
                wait(dw_ready, l, 1)
                v.tensor_copy(dw[:], ps[:, 5, 0:64].rearrange("p (c k) -> p c k", c=2)[:, :, 0:TAPS]).then_inc(vec_copied.sem, 1)
                wait(lam_bc, l, 1)
                v.tensor_copy(nlam[:], ps[:, 4, 0:1]).then_inc(lam_done.sem, 1)

                def mod_add(j, bank):
                    wait(mod_turned, l, j + 1)
                    src = ps[:, bank, 0:HALF].rearrange("p (i g r) -> p g i r", i=GROUP_TILES, g=4)[:, :, :, 0:2]
                    b0 = VCOL["b_mod"] + STEP_TILES * j
                    v.tensor_tensor(modT[:, STEP_TILES * j:STEP_TILES * (j + 1), :].rearrange("p (g i) v -> p g i v", g=4), src,
                                    vec[:, b0:b0 + STEP_TILES].rearrange("p (g i) -> p g i", g=4).unsqueeze(3)
                                    .to_broadcast([P, 4, GROUP_TILES, 2]), ALU.add).then_inc(mod_added.sem, 1)

                def mod_scale(n, scale):
                    wait(mod_added, l, n)
                    v.tensor_scalar(modT[:, scale:scale + KD, :], modT[:, scale:scale + KD, :], 1.0, None,
                                    ALU.add).then_inc(mod_done.sem, 1)

                mod_add(0, 2)
                mod_add(1, 3)
                mod_scale(2, SC1)
                wait(mod_done, l, 1)
                for m in range(1, KD, 2):
                    for a, b, w_ in SEGS:
                        last = v.tensor_scalar(uT[:, m, a:b], xT[:, m, a:b], mod(SC1 + m, w_), mod(SH1 + m, w_),
                                               ALU.mult, ALU.add)
                    last.then_inc(u_dve.sem, 1)
                for c in range(2):
                    wait(proj_act, l, c + 1)
                    wait(proj_ready, l, 2 * c + 2)
                    bank = 1 + 2 * c
                    v.tensor_tensor(glu[:, c, CP:CP + SEQ], glu[:, c, CP:CP + SEQ], ps[:, bank, 0:SEQ], ALU.mult)
                    v.tensor_tensor(glu[:, c, GLU_LAT:GLU_LAT + LAT], glu[:, c, GLU_LAT:GLU_LAT + LAT], ps[:, bank, SEQ:T],
                                    ALU.mult).then_inc(proj_dve.sem, 1)
                wait(proj_dve, l, 2)

                conv_steps = [(tap, c) for tap in range(TAPS) for c in range(2)]
                conv_own = []

                def conv_step():
                    tap, c = conv_steps[len(conv_own)]
                    src, wt = glu[:, c, tap:tap + CONV_N], dw[:, c, tap:tap + 1]
                    if tap == 0:
                        conv_own.append(own.add(v.tensor_scalar(cacc[:, c, :], src, wt, None, ALU.mult)))
                    elif len(conv_own) < len(conv_steps) - 1:
                        after(conv_own[-2])
                        conv_own.append(own.add(v.scalar_tensor_tensor(cacc[:, c, :], src, wt, cacc[:, c, :], ALU.mult, ALU.add)))
                    else:
                        after(conv_own[-1])
                        conv_own.append(0)
                        v.scalar_tensor_tensor(cacc[:, c, :], src, wt, cacc[:, c, :], ALU.mult, ALU.add).then_inc(conv_done.sem, 1)

                for _ in range(14):
                    conv_step()
                wait(proj_act, l, 4)
                n = POOL_COLS
                own.add(v.tensor_tensor(sumX[:, :, 1:n], apad[:, :, 0:n - 1], apad[:, :, 1:n], ALU.add))
                after(own.n)
                own.add(v.tensor_tensor(sumY[:, :, 2:n - 1], sumX[:, :, 1:n - 2], sumX[:, :, 3:n], ALU.add))
                inv = C["inv"].rearrange("p (c n) -> p c n", c=2)
                mid = slice(PP, PP + POOL_N)
                lo, hi = slice(0, 64), slice(64, P)
                after(own.n)
                own.add(v.tensor_tensor(sumX[lo, 0, mid], sumX[lo, 0, mid], inv[lo, 0, :], ALU.mult))
                own.add(v.tensor_tensor(sumX[hi, 0, mid], sumY[hi, 0, mid], inv[hi, 0, :], ALU.mult))
                own.add(v.tensor_tensor(sumX[:, 1, 4:n - 3], sumY[:, 1, 2:n - 5], sumY[:, 1, 6:n - 1], ALU.add))
                after(own.n)
                own.add(v.tensor_tensor(sumY[:, 1, mid], sumX[:, 1, PP - 4:PP - 4 + POOL_N], sumX[:, 1, PP + 4:PP + 4 + POOL_N], ALU.add))
                after(own.n)
                own.add(v.tensor_tensor(sumX[lo, 1, mid], sumX[lo, 1, mid], inv[lo, 1, :], ALU.mult))
                own.add(v.tensor_tensor(sumX[hi, 1, mid], sumY[hi, 1, mid], inv[hi, 1, :], ALU.mult))
                after(own.n)
                v.tensor_tensor(sumX[:, :, mid], sumX[:, :, mid], apad[:, :, mid], ALU.subtract).then_inc(pool_done.sem, 1)
                for n in range(8):
                    x = (qT if n < HEADS else kT)[:, n % HEADS, SEQ:T]
                    b = 2 * (n % 2)
                    wait(proj_act, l, 4 + n + 1)
                    if n >= 2:
                        wait(roped, l, n - 1)
                    own.add(v.tensor_tensor(rope_t[:, b, :], x, C["cos"], ALU.mult))
                    wait(rot_ready, l, n + 1)
                    own.add(v.tensor_tensor(rope_t[:, b + 1, :], ps[:, 4 + n % 2, 0:LAT], C["sin"], ALU.mult))
                    after(own.n)
                    v.tensor_tensor(x, rope_t[:, b, :], rope_t[:, b + 1, :], ALU.add).then_inc(roped.sem, 1)
                    for _ in range(6):
                        conv_step()
                mod_add(2, 7)
                for t in range(NT):
                    src = ps[:, 6 + t // 2, (t % 2) * CONV:(t % 2 + 1) * CONV]
                    wait(crow_ready, l, max(t + 1, 2))
                    own.add(v.bn_stats(bstat[:, t, :], src))
                after(own.n, alone=True)
                for t in range(NT):
                    last = v.bn_aggr(cstat[:, t, 0:2], bstat[:, t, :])
                    if t < NT - 1:
                        own.add(last)
                last.then_inc(cln_var.sem, 1)

                def conv_norm():
                    wait(cln_sd, l, 1)
                    own.add(v.reciprocal(cstat[:, :, 3], cstat[:, :, 2]))
                    after(own.n)
                    for t in range(NT):
                        src = ps[:, 6 + t // 2, (t % 2) * CONV:(t % 2 + 1) * CONV]
                        last = v.tensor_scalar(crow[:, t, :], src, cstat[:, t, 0:1], cstat[:, t, 3:4], ALU.subtract, ALU.mult)
                        if t < NT - 1:
                            own.add(last)
                    last.then_inc(cln_done.sem, 1)

                NU = HEADS * NT
                for u in range(NU + 1):
                    if u < NU:
                        n = SEQ if u % NT == 0 else LAT + PAST
                        b = u % 2
                        wait(scores_ready, l, u + 1)
                        v.tensor_reduce(small[:, b, :, 1], ps[:, 2 * b:2 * b + 2, 0:n], AX, ALU.max,
                                        negate=True).then_inc(neg_max.sem, 1)
                    if u == 1:
                        conv_norm()
                    if u >= 1:
                        b = (u - 1) % 2
                        n = SEQ if (u - 1) % NT == 0 else LAT + PAST
                        wait(scores_used, l, u)
                        own.add(v.reciprocal(small[:, b, :, 3], small[:, b, :, 2]))
                        after(own.n)
                        own.add(v.tensor_tensor(small[:, b, 1, 0:1], small[:, b, 1, 3:4], nlam[:], ALU.mult))
                        own.add(v.tensor_scalar(probs[:, b, 0, 0:n], probs[:, b, 0, 0:n], small[:, b, 0, 3:4], None, ALU.mult))
                        after(own.n)
                        v.scalar_tensor_tensor(probs[:, b, 0, 0:n], probs[:, b, 1, 0:n], small[:, b, 1, 0:1],
                                               probs[:, b, 0, 0:n], ALU.mult, ALU.add).then_inc(prob_ready.sem, 1)

                mod_add(3, 7)
                mod_scale(MOD_STEPS, SC2)
                wait(o_copied, l, NU)
                o3 = orow.rearrange("p t h e -> p (t h) e")
                wait(rms_sd, l, 1)
                own.add(v.reciprocal(rms[:, 0, :], rms[:, 1, :]))
                after(own.n)
                v.tensor_tensor(o3, o3, rms[:, 0, :].unsqueeze(2).to_broadcast([P, NT * HEADS, VD]), ALU.mult).then_inc(o_normed.sem, 1)

                def modulate_dve(m, scale, shift, given, n, sig):
                    wait(given, l, n)
                    for a, b, w_ in SEGS:
                        last = v.tensor_scalar(uT[:, m, a:b], xT[:, m, a:b], mod(scale + m, w_), mod(shift + m, w_),
                                               ALU.mult, ALU.add)
                    last.then_inc(sig.sem, 1)

                def residual_norm(which):
                    o = which * KD
                    for m in range(KD):
                        wait(gated, l, o + m + 1)
                        v.scalar_tensor_tensor(uT[:, m, :], xT[:, m, :], ALPHA, uT[:, m, :], ALU.mult, ALU.add).then_inc(z_ready.sem, 1)
                    wait(mean_ready, l, which + 1)
                    wait(z_ready, l, o + KD)
                    for m in range(KD):
                        v.scalar_tensor_tensor(uT[:, m, :], ps[:, 4, 0:T], -1.0 / D, uT[:, m, :], ALU.mult, ALU.add).then_inc(centred.sem, 1)
                    wait(root_ready, l, which + 1)
                    own.add(v.reciprocal(ln_t[:, 0, :], ln_t[:, 1, :]))
                    after(own.n)
                    wait(centred, l, o + KD)
                    for m in range(KD):
                        v.tensor_tensor(uT[:, m, :], uT[:, m, :], ln_t[:, 0, :], ALU.mult).then_inc(normed.sem, 1)

                residual_norm(0)
                for m in range(1, KD, 2):
                    wait(normed, l, m + 1)
                    v.tensor_scalar(xT[:, m, :], uT[:, m, :], vcol("ln1_g", m), vcol("ln1_b", m), ALU.mult,
                                    ALU.add).then_inc(x_mid_dve.sem, 1)
                    if m >= 3:
                        modulate_dve(m - 2, SC2, SH2, x_mid_dve, m // 2, u2_dve)
                modulate_dve(KD - 1, SC2, SH2, x_mid_dve, KD // 2, u2_dve)

                def bc(x, n):
                    return x.unsqueeze(2).to_broadcast([P, NT, n])

                def bt(x, n):
                    return x.unsqueeze(1).to_broadcast([P, NT, n])

                def step(ins):
                    own.add(ins)
                    after(own.n)

                def first_max(vals, n, mx, cmx, onehot):
                    rank = bt(C["rank"][:, NE - n:NE], n)
                    step(v.tensor_reduce(mx, vals, AX, ALU.max))
                    step(v.tensor_tensor(onehot, vals, bc(mx, n), ALU.is_equal))
                    step(v.tensor_tensor(onehot, onehot, rank, ALU.mult))
                    step(v.tensor_reduce(cmx, onehot, AX, ALU.max))
                    step(v.tensor_tensor(onehot, onehot, bc(cmx, n), ALU.is_equal))

                wait(logits_ready, l, 1)
                step(v.tensor_copy(lg, ps[:, 5, 0:NT * (NG + NE)].rearrange("p (t n) -> p t n", t=NT)))
                first_max(lg[:, :, 0:NG], NG, gmax, gcm, og)
                v.tensor_tensor(gtmp, lg[:, :, 0:NG], bc(gmax, NG), ALU.subtract).then_inc(gdiff.sem, 1)
                step(v.tensor_scalar(og, og, BIG, -BIG, ALU.mult, ALU.add))
                e4 = lg[:, :, NG:].rearrange("p t (g e) -> p t g e", g=NG)
                step(v.tensor_tensor(e4, e4, og.unsqueeze(3).to_broadcast([P, NT, NG, EPG]), ALU.add))
                el = lg[:, :, NG:]
                first_max(el, NE, m1, c1, o1)
                step(v.scalar_tensor_tensor(etmp, o1, -3 * BIG, el, ALU.mult, ALU.add))
                first_max(etmp, NE, m2, c2, o2)
                v.tensor_tensor(asg, o1, o2, ALU.add).then_inc(assign_ready.sem, 1)
                v.tensor_tensor(q, m2, m1, ALU.subtract).then_inc(ediff.sem, 1)
                wait(ranks_ready, l, 1)
                step(v.tensor_copy(tot[:, 0:NE], ps[:, 7, NT * NE:(NT + 1) * NE]))
                ones32 = C["ones"][:, 0:NE]
                step(v.tensor_tensor_scan(start[:, 0:NE], ones32, tot[:, 0:NE], 0.0, ALU.mult, ALU.add))
                step(v.tensor_tensor(start[:, 0:NE], start[:, 0:NE], tot[:, 0:NE], ALU.subtract))
                step(v.tensor_tensor(etmp, ps[:, 7, 0:NE * NT].rearrange("p (t n) -> p t n", t=NT),
                                     bt(start[:, 0:NE], NE), ALU.add))
                own.add(v.tensor_tensor(o1, o1, etmp, ALU.mult))
                step(v.tensor_tensor(o2, o2, etmp, ALU.mult))
                own.add(v.tensor_reduce(s1, o1, AX, ALU.add))
                step(v.tensor_reduce(s2, o2, AX, ALU.add))
                wait(iota_loaded, l, 1)
                for t in range(NT):
                    step(v.tensor_scalar(Pm[:, t, :], iota, s1[:, t:t + 1], None, ALU.is_equal))
                    v.scalar_tensor_tensor(Pm[:, t, :], iota, s2[:, t:t + 1], Pm[:, t, :], ALU.is_equal,
                                           ALU.add).then_inc(P_ready.sem, 1)

                wait(gexp, l, 1)
                step(v.tensor_reduce(gsum, gtmp, AX, ALU.add))
                step(v.reciprocal(gw, gsum))
                wait(eexp, l, 1)
                step(v.tensor_scalar(rq, q, 1.0, None, ALU.add))
                step(v.reciprocal(cm, rq))
                step(v.tensor_tensor(w1, gw, cm, ALU.mult))
                step(v.tensor_tensor(w2, w1, q, ALU.mult))
                own.add(v.memset(le[:, NE:NE + 1], 0.0))
                step(v.tensor_scalar(ce[:, 0:NE], tot[:, 0:NE], 0.0, None, ALU.is_gt))
                for j in range(1, -(-T // W)):
                    step(v.scalar_tensor_tensor(ce[:, 0:NE], tot[:, 0:NE], float(W * j), ce[:, 0:NE], ALU.is_gt, ALU.add))
                step(v.tensor_tensor_scan(cb[:, 0:NE], ones32, ce[:, 0:NE], 0.0, ALU.mult, ALU.add))
                step(v.tensor_scalar(rnd[:, 0:MAX_ROUNDS], C["rounds"], cb[:, NE - 1:NE], None, ALU.is_lt))
                step(v.tensor_reduce(rnd[:, MAX_ROUNDS:], rnd[:, 0:MAX_ROUNDS], AX, ALU.add))
                step(v.tensor_copy(rounds_tab[:, ds(l, 1)], rnd[0:1, MAX_ROUNDS:]))
                step(v.tensor_tensor(before_f[:, ds(l + 1, 1)], before_f[:, ds(l, 1)], rnd[0:1, MAX_ROUNDS:], ALU.add))
                step(v.tensor_copy(before_tab[:, ds(l + 1, 1)], before_f[:, ds(l + 1, 1)]))
                step(v.tensor_tensor(cb[:, 0:NE], cb[:, 0:NE], ce[:, 0:NE], ALU.subtract))
                step(v.tensor_scalar(le[:, 0:NE], cb[:, 0:NE], C["kk"], None, ALU.is_le))
                step(v.tensor_reduce(chk[:, 2:3], le[:, 0:NE], AX, ALU.add))
                step(v.tensor_scalar(chk[:, 0:1], chk[:, 2:3], -1.0, None, ALU.add))
                step(v.tensor_tensor(dd[:, 0:NE], le[:, 0:NE], le[:, 1:NE + 1], ALU.subtract))
                step(v.scalar_tensor_tensor(ce[:, 0:NE], cb[:, 0:NE], float(-W), start[:, 0:NE], ALU.mult, ALU.add))
                step(v.tensor_tensor(ce[:, 0:NE], ce[:, 0:NE], dd[:, 0:NE], ALU.mult))
                step(v.tensor_reduce(chk[:, 2:3], ce[:, 0:NE], AX, ALU.add))
                step(v.tensor_scalar(chk[:, 3:4], C["kk"], float(W), chk[:, 2:3], ALU.mult, ALU.add))
                v.tensor_scalar(chk[:, 1:2], chk[:, 3:4], float(PAIRS), None, ALU.min).then_inc(chunk_cols.sem, 1)
                def weighted(t):
                    if t >= 2:
                        wait(Pw_turned, l, 2 * (t - 1))
                    if t >= 1:
                        wait(Pw_ready, l, t)
                    tmp = tail[:, 0:PAIRS]
                    own.add(v.tensor_scalar(tmp, iota, s1[:, t:t + 1], w1[:, t:t + 1], ALU.is_equal, ALU.mult))
                    step(v.tensor_scalar(Pw[:, t % 2, :], iota, s2[:, t:t + 1], w2[:, t:t + 1], ALU.is_equal, ALU.mult))
                    v.tensor_tensor(Pw[:, t % 2, :], Pw[:, t % 2, :], tmp, ALU.add).then_inc(Pw_ready.sem, 1)

                own.add(v.memset(XsT[:, :, PAIRS:PADDED], 0.0))
                for k in range(KD):
                    wait(gath_ready, l, 2 * k + 2)
                    if k == 0:
                        after(own.n)
                    v.tensor_copy(XsT[:, k, 512:PAIRS], ps[:, (2 * k + 1) % 4, 0:PAIRS - 512]).then_inc(xs_dve.sem, 1)
                    if k == 2:
                        wait(chunk_turned, l, 1)
                        v.tensor_copy(chunk_tab[:], ps[0:1, 6, 0:2 * P].rearrange("p (i n) -> p i n", i=2)
                                      [:, :, 0:MAX_ROUNDS * RING]).then_inc(chunks_ready.sem, 1)
                    if k in (1, 2, 4):
                        weighted((1, 2, 4).index(k))

                rounds = dve.value_load(rounds_tab[0:1, ds(l, 1)], min_val=1, max_val=MAX_ROUNDS)
                with dve.Fori(0, rounds) as r:
                    done = (before + r) * RING

                    def take(i):
                        off = dve.value_load(chunk_tab[0:1, 1, ds(r * RING + i, 1)], min_val=0, max_val=PAIRS)
                        dve.wait_ge(slot_done[i].sem, before + r + l * USES[i] + (USES[i] + 1 + 1))
                        dve.wait_ge(down_dve.sem, done + (i + 2))
                        v.tensor_copy(YsT[:, 4:8, ds(off, W)], ps[:, 3 + 2 * (i % 2), 0:4 * W].rearrange("p (m n) -> p m n", m=4)
                                      ).then_inc(down_dve.sem, 1)

                    for i in range(RING):
                        dve.wait_ge(silu_ready.sem, done + (i + 1))
                        v.tensor_tensor(hT[:, i % 2], sg[:, i % 2], ps[:, i % 2, 2 * W:4 * W].rearrange("p (f n) -> p f n", f=2),
                                        ALU.mult).then_inc(h_ready.sem, 1)
                        if i >= 1:
                            take(i - 1)
                    take(RING - 1)

                for s in range(ST):
                    wait(ys_turned, l, 2 * s + 2)
                    v.tensor_copy(Ysr[:, s, 512:1024], ps[:, (2 * s + 1) % 4, :]).then_inc(ys_dve.sem, 1)
                residual_norm(1)
                own.check()


_INPUTS = ["x_prompt", "x_sample", "cache_k", "cache_v", "c", "c_ctx", "w_mod", "b_mod", "w_in", "w_out", "pool_w",
           "pool_scale", "diff_lambda", "subln_g", "conv_dw", "conv_ln_g", "conv_ln_b", "conv_pw", "ln1_g", "ln1_b",
           "ln2_g", "ln2_b", "router_grp", "router_grp_b", "router_exp", "router_exp_b", "w_gate", "w_up", "w_down"]
_OUTPUTS = [(1, SEQ, D), (1, LAT, D), (1, DEPTH, SEQ, HEADS, 2, HD), (1, DEPTH, SEQ, HEADS, VD)]


def kernel(**inputs):
    import concourse.bacc as bacc
    from concourse.bass_utils import run_bass_kernel_spmd as run

    nc = bacc.Bacc("TRN2", target_bir_lowering=False, num_devices=1)
    arrays, aps = {}, {}

    def add(name, a):
        a = np.ascontiguousarray(a)
        arrays[f"in_{name}"] = a
        aps[name] = nc.dram_tensor(f"in_{name}", a.shape, mybir.dt.from_np(a.dtype), kind="ExternalInput").ap()

    for name in _INPUTS:
        add(name, inputs[name])
    table, iota, lam = shape_constants()
    add("consts", table)
    add("iota", iota)
    add("lam", lam)
    outs = [nc.dram_tensor(f"out_{i}", s, F32, kind="ExternalOutput").ap() for i, s in enumerate(_OUTPUTS)]
    build(nc, aps, aps["consts"], aps["iota"], aps["lam"], *outs)
    r = run(nc, [arrays], core_ids=[0])
    return tuple(r.results[0][f"out_{i}"] for i in range(len(_OUTPUTS)))
```

```python
from contextlib import ExitStack
import math

import numpy as np
import concourse.bass as bass
from concourse import mybir

F32 = mybir.dt.float32
I32 = mybir.dt.int32
ALU = mybir.AluOpType
ACT = mybir.ActivationFunctionType
AX = mybir.AxisListType.X
ds = bass.ds

P = 128
D = 1024
DEPTH = 2
SEQ = 128
LAT = 256
PAST = 128
T = SEQ + LAT
NT = T // P
KD = D // P
GRID_W = 64
POOL = D // 4
HEADS = 4
HD = 64
VD = 2 * HD
QK = HEADS * 2 * HD
AW = HEADS * VD
CONV = D - POOL - AW
TAPS = 31
AXIS = HD // 2
NG = 4
EPG = 8
NE = NG * EPG
FF = D // 4
ALPHA = (2 * DEPTH) ** 0.25
EPS = 1e-5
PAIRS = 2 * T
ST = PAIRS // P
W = 64
PADDED = PAIRS + W
RING = 4
SLOT_COLS = 768
HALF = SLOT_COLS // 2
SLOT = KD * SLOT_COLS
NMOD = 6 * KD
MOD_STEPS = 6 * D // (2 * SLOT_COLS)
STEP_TILES = 2 * SLOT_COLS // P
GROUP_TILES = STEP_TILES // 4
USES = (4, 3, 3, 2)
MAX_CHUNKS = NE + (PAIRS - NE) // W
MAX_ROUNDS = -(-MAX_CHUNKS // RING)
LISTED = MAX_ROUNDS * RING + 2
BIG = 1e30

PP = 8
POOL_COLS = 2 * PP + SEQ + 2 * PP + LAT
POOL_LAT = 3 * PP + SEQ
POOL_N = POOL_COLS - 2 * PP
CP = TAPS // 2
GLU_COLS = 4 * CP + T
GLU_LAT = 3 * CP + SEQ
CONV_N = GLU_COLS - 2 * CP
CONV_LAT = 2 * CP + SEQ

VECS = [("b_mod", NMOD), ("pool_scale", POOL // P), ("subln_g", 1), ("conv_ln_g", CONV // P),
        ("conv_ln_b", CONV // P), ("ln1_g", KD), ("ln1_b", KD), ("ln2_g", KD), ("ln2_b", KD)]
VCOL, NVEC = {}, 0
for _name, _n in VECS:
    VCOL[_name] = NVEC
    NVEC += _n

CONST_COLS = [("ident", P), ("ones", P), ("rot", P), ("cos", LAT), ("sin", LAT),
              ("rank", NE), ("kk", 1), ("rounds", MAX_ROUNDS), ("inv", 2 * POOL_N)]


def shape_constants():
    c = {}
    c["ident"] = np.eye(P)
    c["tri"] = np.triu(np.ones((P, P)), 1)
    c["ones"] = np.ones((P, P))
    rot = np.zeros((P, P))
    half = AXIS // 2
    for j in range(P):
        if (j // half) % 2 == 0:
            rot[j + half, j] = -1.0
        else:
            rot[j - half, j] = 1.0
    c["rot"] = rot
    pos = np.arange(LAT)
    coord = np.stack([pos // GRID_W, pos % GRID_W]).astype(np.float32)
    inv = (np.float32(10000.0) ** (-np.arange(0, AXIS, 2, dtype=np.float32) / np.float32(AXIS))).astype(np.float32)
    p = np.arange(P)
    ang = coord[(p // AXIS) % 2, :] * inv[p % half][:, None]
    c["cos"] = np.cos(ang)
    c["sin"] = np.sin(ang)
    c["rank"] = np.tile(np.arange(NE, 0, -1), (P, 1))
    c["kk"] = np.arange(P)[:, None]
    c["rounds"] = np.tile(np.arange(MAX_ROUNDS) * RING, (P, 1))
    cnt = np.zeros((P, 2, POOL_N))
    for base, length in ((0, SEQ), (POOL_LAT - PP, LAT)):
        t = np.arange(length)
        for g, w in enumerate((2, 4, 8, 16)):
            n = np.clip(t + w // 2, 0, length) - np.clip(t - w // 2, 0, length)
            cnt[64 * (g % 2):64 * (g % 2) + 64, g // 2, base:base + length] = (1.0 / n)
    c["inv"] = cnt.reshape(P, 2 * POOL_N)
    table = np.concatenate([c[n].reshape(P, k) for n, k in CONST_COLS], axis=1).astype(np.float32)
    iota = np.concatenate([np.tile(np.arange(PAIRS), (P, 1)), c["tri"]], axis=1).astype(np.float32)
    lam = np.array([0.8 - 0.6 * math.exp(-0.3 * l) for l in range(DEPTH)])
    lam = np.stack([lam, 1.0 - lam], axis=-1)[:, None, :].repeat(P, axis=1).astype(np.float32)
    return table, iota, lam


class Signal:

    def __init__(self, sem, per_layer, step=1, credit=0):
        self.sem, self.per_layer, self.step, self.credit = sem, per_layer, step, credit

    def at(self, l, n):
        return (l * self.per_layer + n) * self.step + self.credit


class Steps:

    def __init__(self, signal):
        self.raised, self.n = signal, 0

    def add(self, ins):
        self.n += 1
        ins.then_inc(self.raised.sem, 1)
        return self.n

    def check(self):
        assert self.n == self.raised.per_layer, (self.raised.sem, self.n, self.raised.per_layer)


DVE_STEPS = 208


def build(nc, g, consts, iota_dram, lam_dram, y_prompt, y_sample, new_k, new_v):
    with ExitStack() as ctx:
        def sb(name, shape, dt=F32):
            return ctx.enter_context(nc.sbuf_tensor(name, shape, dt))

        def signal(name, per_layer, step=1, credit=0):
            return Signal(ctx.enter_context(nc.semaphore(name)), per_layer, step, credit)

        ring = sb("ring", [P, RING, SLOT])
        tail = sb("tail", [P, KD * 256])
        xT = sb("xT", [P, KD, T])
        uT = sb("uT", [P, KD, T])
        XS = max(KD * PADDED, NT * (D + PAIRS) + 2 * PAIRS)
        arena = sb("arena", [P, 2 * XS])
        PTw = sb("PTw", [P, ST, T])
        cst = sb("cst", [P, sum(n for _, n in CONST_COLS)])
        pool_blk = sb("pool_blk", [P, 2, P])
        conv_pw = sb("conv_pw", [P, 2, CONV])
        krow = sb("krow", [P, QK])
        vec_rows = sb("vec_rows", [NVEC, P])
        vec = sb("vec", [P, NVEC])
        dw = sb("dw", [P, 2, TAPS])
        router_w = sb("router_w", [P, KD, NG + NE])
        router_b = sb("router_b", [NG + NE, 1])
        modT = sb("modT", [P, NMOD, 2])
        sT = sb("sT", [P, 2 * KD + 30])
        lam_in = sb("lam_in", [1, 4, HD])
        lam_c = sb("lam_c", [P, 2])
        lam_s = sb("lam_s", [1, 4])
        nlam = sb("nlam", [P, 1])
        subg = sb("subg", [P, 1])
        epsc = sb("epsc", [P, 1])
        chunk_tab = sb("chunk_tab", [1, 2, LISTED], I32)
        rounds_tab = sb("rounds_tab", [1, 2, DEPTH], I32)
        before_f = sb("before_f", [1, 2, DEPTH + 1])
        before_tab = sb("before_tab", [1, 2, DEPTH + 1], I32)

        C, at = {}, 0
        for name, n in CONST_COLS:
            C[name] = cst[:, at:at + n]
            at += n
        ident = C["ident"]

        def place(base, *sizes):
            out, at = [], base
            for n in sizes:
                out.append(arena[:, at:at + n])
                at += n
            return out, at

        (mixT, qT, kT, ckT), end = place(0, KD * T, HEADS * T, HEADS * T, HEADS * PAST)
        assert end <= XS
        (vrow, cv, ck_rows, apad, glu, cacc, probs, dw_rows), end = place(
            XS, NT * AW, AW, QK, 2 * POOL_COLS, 2 * GLU_COLS, 2 * CONV_N, 4 * T, CONV)
        assert end <= 2 * XS
        mixT = mixT.rearrange("p (m t) -> p m t", m=KD)
        qT = qT.rearrange("p (h t) -> p h t", h=HEADS)
        kT = kT.rearrange("p (h t) -> p h t", h=HEADS)
        ckT = ckT.rearrange("p (h t) -> p h t", h=HEADS)
        vrow = vrow.rearrange("p (t n) -> p t n", t=NT)
        apad = apad.rearrange("p (c n) -> p c n", c=2)
        glu = glu.rearrange("p (c n) -> p c n", c=2)
        cacc = cacc.rearrange("p (c n) -> p c n", c=2)
        csil = arena[:, XS + NT * AW + AW + QK + 2 * POOL_COLS:][:, 0:2 * T].rearrange("p (c n) -> p c n", c=2)
        sq_out = cacc.rearrange("p c n -> p (c n)")[:, 0:6 * VD].rearrange("p (b n) -> p b n", b=6)
        probs = probs.rearrange("p (b m n) -> p b m n", b=2, m=2)
        rope_t = probs.rearrange("p b m n -> p (b m n)")[:, 0:4 * LAT].rearrange("p (b n) -> p b n", b=4)
        uflat = uT[:].rearrange("p m t -> p (m t)")
        aT = uflat[:, 0:2 * T].rearrange("p (b k q) -> p b k q", b=2, k=NT)
        orow = uflat[:, 2 * T:2 * T + NT * AW].rearrange("p (t h e) -> p t h e", t=NT, h=HEADS)
        crow = uflat[:, 2 * T + NT * AW:2 * T + NT * AW + NT * CONV].rearrange("p (t n) -> p t n", t=NT)
        ptflat = PTw[:].rearrange("p s t -> p (s t)")
        sumX = ptflat[:, 0:2 * POOL_COLS].rearrange("p (c n) -> p c n", c=2)
        sumY = ptflat[:, 2 * POOL_COLS:4 * POOL_COLS].rearrange("p (c n) -> p c n", c=2)
        mrow = arena[:, 0:2 * HALF].rearrange("p (b n) -> p b n", b=2)
        XsT = arena[:, 0:KD * PADDED].rearrange("p (k n) -> p k n", k=KD)
        YsT = arena[:, XS:XS + KD * PADDED].rearrange("p (k n) -> p k n", k=KD)
        Ysr = arena[:, 0:ST * D].rearrange("p (s n) -> p s n", s=ST)
        urow = arena[:, XS:XS + NT * D].rearrange("p (t n) -> p t n", t=NT)
        Pm = arena[:, XS + NT * D:XS + NT * D + NT * PAIRS].rearrange("p (t n) -> p t n", t=NT)
        Pw = arena[:, XS + NT * (D + PAIRS):XS + NT * (D + PAIRS) + 2 * PAIRS].rearrange("p (t n) -> p t n", t=2)
        assert XS + NT * (D + PAIRS) + 2 * PAIRS <= 2 * XS
        xc = tail[:, 0:2 * KD * W].rearrange("p (b k n) -> p b k n", b=2, k=KD)
        yrow = tail[:, 2 * KD * W:2 * KD * W + D].rearrange("p (b n) -> p b n", b=2)
        sg = arena[:, KD * PADDED:KD * PADDED + FF].rearrange("p (b n) -> p b n", b=2)
        hrow = arena[:, XS + KD * PADDED:XS + KD * PADDED + FF].rearrange("p (b n) -> p b n", b=2)
        assert KD * PADDED + FF <= XS and 2 * W == P and FF == 2 * P
        hT = krow[:, 0:FF].rearrange("p (b n) -> p b n", b=2)
        iota_tri = tail[:, PAIRS:2 * PAIRS + P]
        iota, tri = iota_tri[:, 0:PAIRS], iota_tri[:, PAIRS:]
        ln_t = arena[:, XS + NT * AW:XS + NT * AW + (2 + KD) * T].rearrange("p (b n) -> p b n", b=2 + KD)
        xrow = arena[:, 0:NT * D].rearrange("p (t n) -> p t n", t=NT)
        RT_COLS = NT * (NG + NE) + NT * NG + 4 * NT * NE
        at = [0]

        def rts(*shape):
            n = int(np.prod(shape))
            v = arena[:, at[0]:at[0] + n]
            at[0] += n
            return v if len(shape) == 1 else v.rearrange("p (a b) -> p a b", a=shape[0])
        lg = rts(NT, NG + NE)
        og = rts(NT, NG)
        o1, o2 = rts(NT, NE), rts(NT, NE)
        etmp, asg = rts(NT, NE), rts(NT, NE)
        r3 = sb("r3", [P, 15, NT])
        gmax, gsum, gw, m1, m2, cm, q, s1, s2, w1, w2, rq, gcm, c1, c2 = [r3[:, i, :] for i in range(15)]
        assert at[0] == RT_COLS
        asg_flat = asg.rearrange("p t n -> p (t n)")
        lgT = arena[0:NG + NE, RT_COLS:RT_COLS + T]
        tot, start, cb, le, dd, ce = [tail[:, 2 * PAIRS + P + (NE + 1) * i:2 * PAIRS + P + (NE + 1) * (i + 1)] for i in range(6)]
        gtmp = tail[:, 2 * PAIRS + P + 6 * (NE + 1):][:, 0:NT * NG].rearrange("p (a b) -> p a b", a=NT)
        chk = sb("chk", [P, 4])
        small = sb("small", [P, 2, 2, 4])
        rnd = sb("rnd", [P, MAX_ROUNDS + 3])
        bstat = sb("bstat", [P, NT, 6])
        cstat = sb("cstat", [P, NT, 4])
        rms = sb("rms", [P, 2, NT * HEADS])

        ps = ctx.enter_context(nc.psum_tensor("ps", [P, 8, 512], F32))

        s_cst = signal("const_loaded", 0, 16)
        s_xin = signal("x_rows_loaded", 0, 16)
        s_cin = signal("cond_loaded", 0, 16)
        s_xt = signal("x_turned", 0)
        s_ctl = signal("tables_zeroed", 0)
        s_crow = signal("cond_rows_silu", 0)
        s_cT = signal("cond_transposed", 0)
        s_sT = signal("cond_ready", 0)
        s_zero = signal("zeros_written", 0)
        vec_loaded = signal("vec_loaded", len(VECS) + 2, 16)
        vec_ready = signal("vec_transposed", 1, credit=1)
        dw_ready = signal("taps_transposed", 1)
        vec_copied = signal("vec_copied", 1)
        lam_dot = signal("lambda_dots", 1)
        lam_exp = signal("lambda_exps", 1)
        lam_ready = signal("lambda_ready", 1, credit=1)
        lam_done = signal("lambda_copied", 1)
        mix_loaded = signal("mixer_params_loaded", 7, 16)
        taps_loaded = signal("taps_loaded", 1, 16)
        rt_loaded = signal("router_loaded", 4, 16)
        iota_loaded = signal("iota_loaded", 1, 16)
        layer_x = signal("x_ready", KD)
        slot_done = [signal(f"slot_done{s}", USES[s], credit=1) for s in range(RING)]
        slot_loaded = [signal(f"slot_loaded{s}", USES[s], 32) for s in range(RING)]
        glu_cols_loaded = signal("glu_columns_loaded", 1, 16)
        exp_loaded = [signal(f"expert_loaded{s}", 0, 16) for s in range(RING)]
        tail_loaded = signal("tail_loaded", 1, 16)
        tail_used = signal("tail_used", 1)
        mod_rows = signal("mod_rows", 2 * MOD_STEPS)
        mod_rows_copied = signal("mod_rows_copied", MOD_STEPS)
        mod_turned = signal("mod_turned", MOD_STEPS)
        mod_added = signal("mod_bias_added", MOD_STEPS)
        mod_done = signal("mod_done", 2)
        u_act = signal("u_tiles_act", KD // 2)
        u_dve = signal("u_tiles_dve", KD // 2)
        proj_ready = signal("proj_ready", 14)
        proj_act = signal("proj_taken_act", 15)
        proj_dve = signal("proj_taken_dve", 2)
        rot_ready = signal("rot_ready", 8)
        roped = signal("roped", 8)
        ck_turned = signal("ck_turned", 2)
        ck_copied = signal("ck_copied", 2)
        lam_bc = signal("lambda_broadcast", 1)
        scores_ready = signal("scores_ready", 12)
        scores_used = signal("scores_used", 12)
        neg_max = signal("neg_max", 12)
        prob_ready = signal("prob_ready", 12)
        prob_turned = signal("prob_turned", 12)
        prob_copied = signal("prob_copied", 12)
        o_ready = signal("o_ready", 12)
        o_copied = signal("o_copied", 12)
        pads_zero = signal("pads_zero", 1)
        logits_T = signal("logits_columns", 1)
        logits_copied = signal("logits_columns_copied", 1)
        conv_done = signal("conv_done", 1)
        pool_done = signal("pool_sums_done", 1)
        pool_ready = signal("pool_mixed", 2)
        o_squared = signal("o_rows_squared", 12)
        rms_sd = signal("rms_root", 1)
        o_normed = signal("o_normed", HEADS)
        o_turned = signal("o_turned", HEADS)
        crow_ready = signal("conv_rows_turned", NT)
        cln_var = signal("conv_var", 1)
        cln_sd = signal("conv_root", 1)
        cln_done = signal("conv_rows_normed", 1)
        cback = signal("conv_turned_back", 2)
        csil_ready = signal("conv_silu", 2)
        cpw_ready = signal("conv_pointwise", 2)
        mix_ready = signal("mix_tiles", KD)
        y1_ready = signal("y1_ready", KD - 2)
        y2_ready = signal("y2_ready", KD)
        x_scaled = signal("x_scaled", 2 * KD)
        z_ready = signal("z_ready", 2 * KD)
        mean_ready = signal("mean_ready", 2)
        centred = signal("centred", 2 * KD)
        squared = signal("squared", 2 * KD)
        sq_used = signal("squares_summed", 2)
        root_ready = signal("root_ready", 2)
        normed = signal("normed", 2 * KD)
        x_mid = signal("x_mid", KD // 2)
        x_mid_dve = signal("x_mid_dve", KD // 2)
        u2_act = signal("u2_act", KD // 2)
        u2_dve = signal("u2_dve", KD // 2)
        logits_ready = signal("logits_ready", 1)
        urow_turned = signal("urow_turned", 6)
        urow_ready = signal("urow_ready", 6)
        gdiff = signal("group_diff", 1)
        gexp = signal("group_exp", 1)
        ediff = signal("expert_diff", 1)
        eexp = signal("expert_exp", 1)
        assign_ready = signal("assignment", 1)
        ranks_ready = signal("ranks", 1)
        chunk_cols = signal("chunk_columns", 1)
        chunk_turned = signal("chunk_turned", 1)
        chunks_ready = signal("chunk_list", 1)
        P_ready = signal("gather_matrix", 2 * NT)
        Pw_ready = signal("weighted_matrix", NT)
        Pw_turned = signal("weighted_turned", 2 * NT)
        PT_ready = signal("unsort_matrix", 2 * NT)
        gath_ready = signal("gathered", 2 * KD)
        xs_act = signal("sorted_x_act", KD)
        xs_dve = signal("sorted_x_dve", KD)
        xc_ready = signal("chunk_x_copied", 0)
        gu_ready = signal("gate_up_ready", 0, credit=4)
        silu_ready = signal("silu_ready", 0)
        h_ready = signal("h_rows_ready", 0, credit=2)
        h_turned = signal("h_turned", 0, credit=2)
        hT_ready = signal("h_columns_ready", 0, credit=2)
        down_ready = signal("down_half_ready", 0)
        y_rows = signal("y_rows_copied", 0, credit=2)
        y_turned = signal("y_turned", 0, credit=2)
        y_placed = signal("y_placed", 0, credit=2)
        ys_turned = signal("ys_turned", 12, credit=1)
        ys_act = signal("ys_rows_act", 6)
        ys_dve = signal("ys_rows_dve", 6)
        out_k = signal("new_kv_stored", 2, 16)
        kv_free = signal("kv_rows_free", 1, credit=1)
        out_turned = signal("out_turned", 0)
        out_rows = signal("out_rows", 0)
        s_out = signal("y_stored", 0, 16)
        dve_self = signal("dve_step", DVE_STEPS)

        def engine_wait(eng):
            def wait(sig, l, n, alone=False):
                eng.wait_ge(sig.sem, sig.at(l, n))
                if alone:
                    eng.nop(nofuse=True)
            return wait

        def rounds_before(eng, l):
            full = eng.value_load(before_tab[0:1, 0, ds(l, 1)], min_val=0, max_val=DEPTH * MAX_ROUNDS)
            halves = eng.value_load(before_tab[0:1, 1, ds(l, 1)], min_val=0, max_val=2 * DEPTH)
            return full, halves, lambda s: full + halves if s < 2 else full

        def rounds_now(eng, l):
            return (eng.value_load(rounds_tab[0:1, 0, ds(l, 1)], min_val=1, max_val=MAX_ROUNDS - 1),
                    eng.value_load(rounds_tab[0:1, 1, ds(l, 1)], min_val=1, max_val=2))

        w_mod, w_in, w_out = g["w_mod"], g["w_in"], g["w_out"]
        q0, k0, v0, c0 = POOL, POOL + QK, POOL + 2 * QK, POOL + 2 * QK + AW
        slot = [ring[:, s, :].rearrange("p (k n) -> p k n", k=KD) for s in range(RING)]
        gate_w = [ring[:, s, 0:KD * FF].rearrange("p (k f) -> p k f", k=KD) for s in range(RING)]
        up_w = [ring[:, s, KD * FF:2 * KD * FF].rearrange("p (k f) -> p k f", k=KD) for s in range(RING)]
        gate_up_w = [ring[:, s, 0:2 * KD * FF].rearrange("p (j k f) -> p j k f", j=2, k=KD) for s in range(RING)]
        down_w = [ring[:, s, 2 * KD * FF:3 * KD * FF].rearrange("p (k n) -> p k n", k=2) for s in range(RING)]
        tail_w = tail[:].rearrange("p (k n) -> p k n", k=KD)
        GATHERED = ((0, 512), (512, PAIRS))
        PW_TURNS = (8, 10, 14)
        MOD_SLOTS = ((0, 1), (2, 3), (0, 1), (0, 2))
        MOD_USE = ((0, 0), (0, 0), (2, 2), (3, 2))
        SEGS = ((0, SEQ, 1), (SEQ, T, 0))
        SH1, SC1, GA1, SH2, SC2, GA2 = [i * KD for i in range(6)]

        def mod(i, v):
            return modT[:, i, v:v + 1]

        def vcol(name, i=0):
            return vec[:, VCOL[name] + i:VCOL[name] + i + 1]

        block = ctx.enter_context(nc.Block())

        @block.sync
        def _(sp):
            wait = engine_wait(sp)
            sp.dma_start(cst[:], consts).then_inc(s_cst.sem, 16)
            sp.dma_start(xrow[:, 0, :], g["x_prompt"][0]).then_inc(s_xin.sem, 16)
            sp.dma_start(xrow[:, 1:NT, :], g["x_sample"][0].rearrange("(t p) d -> p t d", p=P)).then_inc(s_xin.sem, 16)

            sp.wait_ge(s_ctl.sem, 4)
            with sp.Fori(0, DEPTH) as l:
                before, halves_before, slot_before = rounds_before(sp, l)

                def load_slot(s, use, parts, first=None):
                    sp.wait_ge(slot_done[s].sem, slot_before(s) + l * USES[s] + (use + 1))
                    sp.nop(nofuse=True)
                    for i, (dst, src) in enumerate(parts):
                        sp.dma_start(dst, src).then_inc((first if first and i == 0 else slot_loaded[s]).sem, 16)

                def cols(w, a, b, k0_, k1_):
                    return w[ds(l, 1), k0_ * P:k1_ * P, a:b].rearrange("o (k p) n -> p (o k) n", p=P)

                h2 = KD // 2
                def load_mod(j):
                    for i in range(2):
                        s = MOD_SLOTS[j][i]
                        a = (2 * j + i) * SLOT_COLS
                        load_slot(s, MOD_USE[j][i], [(slot[s][:, 0:h2, :], cols(w_mod, a, a + SLOT_COLS, 0, h2)),
                                           (slot[s][:, h2:KD, :], cols(w_mod, a, a + SLOT_COLS, h2, KD))])

                load_mod(0)
                load_mod(1)
                load_slot(0, 1, [(slot[0][:, :, POOL:SLOT_COLS], cols(w_in, c0, c0 + 2 * CONV, 0, KD)),
                                 (slot[0][:, 0:h2, 0:POOL], cols(w_in, 0, POOL, 0, h2)),
                                 (slot[0][:, h2:KD, 0:POOL], cols(w_in, 0, POOL, h2, KD))], first=glu_cols_loaded)
                for s in (1, 2):
                    a = q0 + (s - 1) * SLOT_COLS
                    load_slot(s, 1, [(slot[s][:, 0:h2, :], cols(w_in, a, a + SLOT_COLS, 0, h2)),
                                     (slot[s][:, h2:KD, :], cols(w_in, a, a + SLOT_COLS, h2, KD))])
                load_slot(3, 1, [(slot[3][:, 0:h2, :], cols(w_out, 0, SLOT_COLS, 0, h2)),
                                 (slot[3][:, h2:KD, :], cols(w_out, 0, SLOT_COLS, h2, KD))])
                wait(ys_turned, l, 0, alone=True)
                sp.dma_start(tail_w, cols(w_out, SLOT_COLS, D, 0, KD)).then_inc(tail_loaded.sem, 16)
                load_mod(2)
                load_mod(3)

                wait(chunks_ready, l, 1, alone=True)
                rounds, halves = rounds_now(sp, l)

                def load_experts(n, first, used):
                    for i in range(n):
                        e = sp.value_load(chunk_tab[0:1, 0, ds(first + i, 1)], min_val=0, max_val=NE - 1)
                        sp.wait_ge(slot_done[i].sem, used(i) + l * USES[i] + (USES[i] + 1))
                        sp.nop(nofuse=True)
                        sp.dma_start(gate_w[i], g["w_gate"][ds(l, 1), ds(e, 1)].rearrange(
                            "o a (p k) f -> p (o a k) f", k=KD)).then_inc(exp_loaded[i].sem, 16)
                        sp.dma_start(up_w[i], g["w_up"][ds(l, 1), ds(e, 1)].rearrange(
                            "o a (p k) f -> p (o a k) f", k=KD)).then_inc(exp_loaded[i].sem, 16)
                        sp.dma_start(down_w[i], g["w_down"][ds(l, 1), ds(e, 1)].rearrange(
                            "o a (k p) n -> p (o a k) n", p=P)).then_inc(exp_loaded[i].sem, 16)

                with sp.Fori(0, rounds) as r:
                    load_experts(RING, r * RING, lambda i: slot_before(i) + r)
                with sp.Fori(0, halves) as r:
                    load_experts(2, rounds * RING + r * 2, lambda i: slot_before(i) + rounds + r)

        @block.gpsimd
        def _(pool):
            wait = engine_wait(pool)
            nc.gpsimd.memset(pool_blk[:], 0.0).then_inc(s_zero.sem, 1)
            for sig in slot_done + [vec_ready, lam_ready, ys_turned, gu_ready, h_ready, h_turned, hT_ready, y_rows,
                                    y_turned, y_placed, kv_free]:
                pool.sem_inc(sig.sem, sig.credit)
            pool.dma_start(krow[0:8, 0:P], g["c"][0].rearrange("(k p) -> k p", p=P)).then_inc(s_cin.sem, 16)
            pool.dma_start(krow[0:8, P:2 * P], g["c_ctx"].rearrange("(k p) -> k p", p=P)).then_inc(s_cin.sem, 16)
            pool.wait_ge(s_zero.sem, 1)
            with pool.Fori(0, DEPTH) as l:
                def row(name, n):
                    return g[name][ds(l, 1)].rearrange("o (k p) -> (o k) p", p=P)

                wait(vec_ready, l, 0, alone=True)
                for name, n in VECS:
                    pool.dma_start(vec_rows[VCOL[name]:VCOL[name] + n, :], row(name, n)).then_inc(vec_loaded.sem, 16)
                wait(lam_ready, l, 0, alone=True)
                pool.dma_start(lam_in[:], g["diff_lambda"][ds(l, 1)]).then_inc(vec_loaded.sem, 16)
                pool.dma_start(lam_c[:], lam_dram[ds(l, 1)].rearrange("o p c -> (o p) c")).then_inc(vec_loaded.sem, 16)
                wait(layer_x, l, KD, alone=True)
                pool.dma_start(dw_rows[0:TAPS, :], g["conv_dw"][ds(l, 1)].rearrange("o k n -> (o k) n")).then_inc(taps_loaded.sem, 16)
                pool.dma_start(ck_rows, g["cache_k"][0, ds(l, 1)].rearrange("o t h m d -> (o t) (h m d)")).then_inc(mix_loaded.sem, 16)
                pool.dma_start(cv, g["cache_v"][0, ds(l, 1)].rearrange("o t h e -> (o t) (h e)")).then_inc(mix_loaded.sem, 16)
                pool.dma_start(conv_pw[:], g["conv_pw"][ds(l, 1)].rearrange("o (k p) n -> p (o k) n", p=P)).then_inc(mix_loaded.sem, 16)
                for b in range(4):
                    q = 64 * (b % 2)
                    pool.dma_start(pool_blk[q:q + 64, b // 2, q:q + 64], g["pool_w"][ds(l, 1), b].rearrange(
                        "o c d -> (o c) d")).then_inc(mix_loaded.sem, 16)
                pool.dma_start(router_w[:, :, 0:NG], g["router_grp"][ds(l, 1)].rearrange(
                    "o (k p) n -> p (o k) n", p=P)).then_inc(rt_loaded.sem, 16)
                pool.dma_start(router_w[:, :, NG:], g["router_exp"][ds(l, 1)].rearrange(
                    "o (k p) n -> p (o k) n", p=P)).then_inc(rt_loaded.sem, 16)
                pool.dma_start(router_b[0:NG, :], g["router_grp_b"][ds(l, 1)].rearrange("o n -> n o")).then_inc(rt_loaded.sem, 16)
                pool.dma_start(router_b[NG:, :], g["router_exp_b"][ds(l, 1)].rearrange("o n -> n o")).then_inc(rt_loaded.sem, 16)
                wait(ck_copied, l, 2, alone=True)
                pool.dma_start(new_k[0, ds(l, 1)].rearrange("o t h m d -> (o t) (h m d)"), krow[:]).then_inc(out_k.sem, 16)
                wait(proj_act, l, 13, alone=True)
                pool.dma_start(new_v[0, ds(l, 1)].rearrange("o t h e -> (o t) (h e)"), vrow[:, 0, :]).then_inc(out_k.sem, 16)
                wait(tail_used, l, 1, alone=True)
                pool.dma_start(iota_tri, iota_dram).then_inc(iota_loaded.sem, 16)
                wait(out_k, l, 2, alone=True)
                pool.sem_inc(kv_free.sem, 1)
            for t in range(NT):
                pool.wait_ge(out_rows.sem, 2 * t + 2)
                dst = y_prompt[0] if t == 0 else y_sample[0, (t - 1) * P:t * P, :]
                pool.dma_start(dst, xrow[:, t, :]).then_inc(s_out.sem, 16)
            pool.wait_ge(s_out.sem, 16 * NT)

        @block.tensor
        def _(pe):
            wait = engine_wait(pe)
            mm, tr = nc.tensor.matmul, nc.tensor.transpose

            pe.wait_ge(s_cst.sem, 16)
            pe.wait_ge(s_xin.sem, 32)
            for m in range(KD):
                for t in range(NT):
                    last = tr(ps[:, m, t * P:(t + 1) * P], xrow[:, t, m * P:(m + 1) * P], ident)
                last.then_inc(s_xt.sem, 1)
            pe.wait_ge(s_crow.sem, 1)
            pe.wait_ge(layer_x.sem, 1)
            for v in range(2):
                last = tr(ps[:, 0, 8 * v:8 * v + 8], krow[0:8, 256 + v * P:256 + (v + 1) * P], ident[0:8, 0:8])
            last.then_inc(s_cT.sem, 1)
            pe.wait_ge(s_sT.sem, 1)
            pe.wait_ge(layer_x.sem, KD)
            pe.wait_ge(s_ctl.sem, 4)

            with pe.Fori(0, DEPTH) as l:
                before, halves_before, slot_before = rounds_before(pe, l)

                def vectors():
                    wait(vec_loaded, l, len(VECS) + 2)
                    tr(ps[:, 6, 0:NVEC], vec_rows[:], ident[0:NVEC, 0:NVEC]).then_inc(vec_ready.sem, 1)

                def mod_product(j, bank, ks):
                    sa, sb_ = MOD_SLOTS[j]
                    if ks[0] == 0:
                        for s, use in zip(MOD_SLOTS[j], MOD_USE[j]):
                            pe.wait_ge(slot_loaded[s].sem, l * (32 * USES[s]) + 32 * (use + 1))
                    for k in ks:
                        both = sT[:, 2 * k:2 * k + 32]
                        for g_ in range(4):
                            s = (sa, sb_)[g_ // 2]
                            last = mm(ps[32 * g_:32 * (g_ + 1), bank, 0:HALF], both,
                                      slot[s][:, k, (g_ % 2) * HALF:(g_ % 2 + 1) * HALF],
                                      start=(k == 0), stop=(k == KD - 1), tile_position=(0, 32 * g_))
                            if k == KD - 1:
                                last.then_inc((slot_done[s] if g_ % 2 else mod_rows).sem, 1)

                def mod_turn(j, bank):
                    wait(mod_rows_copied, l, j + 1)
                    for i in range(GROUP_TILES):
                        last = tr(ps[:, bank, i * P:(i + 1) * P], mrow[:, j % 2, i * P:(i + 1) * P], ident)
                    last.then_inc(mod_turned.sem, 1)

                mod_product(0, 0, range(KD))
                mod_product(1, 1, range(KD))
                wait(layer_x, l, KD)
                vectors()
                mod_turn(0, 2)
                mod_turn(1, 3)

                ACT_TAKES = [0, 2] + list(range(4, 17))

                def project(n, s, c, rows=None, sig=proj_ready):
                    if n >= 4:
                        if n - 4 in ACT_TAKES:
                            wait(proj_act, l, ACT_TAKES.index(n - 4) + 1)
                        else:
                            wait(proj_dve, l, (n - 4) // 2 + 1)
                    for k in range(KD):
                        if n == 0:
                            wait(u_dve if k % 2 else u_act, l, k // 2 + 1)
                        if rows is None:
                            last = mm(ps[:, n % 4, 0:T], slot[s][:, k, c:c + P], uT[:, k, :],
                                      start=(k == 0), stop=(k == KD - 1))
                        else:
                            last = mm(ps[:, n % 4, 0:AW], uT[:, k, rows * P:(rows + 1) * P], slot[s][:, k, c:c + AW],
                                      start=(k == 0), stop=(k == KD - 1))
                    last.then_inc(sig.sem, 1)

                def rotate(n):
                    wait(proj_act, l, 4 + n + 1)
                    if n >= 2:
                        wait(roped, l, n - 1)
                    else:
                        wait(vec_copied if n else lam_done, l, 1)
                    src = (qT if n < HEADS else kT)[:, n % HEADS, SEQ:T]
                    mm(ps[:, 4 + n % 2, 0:LAT], C["rot"], src, start=True, stop=True).then_inc(rot_ready.sem, 1)

                wait(glu_cols_loaded, l, 1)
                for n, c in ((0, 4), (1, 2), (2, 5), (3, 3)):
                    project(n, 0, c * P)
                wait(taps_loaded, l, 1, alone=True)
                for c in range(2):
                    last = tr(ps[:, 5, 32 * c:32 * c + TAPS], dw_rows[0:TAPS, c * P:(c + 1) * P], ident[0:TAPS, 0:TAPS])
                last.then_inc(dw_ready.sem, 1)
                pe.wait_ge(slot_loaded[0].sem, l * (32 * USES[0]) + 64)
                project(4, 0, 0)
                wait(lam_ready, l, 1)
                mm(ps[:, 4, 0:1], C["ones"][0:1, :], lam_s[0:1, 3:4], start=True, stop=True).then_inc(lam_bc.sem, 1)
                project(5, 0, P, sig=slot_done[0])
                pe.wait_ge(slot_loaded[1].sem, l * (32 * USES[1]) + 64)
                for n in range(8):
                    if n == 6:
                        pe.wait_ge(slot_loaded[2].sem, l * (32 * USES[2]) + 64)
                    project(6 + n, 1 + n // 6, (n % 6) * P, sig=slot_done[1] if n == 5 else proj_ready)
                    if n >= 1:
                        rotate(n - 1)
                for t in range(NT):
                    project(14 + t, 2, 2 * P, rows=t, sig=slot_done[2] if t == NT - 1 else proj_ready)
                    if t == 0:
                        rotate(7)
                        mod_product(2, 7, range(KD))
                mod_turn(2, 7)

                wait(proj_act, l, 13)
                wait(mix_loaded, l, 7)
                for h in range(HEADS):
                    last = tr(ps[:, 2, h * P:(h + 1) * P], ck_rows[:, h * P:(h + 1) * P], ident)
                last.then_inc(ck_turned.sem, 1)
                wait(proj_act, l, 14)
                for h in range(HEADS):
                    last = tr(ps[:, 3, h * P:(h + 1) * P], kT[:, h, 0:SEQ], ident)
                last.then_inc(ck_turned.sem, 1)
                wait(conv_done, l, 1)
                for t in range(NT):
                    if t == 2:
                        wait(mod_added, l, 3)
                    a = 0 if t == 0 else CONV_LAT + (t - 1) * P
                    for c in range(2):
                        last = tr(ps[:, 6 + t // 2, (t % 2) * CONV + c * P:(t % 2) * CONV + (c + 1) * P],
                                  cacc[:, c, a:a + P], ident)
                    last.then_inc(crow_ready.sem, 1)

                wait(ck_copied, l, 2)
                wait(roped, l, 8)

                def scores(u):
                    h, t = u // NT, u % NT
                    if u >= 2:
                        wait(scores_used, l, u - 1)
                    for m in range(2):
                        r = slice(64 * m, 64 * m + 64)
                        b = 2 * (u % 2) + m
                        q = qT[r, h, t * P:(t + 1) * P]
                        if t == 0:
                            last = mm(ps[:, b, 0:SEQ], q, kT[r, h, 0:SEQ], start=True, stop=True)
                        else:
                            mm(ps[:, b, 0:LAT], q, kT[r, h, SEQ:T], start=True, stop=True)
                            last = mm(ps[:, b, LAT:LAT + PAST], q, ckT[r, h, :], start=True, stop=True)
                    last.then_inc(scores_ready.sem, 1)

                def turn(u):
                    wait(prob_ready, l, u + 1)
                    if u >= 2:
                        wait(prob_copied, l, u - 1)
                    for k in range(1 if u % NT == 0 else NT):
                        last = tr(ps[:, 4 + u % 2, k * P:(k + 1) * P], probs[:, u % 2, 0, k * P:(k + 1) * P], ident)
                    last.then_inc(prob_turned.sem, 1)

                def values(u):
                    h, t = u // NT, u % NT
                    wait(prob_copied, l, u + 1)
                    if u >= 1:
                        wait(o_copied, l, u)
                    hs = slice(h * VD, (h + 1) * VD)
                    vs = [vrow[:, 0, hs]] if t == 0 else [vrow[:, 1, hs], vrow[:, 2, hs], cv[:, hs]]
                    for k, v in enumerate(vs):
                        last = mm(ps[:, 6, 0:VD], aT[:, u % 2, k, :], v, start=(k == 0), stop=(k == len(vs) - 1))
                    last.then_inc(o_ready.sem, 1)

                wait(proj_act, l, 15)
                NU = HEADS * NT

                def pool_product():
                    wait(pool_done, l, 1)
                    wait(scores_used, l, NU - 1)
                    for c in range(2):
                        mm(ps[:, c, 0:SEQ], pool_blk[:, c, :], sumX[:, c, PP:PP + SEQ], start=True, stop=True)
                        mm(ps[:, c, SEQ:T], pool_blk[:, c, :], sumX[:, c, POOL_LAT:POOL_LAT + LAT],
                           start=True, stop=True).then_inc(pool_ready.sem, 1)

                def conv_back():
                    wait(scores_used, l, NU)
                    for c in range(2):
                        for t in range(NT):
                            last = tr(ps[:, 2 + c, t * P:(t + 1) * P], crow[:, t, c * P:(c + 1) * P], ident)
                        last.then_inc(cback.sem, 1)

                for u in range(NU + 3):
                    if u < NU:
                        scores(u)
                    if u == 3:
                        wait(cln_done, l, 1)
                    if u == NU:
                        pool_product()
                    if u == NU + 1:
                        conv_back()
                    if 2 <= u and u - 2 < NU:
                        turn(u - 2)
                    if u >= 3:
                        values(u - 3)
                    if u in (5, 6):
                        mod_product(3, 7, range(4 * (u - 5), 4 * (u - 5) + 4))
                    elif u == 9:
                        mod_turn(3, 7)
                wait(mod_added, l, MOD_STEPS)
                wait(mix_ready, l, 2)
                for h in range(HEADS):
                    wait(o_normed, l, h + 1)
                    for t in range(NT):
                        last = tr(ps[:, (6 + h) % 8, t * P:(t + 1) * P], orow[:, t, h, :], ident)
                    last.then_inc(o_turned.sem, 1)
                wait(csil_ready, l, 2)
                for n in range(2):
                    for c in range(2):
                        last = mm(ps[:, 4 + n, 0:T], conv_pw[:, c, n * P:(n + 1) * P], csil[:, c, :],
                                  start=(c == 0), stop=(c == 1))
                    last.then_inc(cpw_ready.sem, 1)

                def layer_norm(which, n):
                    wait(z_ready, l, which * KD + n + 1)
                    last = mm(ps[:, 4, 0:T], C["ones"], uT[:, n, :], start=(n == 0), stop=(n == KD - 1))
                    if n == KD - 1:
                        last.then_inc(mean_ready.sem, 1)
                        for m in range(KD):
                            wait(squared, l, which * KD + m + 1)
                            last = mm(ps[:, 5, 0:T], C["ones"], ln_t[:, 2 + m, :], start=(m == 0), stop=(m == KD - 1))
                        last.then_inc(sq_used.sem, 1)

                pe.wait_ge(slot_loaded[3].sem, l * (32 * USES[3]) + 64)
                wait(tail_loaded, l, 1)
                for m in range(KD):
                    if m >= 4:
                        wait(z_ready, l, m - 3)
                    for k in range(KD):
                        if m == 0 and k in (0, 6, 7):
                            wait(mix_ready, l, max(k + 1, 6))
                        wt = slot[3][:, k, m * P:(m + 1) * P] if m < 6 else tail_w[:, k, (m - 6) * P:(m - 5) * P]
                        last = mm(ps[:, m % 4, 0:T], wt, mixT[:, k, :], start=(k == 0), stop=(k == KD - 1))
                    last.then_inc({5: slot_done[3], 7: tail_used}.get(m, y1_ready).sem, 1)
                    if m >= 1:
                        layer_norm(0, m - 1)
                layer_norm(0, KD - 1)

                wait(rt_loaded, l, 4)
                for k in range(KD):
                    wait(u2_dve if k % 2 else u2_act, l, k // 2 + 1)
                    last = mm(ps[0:NG + NE, 6, 0:T], router_w[:, k, :], uT[:, k, :], start=(k == 0), stop=(k == KD - 1))
                last.then_inc(logits_T.sem, 1)
                wait(logits_copied, l, 1, alone=True)
                for t in range(NT):
                    last = tr(ps[:, 5, t * (NG + NE):(t + 1) * (NG + NE)], lgT[:, t * P:(t + 1) * P],
                              ident[0:NG + NE, 0:NG + NE])
                last.then_inc(logits_ready.sem, 1)
                for n in range(6):
                    t, h = n // 2, n % 2
                    if n >= 4:
                        wait(urow_ready, l, n - 3)
                    for m in range(4):
                        last = tr(ps[:, n % 4, m * P:(m + 1) * P], uT[:, 4 * h + m, t * P:(t + 1) * P], ident)
                    last.then_inc(urow_turned.sem, 1)
                wait(assign_ready, l, 1)
                wait(iota_loaded, l, 1)
                mm(ps[:, 7, 0:NT * NE], tri, asg_flat, start=True, stop=False, skip_group_check=True)
                for n in range(NT, 0, -1):
                    last = mm(ps[:, 7, (NT + 1 - n) * NE:(NT + 1) * NE], C["ones"], asg_flat[:, 0:n * NE], start=False,
                              stop=(n == 1), skip_group_check=True)
                last.then_inc(ranks_ready.sem, 1)
                wait(urow_ready, l, 6)

                def chunk_turn():
                    wait(chunk_cols, l, 1)
                    for i in range(2):
                        last = tr(ps[0:1, 6, i * P:(i + 1) * P], chk[:, i:i + 1], ident)
                    last.then_inc(chunk_turned.sem, 1)

                def weighted_turn(t):
                    wait(Pw_ready, l, t + 1)
                    if t >= 1:
                        wait(PT_ready, l, 2 * t)
                    for h in range(2):
                        for s in range(3):
                            last = tr(ps[:, 4 + h, s * P:(s + 1) * P], Pw[:, t % 2, (3 * h + s) * P:(3 * h + s + 1) * P], ident)
                        last.then_inc(Pw_turned.sem, 1)

                for n in range(2 * KD):
                    k, h = n // 2, n % 2
                    if n == 3:
                        chunk_turn()
                    if n in PW_TURNS:
                        weighted_turn(PW_TURNS.index(n))
                    if n >= 4:
                        wait(xs_act if h == 0 else xs_dve, l, k - 1)
                    a, b = GATHERED[h]
                    if n < 2:
                        wait(P_ready, l, (n + 1) * NT)
                    for t in range(NT):
                        last = mm(ps[:, n % 4, 0:b - a], urow[:, t, k * P:(k + 1) * P], Pm[:, t, a:b],
                                  start=(t == 0), stop=(t == NT - 1))
                    last.then_inc(gath_ready.sem, 1)
                wait(xs_act, l, KD)
                wait(xs_dve, l, KD)
                wait(PT_ready, l, 2 * NT)
                wait(chunks_ready, l, 1)
                rounds, halves = rounds_now(pe, l)

                def chunks(n, first, done, used):

                    def gate_up(i):
                        pe.wait_ge(exp_loaded[i].sem, used(i) * 48 + 48)
                        pe.wait_ge(xc_ready.sem, done + l * 2 + (i + 1))
                        pe.wait_ge(h_ready.sem, done + (i + 1))
                        for k in range(KD):
                            for half in range(2):
                                last = mm(ps[W * half:W * (half + 1), i % 2, 0:2 * P].rearrange("p (j f) -> p j f", j=2),
                                          xc[:, i % 2, k, :], gate_up_w[i][:, :, k, half * P:(half + 1) * P],
                                          start=(k == 0), stop=(k == KD - 1), tile_position=(0, W * half))
                                if k == KD - 1:
                                    last.then_inc(gu_ready.sem, 1)

                    def down(i):
                        pe.wait_ge(h_ready.sem, done + (i + 3))
                        pe.wait_ge(hT_ready.sem, done + (i + 1))
                        tr(ps[:, 2 + 5 * (i % 2), 0:P], hrow[:, i % 2, :], ident).then_inc(h_turned.sem, 1)
                        pe.wait_ge(hT_ready.sem, done + (i + 3))
                        pe.wait_ge(y_rows.sem, done + (i + 1))
                        for f in range(2):
                            for half in range(2):
                                last = mm(ps[W * half:W * (half + 1), 3 + i % 2, :], hT[:, i % 2, f * W:(f + 1) * W],
                                          down_w[i][:, f, half * 512:(half + 1) * 512],
                                          start=(f == 0), stop=(f == 1), tile_position=(0, W * half))
                                if f == 1:
                                    last.then_inc((slot_done[i] if half else down_ready).sem, 1)

                    def turn_y(i):
                        pe.wait_ge(y_rows.sem, done + (i + 3))
                        pe.wait_ge(y_placed.sem, done + (i + 1))
                        for c in range(4):
                            last = tr(ps[:, 5 + i % 2, c * P:(c + 1) * P], yrow[:, i % 2, c * P:(c + 1) * P], ident)
                        last.then_inc(y_turned.sem, 1)

                    for i in range(n):
                        gate_up(i)
                        if i >= 1:
                            down(i - 1)
                        if i >= 2:
                            turn_y(i - 2)
                    down(n - 1)
                    turn_y(n - 2)
                    turn_y(n - 1)

                with pe.Fori(0, rounds) as r:
                    chunks(RING, r * RING, (before + r) * RING + halves_before * 2, lambda i: slot_before(i) + r)
                with pe.Fori(0, halves) as r:
                    chunks(2, rounds * RING + r * 2, (before + rounds) * RING + (halves_before + r) * 2,
                           lambda i: slot_before(i) + rounds + r)

                after = (before + rounds) * RING + (halves_before + halves) * 2
                pe.wait_ge(y_placed.sem, after + 2)
                for n in range(2 * ST):
                    s, h = n // 2, n % 2
                    if n >= 4:
                        wait(ys_act if h == 0 else ys_dve, l, s - 1)
                    for m in range(4):
                        last = tr(ps[:, n % 4, m * P:(m + 1) * P], YsT[:, 4 * h + m, s * P:(s + 1) * P], ident)
                    last.then_inc(ys_turned.sem, 1)
                wait(ys_act, l, ST)
                wait(ys_dve, l, ST)
                for m in range(KD):
                    if m >= 4:
                        wait(z_ready, l, KD + m - 3)
                    for s in range(ST):
                        last = mm(ps[:, m % 4, 0:T], Ysr[:, s, m * P:(m + 1) * P], PTw[:, s, :],
                                  start=(s == 0), stop=(s == ST - 1))
                    last.then_inc(y2_ready.sem, 1)
                    if m >= 1:
                        layer_norm(1, m - 1)
                layer_norm(1, KD - 1)

            wait(layer_x, DEPTH, KD)
            for n in range(2 * NT):
                t, h = n // 2, n % 2
                for m in range(4):
                    last = tr(ps[:, n, m * P:(m + 1) * P], xT[:, 4 * h + m, t * P:(t + 1) * P], ident)
                last.then_inc(out_turned.sem, 1)

        @block.scalar
        def _(act):
            wait = engine_wait(act)
            fn = nc.scalar.activation
            ID = ACT.Identity

            act.wait_ge(s_cin.sem, 32)
            fn(krow[0:8, 2 * P:4 * P], krow[0:8, 0:2 * P], ACT.Silu).then_inc(s_crow.sem, 1)
            for m in range(KD):
                act.wait_ge(s_xt.sem, m + 1)
                fn(xT[:, m, :], ps[:, m, 0:T], ID).then_inc(layer_x.sem, 1)
            act.wait_ge(s_cT.sem, 1)
            fn(sT[:, 0:2 * KD].rearrange("p (k v) -> p v k", v=2), ps[:, 0, 0:16].rearrange("p (v k) -> p v k", v=2), ID).then_inc(s_sT.sem, 1)
            act.wait_ge(s_ctl.sem, 4)

            with act.Fori(0, DEPTH) as l:
                before, halves_before, slot_before = rounds_before(act, l)

                def modulate(m, shift, scale, sig):
                    for a, b, v in SEGS:
                        last = fn(uT[:, m, a:b], xT[:, m, a:b], ID, bias=mod(shift + m, v), scale=mod(scale + m, v))
                    last.then_inc(sig.sem, 1)

                def mod_rows_out(j, bank):
                    wait(mod_rows, l, 2 * j + 2)
                    for s, use in zip(MOD_SLOTS[j], MOD_USE[j]):
                        act.wait_ge(slot_done[s].sem, slot_before(s) + l * USES[s] + (use + 1 + 1))
                    if j >= 2:
                        wait(mod_turned, l, j - 1)
                    fn(mrow[:, j % 2, :], ps[:, bank, 0:HALF], ID).then_inc(mod_rows_copied.sem, 1)

                wait(layer_x, l, KD)
                mod_rows_out(0, 0)
                mod_rows_out(1, 1)
                wait(mod_done, l, 1)
                for m in range(0, KD, 2):
                    modulate(m, SH1, SC1, u_act)
                wait(lam_dot, l, 1)
                fn(lam_s[:, 0:2], lam_s[:, 0:2], ACT.Exp).then_inc(lam_exp.sem, 1)

                def proj_wait(n):
                    if n == 5:
                        act.wait_ge(slot_done[0].sem, slot_before(0) + l * USES[0] + (2 + 1))
                    elif n == 11:
                        act.wait_ge(slot_done[1].sem, slot_before(1) + l * USES[1] + (2 + 1))
                    elif n == 16:
                        act.wait_ge(slot_done[2].sem, slot_before(2) + l * USES[2] + (2 + 1))
                    else:
                        wait(proj_ready, l, n + 1 - (n > 5) - (n > 11))

                wait(pads_zero, l, 1)
                for n in (0, 2):
                    proj_wait(n)
                    c = n // 2
                    fn(glu[:, c, CP:CP + SEQ], ps[:, n % 4, 0:SEQ], ACT.Sigmoid)
                    fn(glu[:, c, GLU_LAT:GLU_LAT + LAT], ps[:, n % 4, SEQ:T], ACT.Sigmoid).then_inc(proj_act.sem, 1)
                for n in (4, 5):
                    proj_wait(n)
                    fn(apad[:, n - 4, PP:PP + SEQ], ps[:, n % 4, 0:SEQ], ID)
                    fn(apad[:, n - 4, POOL_LAT:POOL_LAT + LAT], ps[:, n % 4, SEQ:T], ID).then_inc(proj_act.sem, 1)
                for n in range(8):
                    proj_wait(6 + n)
                    fn((qT if n < HEADS else kT)[:, n % HEADS, :], ps[:, (6 + n) % 4, 0:T], ID,
                       scale=HD ** -0.5 if n < HEADS else 1.0).then_inc(proj_act.sem, 1)
                wait(kv_free, l, 0)
                for t in range(NT):
                    proj_wait(14 + t)
                    fn(vrow[:, t, :], ps[:, (14 + t) % 4, 0:AW], ID).then_inc(proj_act.sem, 1)
                    if t == 1:
                        mod_rows_out(2, 7)
                wait(ck_turned, l, 1)
                fn(ckT, ps[:, 2, :].rearrange("p (h t) -> p h t", h=HEADS), ID).then_inc(ck_copied.sem, 1)
                wait(ck_turned, l, 2)
                fn(krow[:], ps[:, 3, :], ID).then_inc(ck_copied.sem, 1)
                wait(cln_var, l, 1)
                fn(cstat[:, :, 2], cstat[:, :, 1], ACT.Sqrt, bias=epsc[:]).then_inc(cln_sd.sem, 1)

                NU = HEADS * NT
                for u in range(NU + 3):
                    if 2 <= u and u - 2 < NU:
                        w_ = u - 2
                        n = P * (1 if w_ % NT == 0 else NT)
                        wait(prob_turned, l, w_ + 1)
                        if w_ >= 2:
                            wait(o_ready, l, w_ - 1)
                        fn(aT[:, w_ % 2].rearrange("p k q -> p (k q)")[:, 0:n], ps[:, 4 + w_ % 2, 0:n], ID).then_inc(prob_copied.sem, 1)
                    if u < NU:
                        n = SEQ if u % NT == 0 else LAT + PAST
                        wait(neg_max, l, u + 1)
                        if u >= 2:
                            wait(prob_turned, l, u - 1)
                        for m in range(2):
                            last = fn(probs[:, u % 2, m, 0:n], ps[:, 2 * (u % 2) + m, 0:n], ACT.Exp,
                                      bias=small[:, u % 2, m, 1:2], accum_out=small[:, u % 2, m, 2:3])
                        last.then_inc(scores_used.sem, 1)
                    if u >= 3:
                        w_ = u - 3
                        wait(o_ready, l, w_ + 1)
                        h, t = w_ // NT, w_ % NT
                        if w_ >= 6:
                            wait(o_squared, l, w_ - 5)
                        fn(sq_out[:, w_ % 6, :], ps[:, 6, 0:VD], ACT.Square,
                           accum_out=rms[:, 0, t * HEADS + h:t * HEADS + h + 1]).then_inc(o_squared.sem, 1)
                        fn(orow[:, t, h, :], ps[:, 6, 0:VD], ID).then_inc(o_copied.sem, 1)
                    if u == 7:
                        mod_rows_out(3, 7)
                    if u == NU + 1:
                        wait(vec_copied, l, 1)
                        for c in range(2):
                            wait(pool_ready, l, c + 1)
                            fn(mixT[:, c, :], ps[:, c, 0:T], ID, scale=vcol("pool_scale", c)).then_inc(mix_ready.sem, 1)

                wait(o_squared, l, NU)
                fn(rms[:, 1, :], rms[:, 0, :], ACT.Sqrt, bias=epsc[:], scale=1.0 / VD).then_inc(rms_sd.sem, 1)
                for c in range(2):
                    wait(cback, l, c + 1)
                    fn(csil[:, c, :], ps[:, 2 + c, 0:T], ACT.Silu, bias=vcol("conv_ln_b", c),
                       scale=vcol("conv_ln_g", c)).then_inc(csil_ready.sem, 1)
                for h in range(HEADS):
                    wait(o_turned, l, h + 1)
                    fn(mixT[:, 2 + h, :], ps[:, (6 + h) % 8, 0:T], ID, scale=subg[:]).then_inc(mix_ready.sem, 1)
                for c in range(2):
                    wait(cpw_ready, l, c + 1)
                    fn(mixT[:, 6 + c, :], ps[:, 4 + c, 0:T], ID).then_inc(mix_ready.sem, 1)

                def scale_x():
                    for m in range(KD):
                        fn(uT[:, m, :], xT[:, m, :], ID, scale=ALPHA).then_inc(x_scaled.sem, 1)

                def squares_root(which):
                    for m in range(KD):
                        wait(centred, l, which * KD + m + 1)
                        fn(ln_t[:, 2 + m, :], uT[:, m, :], ACT.Square).then_inc(squared.sem, 1)
                    wait(sq_used, l, which + 1)
                    fn(ln_t[:, 1, :], ps[:, 5, 0:T], ACT.Sqrt, bias=epsc[:], scale=1.0 / D).then_inc(root_ready.sem, 1)

                scale_x()
                squares_root(0)
                for i in range(KD // 2 + 1):
                    if i < KD // 2:
                        m = 2 * i
                        wait(normed, l, m + 1)
                        fn(xT[:, m, :], uT[:, m, :], ID, bias=vcol("ln1_b", m), scale=vcol("ln1_g", m)).then_inc(x_mid.sem, 1)
                    if i >= 1:
                        wait(x_mid, l, i)
                        modulate(m - 2 if i < KD // 2 else m, SH2, SC2, u2_act)

                wait(logits_T, l, 1)
                fn(lgT, ps[0:NG + NE, 6, 0:T], ID, bias=router_b[:]).then_inc(logits_copied.sem, 1)
                wait(gdiff, l, 1)
                fn(gtmp, gtmp, ACT.Exp).then_inc(gexp.sem, 1)
                wait(out_k, l, 2)
                for n in range(6):
                    t, h = n // 2, n % 2
                    wait(urow_turned, l, n + 1)
                    dst = urow[:, t, :].rearrange("q (k p) -> q p k", k=KD)[:, h * 64:(h + 1) * 64, :]
                    fn(dst, ps[:, n % 4, :].rearrange("q (p k) -> q p k", k=KD), ID).then_inc(urow_ready.sem, 1)
                wait(ediff, l, 1)
                fn(q, q, ACT.Exp).then_inc(eexp.sem, 1)
                for k in range(KD):
                    if 2 * k in PW_TURNS:
                        t = PW_TURNS.index(2 * k)
                        for h in range(2):
                            wait(Pw_turned, l, 2 * t + h + 1)
                            fn(PTw[:, 3 * h:3 * h + 3, t * P:(t + 1) * P],
                               ps[:, 4 + h, 0:3 * P].rearrange("p (s q) -> p s q", s=3), ID).then_inc(PT_ready.sem, 1)
                    wait(gath_ready, l, 2 * k + 1)
                    fn(XsT[:, k, 0:512], ps[:, (2 * k) % 4, 0:512], ID).then_inc(xs_act.sem, 1)

                wait(chunks_ready, l, 1)
                rounds, halves = rounds_now(act, l)

                def chunks(n, first, done, used):

                    def take(i):
                        act.wait_ge(down_ready.sem, done + (i + 1))
                        act.wait_ge(slot_done[i].sem, used(i) + l * USES[i] + (USES[i] + 1 + 1))
                        act.wait_ge(y_turned.sem, done + (i + 1))
                        fn(yrow[:, i % 2, :], ps[:, 3 + i % 2, :], ID).then_inc(y_rows.sem, 1)

                    for i in range(n):
                        act.wait_ge(gu_ready.sem, (done + (i + 3)) * 2)
                        act.wait_ge(h_ready.sem, done + (i + 1))
                        fn(sg[:, i % 2, :], ps[:, i % 2, 0:P], ACT.Silu).then_inc(silu_ready.sem, 1)
                        if i >= 1:
                            take(i - 1)
                    take(n - 1)

                with act.Fori(0, rounds) as r:
                    chunks(RING, r * RING, (before + r) * RING + halves_before * 2, lambda i: slot_before(i) + r)
                with act.Fori(0, halves) as r:
                    chunks(2, rounds * RING + r * 2, (before + rounds) * RING + (halves_before + r) * 2,
                           lambda i: slot_before(i) + rounds + r)

                for s in range(ST):
                    wait(ys_turned, l, 2 * s + 1)
                    fn(Ysr[:, s, 0:512], ps[:, (2 * s) % 4, :], ID).then_inc(ys_act.sem, 1)
                scale_x()
                squares_root(1)
                for m in range(KD):
                    wait(normed, l, KD + m + 1)
                    fn(xT[:, m, :], uT[:, m, :], ID, bias=vcol("ln2_b", m), scale=vcol("ln2_g", m)).then_inc(layer_x.sem, 1)

            for n in range(2 * NT):
                t, h = n // 2, n % 2
                act.wait_ge(out_turned.sem, n + 1)
                fn(xrow[:, t, 512 * h:512 * h + 512], ps[:, n, :], ID).then_inc(out_rows.sem, 1)

        @block.vector
        def _(dve):
            wait = engine_wait(dve)
            v = nc.vector
            before_z = v.memset(before_tab[:], 0)
            before_z.then_inc(s_ctl.sem, 1)
            v.memset(before_f[:], 0.0).then_inc(s_ctl.sem, 1)
            v.memset(sT[:, 2 * KD:], 0.0).then_inc(s_ctl.sem, 1)
            v.memset(epsc[:], EPS).then_inc(s_ctl.sem, 1)
            dve.wait_ge(s_ctl.sem, 4)

            with dve.Fori(0, DEPTH) as l:
                before, halves_before, slot_before = rounds_before(dve, l)
                own = Steps(dve_self)

                def after(n, alone=False):
                    wait(dve_self, l, n, alone)

                wait(vec_loaded, l, len(VECS) + 2)
                pairs = lam_in[:].rearrange("o (a b) d -> o a b d", b=2)
                own.add(v.tensor_tensor(pairs[:, :, 0, :], pairs[:, :, 0, :], pairs[:, :, 1, :], ALU.mult))
                after(own.n)
                v.tensor_reduce(lam_s[:, 0:2], pairs[:, :, 0, :], AX, ALU.add).then_inc(lam_dot.sem, 1)
                wait(layer_x, l, KD)
                v.memset(arena[:, XS + NT * AW + AW + QK:XS + NT * AW + AW + QK + 2 * (POOL_COLS + GLU_COLS)],
                         0.0).then_inc(pads_zero.sem, 1)
                wait(vec_ready, l, 1)
                own.add(v.tensor_copy(vec[:], ps[:, 6, 0:NVEC]))
                after(own.n)

                def mod_add(j, bank):
                    wait(mod_turned, l, j + 1)
                    src = ps[:, bank, 0:HALF].rearrange("p (i g r) -> p g i r", i=GROUP_TILES, g=4)[:, :, :, 0:2]
                    b0 = VCOL["b_mod"] + STEP_TILES * j
                    v.tensor_tensor(modT[:, STEP_TILES * j:STEP_TILES * (j + 1), :].rearrange("p (g i) v -> p g i v", g=4), src,
                                    vec[:, b0:b0 + STEP_TILES].rearrange("p (g i) -> p g i", g=4).unsqueeze(3)
                                    .to_broadcast([P, 4, GROUP_TILES, 2]), ALU.add).then_inc(mod_added.sem, 1)

                def mod_scale(n, scale):
                    wait(mod_added, l, n)
                    v.tensor_scalar(modT[:, scale:scale + KD, :], modT[:, scale:scale + KD, :], 1.0, None,
                                    ALU.add).then_inc(mod_done.sem, 1)

                mod_add(0, 2)
                mod_add(1, 3)
                mod_scale(2, SC1)
                wait(mod_done, l, 1)
                for m in range(1, KD, 2):
                    for a, b, w_ in SEGS:
                        last = v.tensor_scalar(uT[:, m, a:b], xT[:, m, a:b], mod(SC1 + m, w_), mod(SH1 + m, w_),
                                               ALU.mult, ALU.add)
                    last.then_inc(u_dve.sem, 1)
                own.add(v.tensor_scalar(subg[:], vcol("subln_g"), lam_c[:, 1:2], None, ALU.mult))
                wait(lam_exp, l, 1)
                own.add(v.tensor_tensor(lam_s[:, 2:3], lam_s[:, 1:2], lam_s[:, 0:1], ALU.subtract))
                after(own.n)
                v.tensor_tensor(lam_s[:, 3:4], lam_s[:, 2:3], lam_c[0:1, 0:1], ALU.subtract).then_inc(lam_ready.sem, 1)
                for c in range(2):
                    wait(proj_act, l, c + 1)
                    wait(proj_ready, l, 2 * c + 2)
                    bank = 1 + 2 * c
                    v.tensor_tensor(glu[:, c, CP:CP + SEQ], glu[:, c, CP:CP + SEQ], ps[:, bank, 0:SEQ], ALU.mult)
                    v.tensor_tensor(glu[:, c, GLU_LAT:GLU_LAT + LAT], glu[:, c, GLU_LAT:GLU_LAT + LAT], ps[:, bank, SEQ:T],
                                    ALU.mult).then_inc(proj_dve.sem, 1)
                wait(proj_dve, l, 2)
                wait(dw_ready, l, 1)
                v.tensor_copy(dw[:], ps[:, 5, 0:64].rearrange("p (c k) -> p c k", c=2)[:, :, 0:TAPS]).then_inc(vec_copied.sem, 1)
                wait(vec_copied, l, 1)
                wait(lam_bc, l, 1)
                v.tensor_copy(nlam[:], ps[:, 4, 0:1]).then_inc(lam_done.sem, 1)

                conv_steps = [(tap, c) for tap in range(TAPS) for c in range(2)]
                conv_own = []

                def conv_step():
                    tap, c = conv_steps[len(conv_own)]
                    src, wt = glu[:, c, tap:tap + CONV_N], dw[:, c, tap:tap + 1]
                    if tap == 0:
                        conv_own.append(own.add(v.tensor_scalar(cacc[:, c, :], src, wt, None, ALU.mult)))
                    elif len(conv_own) < len(conv_steps) - 1:
                        after(conv_own[-2])
                        conv_own.append(own.add(v.scalar_tensor_tensor(cacc[:, c, :], src, wt, cacc[:, c, :], ALU.mult, ALU.add)))
                    else:
                        after(conv_own[-1])
                        conv_own.append(0)
                        v.scalar_tensor_tensor(cacc[:, c, :], src, wt, cacc[:, c, :], ALU.mult, ALU.add).then_inc(conv_done.sem, 1)

                for _ in range(14):
                    conv_step()
                wait(proj_act, l, 4)
                n = POOL_COLS
                own.add(v.tensor_tensor(sumX[:, :, 1:n], apad[:, :, 0:n - 1], apad[:, :, 1:n], ALU.add))
                after(own.n)
                own.add(v.tensor_tensor(sumY[:, :, 2:n - 1], sumX[:, :, 1:n - 2], sumX[:, :, 3:n], ALU.add))
                inv = C["inv"].rearrange("p (c n) -> p c n", c=2)
                mid = slice(PP, PP + POOL_N)
                lo, hi = slice(0, 64), slice(64, P)
                after(own.n)
                own.add(v.tensor_tensor(sumX[lo, 0, mid], sumX[lo, 0, mid], inv[lo, 0, :], ALU.mult))
                own.add(v.tensor_tensor(sumX[hi, 0, mid], sumY[hi, 0, mid], inv[hi, 0, :], ALU.mult))
                own.add(v.tensor_tensor(sumX[:, 1, 4:n - 3], sumY[:, 1, 2:n - 5], sumY[:, 1, 6:n - 1], ALU.add))
                after(own.n)
                own.add(v.tensor_tensor(sumY[:, 1, mid], sumX[:, 1, PP - 4:PP - 4 + POOL_N], sumX[:, 1, PP + 4:PP + 4 + POOL_N], ALU.add))
                after(own.n)
                own.add(v.tensor_tensor(sumX[lo, 1, mid], sumX[lo, 1, mid], inv[lo, 1, :], ALU.mult))
                own.add(v.tensor_tensor(sumX[hi, 1, mid], sumY[hi, 1, mid], inv[hi, 1, :], ALU.mult))
                after(own.n)
                v.tensor_tensor(sumX[:, :, mid], sumX[:, :, mid], apad[:, :, mid], ALU.subtract).then_inc(pool_done.sem, 1)
                for n in range(8):
                    x = (qT if n < HEADS else kT)[:, n % HEADS, SEQ:T]
                    b = 2 * (n % 2)
                    wait(proj_act, l, 4 + n + 1)
                    if n >= 2:
                        wait(roped, l, n - 1)
                    own.add(v.tensor_tensor(rope_t[:, b, :], x, C["cos"], ALU.mult))
                    wait(rot_ready, l, n + 1)
                    own.add(v.tensor_tensor(rope_t[:, b + 1, :], ps[:, 4 + n % 2, 0:LAT], C["sin"], ALU.mult))
                    after(own.n)
                    v.tensor_tensor(x, rope_t[:, b, :], rope_t[:, b + 1, :], ALU.add).then_inc(roped.sem, 1)
                    for _ in range(6):
                        conv_step()
                mod_add(2, 7)
                for t in range(NT):
                    src = ps[:, 6 + t // 2, (t % 2) * CONV:(t % 2 + 1) * CONV]
                    wait(crow_ready, l, max(t + 1, 2))
                    own.add(v.bn_stats(bstat[:, t, :], src))
                after(own.n, alone=True)
                for t in range(NT):
                    last = v.bn_aggr(cstat[:, t, 0:2], bstat[:, t, :])
                    if t < NT - 1:
                        own.add(last)
                last.then_inc(cln_var.sem, 1)

                def conv_norm():
                    wait(cln_sd, l, 1)
                    own.add(v.reciprocal(cstat[:, :, 3], cstat[:, :, 2]))
                    after(own.n)
                    for t in range(NT):
                        src = ps[:, 6 + t // 2, (t % 2) * CONV:(t % 2 + 1) * CONV]
                        last = v.tensor_scalar(crow[:, t, :], src, cstat[:, t, 0:1], cstat[:, t, 3:4], ALU.subtract, ALU.mult)
                        if t < NT - 1:
                            own.add(last)
                    last.then_inc(cln_done.sem, 1)

                NU = HEADS * NT
                for u in range(NU + 1):
                    if u < NU:
                        n = SEQ if u % NT == 0 else LAT + PAST
                        b = u % 2
                        wait(scores_ready, l, u + 1)
                        v.tensor_reduce(small[:, b, :, 1], ps[:, 2 * b:2 * b + 2, 0:n], AX, ALU.max,
                                        negate=True).then_inc(neg_max.sem, 1)
                    if u == 1:
                        conv_norm()
                    if u >= 1:
                        b = (u - 1) % 2
                        n = SEQ if (u - 1) % NT == 0 else LAT + PAST
                        wait(scores_used, l, u)
                        own.add(v.reciprocal(small[:, b, :, 3], small[:, b, :, 2]))
                        after(own.n)
                        own.add(v.tensor_tensor(small[:, b, 1, 0:1], small[:, b, 1, 3:4], nlam[:], ALU.mult))
                        own.add(v.tensor_scalar(probs[:, b, 0, 0:n], probs[:, b, 0, 0:n], small[:, b, 0, 3:4], None, ALU.mult))
                        after(own.n)
                        v.scalar_tensor_tensor(probs[:, b, 0, 0:n], probs[:, b, 1, 0:n], small[:, b, 1, 0:1],
                                               probs[:, b, 0, 0:n], ALU.mult, ALU.add).then_inc(prob_ready.sem, 1)

                mod_add(3, 7)
                mod_scale(MOD_STEPS, SC2)
                wait(o_copied, l, NU)
                factor = rms[:, 0, :].rearrange("p (t h) -> p t h", t=NT)
                wait(rms_sd, l, 1)
                own.add(v.reciprocal(rms[:, 0, :], rms[:, 1, :]))
                after(own.n)
                for h in range(HEADS):
                    v.tensor_tensor(orow[:, :, h, :], orow[:, :, h, :], factor[:, :, h].unsqueeze(2).to_broadcast([P, NT, VD]),
                                    ALU.mult).then_inc(o_normed.sem, 1)

                def modulate_dve(m, scale, shift, given, n, sig):
                    wait(given, l, n)
                    for a, b, w_ in SEGS:
                        last = v.tensor_scalar(uT[:, m, a:b], xT[:, m, a:b], mod(scale + m, w_), mod(shift + m, w_),
                                               ALU.mult, ALU.add)
                    last.then_inc(sig.sem, 1)

                def residual_norm(which):
                    o = which * KD
                    wait(mod_done, l, 2)
                    for m in range(KD):
                        wait(x_scaled, l, o + m + 1)
                        if which:
                            wait(y2_ready, l, m + 1)
                        elif m == 5:
                            dve.wait_ge(slot_done[3].sem, slot_before(3) + l * USES[3] + (2 + 1))
                        elif m == 7:
                            wait(tail_used, l, 1)
                        else:
                            wait(y1_ready, l, m + 1 - (m > 5))
                        for a, b, w_ in SEGS:
                            last = v.scalar_tensor_tensor(uT[:, m, a:b], ps[:, m % 4, a:b], mod((GA2 if which else GA1) + m, w_),
                                                          uT[:, m, a:b], ALU.mult, ALU.add)
                        last.then_inc(z_ready.sem, 1)
                    wait(mean_ready, l, which + 1)
                    wait(z_ready, l, o + KD)
                    for m in range(KD):
                        v.scalar_tensor_tensor(uT[:, m, :], ps[:, 4, 0:T], -1.0 / D, uT[:, m, :], ALU.mult, ALU.add).then_inc(centred.sem, 1)
                    wait(root_ready, l, which + 1)
                    own.add(v.reciprocal(ln_t[:, 0, :], ln_t[:, 1, :]))
                    after(own.n)
                    wait(centred, l, o + KD)
                    for m in range(KD):
                        v.tensor_tensor(uT[:, m, :], uT[:, m, :], ln_t[:, 0, :], ALU.mult).then_inc(normed.sem, 1)

                residual_norm(0)
                for m in range(1, KD, 2):
                    wait(normed, l, m + 1)
                    v.tensor_scalar(xT[:, m, :], uT[:, m, :], vcol("ln1_g", m), vcol("ln1_b", m), ALU.mult,
                                    ALU.add).then_inc(x_mid_dve.sem, 1)
                    if m >= 3:
                        modulate_dve(m - 2, SC2, SH2, x_mid_dve, m // 2, u2_dve)
                modulate_dve(KD - 1, SC2, SH2, x_mid_dve, KD // 2, u2_dve)

                def bc(x, n):
                    return x.unsqueeze(2).to_broadcast([P, NT, n])

                def bt(x, n):
                    return x.unsqueeze(1).to_broadcast([P, NT, n])

                def step(ins):
                    own.add(ins)
                    after(own.n)

                def first_max(vals, n, mx, cmx, onehot):
                    rank = bt(C["rank"][:, NE - n:NE], n)
                    step(v.tensor_reduce(mx, vals, AX, ALU.max))
                    step(v.tensor_tensor(onehot, vals, bc(mx, n), ALU.is_equal))
                    step(v.tensor_tensor(onehot, onehot, rank, ALU.mult))
                    step(v.tensor_reduce(cmx, onehot, AX, ALU.max))
                    step(v.tensor_tensor(onehot, onehot, bc(cmx, n), ALU.is_equal))

                wait(logits_ready, l, 1)
                step(v.tensor_copy(lg, ps[:, 5, 0:NT * (NG + NE)].rearrange("p (t n) -> p t n", t=NT)))
                first_max(lg[:, :, 0:NG], NG, gmax, gcm, og)
                v.tensor_tensor(gtmp, lg[:, :, 0:NG], bc(gmax, NG), ALU.subtract).then_inc(gdiff.sem, 1)
                step(v.tensor_scalar(og, og, BIG, -BIG, ALU.mult, ALU.add))
                e4 = lg[:, :, NG:].rearrange("p t (g e) -> p t g e", g=NG)
                step(v.tensor_tensor(e4, e4, og.unsqueeze(3).to_broadcast([P, NT, NG, EPG]), ALU.add))
                el = lg[:, :, NG:]
                first_max(el, NE, m1, c1, o1)
                step(v.scalar_tensor_tensor(etmp, o1, -3 * BIG, el, ALU.mult, ALU.add))
                first_max(etmp, NE, m2, c2, o2)
                v.tensor_tensor(asg, o1, o2, ALU.add).then_inc(assign_ready.sem, 1)
                v.tensor_tensor(q, m2, m1, ALU.subtract).then_inc(ediff.sem, 1)
                wait(ranks_ready, l, 1)
                step(v.tensor_copy(tot[:, 0:NE], ps[:, 7, NT * NE:(NT + 1) * NE]))
                ones32 = C["ones"][:, 0:NE]
                step(v.tensor_tensor_scan(start[:, 0:NE], ones32, tot[:, 0:NE], 0.0, ALU.mult, ALU.add))
                step(v.tensor_tensor(start[:, 0:NE], start[:, 0:NE], tot[:, 0:NE], ALU.subtract))
                step(v.tensor_tensor(etmp, ps[:, 7, 0:NE * NT].rearrange("p (t n) -> p t n", t=NT),
                                     bt(start[:, 0:NE], NE), ALU.add))
                own.add(v.tensor_tensor(o1, o1, etmp, ALU.mult))
                step(v.tensor_tensor(o2, o2, etmp, ALU.mult))
                own.add(v.tensor_reduce(s1, o1, AX, ALU.add))
                step(v.tensor_reduce(s2, o2, AX, ALU.add))
                wait(iota_loaded, l, 1)
                for a, b in GATHERED:
                    for t in range(NT):
                        step(v.tensor_scalar(Pm[:, t, a:b], iota[:, a:b], s1[:, t:t + 1], None, ALU.is_equal))
                        v.scalar_tensor_tensor(Pm[:, t, a:b], iota[:, a:b], s2[:, t:t + 1], Pm[:, t, a:b], ALU.is_equal,
                                               ALU.add).then_inc(P_ready.sem, 1)
                own.add(v.memset(le[:, NE:NE + 1], 0.0))
                step(v.tensor_scalar(ce[:, 0:NE], tot[:, 0:NE], 0.0, None, ALU.is_gt))
                for j in range(1, -(-T // W)):
                    step(v.scalar_tensor_tensor(ce[:, 0:NE], tot[:, 0:NE], float(W * j), ce[:, 0:NE], ALU.is_gt, ALU.add))
                step(v.tensor_tensor_scan(cb[:, 0:NE], ones32, ce[:, 0:NE], 0.0, ALU.mult, ALU.add))
                nchunks = cb[:, NE:NE + 1]
                step(v.tensor_copy(nchunks, cb[:, NE - 1:NE]))
                step(v.tensor_tensor(cb[:, 0:NE], cb[:, 0:NE], ce[:, 0:NE], ALU.subtract))
                step(v.tensor_scalar(le[:, 0:NE], cb[:, 0:NE], C["kk"], None, ALU.is_le))
                step(v.tensor_reduce(chk[:, 2:3], le[:, 0:NE], AX, ALU.add))
                step(v.tensor_scalar(chk[:, 0:1], chk[:, 2:3], -1.0, None, ALU.add))
                step(v.tensor_tensor(dd[:, 0:NE], le[:, 0:NE], le[:, 1:NE + 1], ALU.subtract))
                step(v.scalar_tensor_tensor(ce[:, 0:NE], cb[:, 0:NE], float(-W), start[:, 0:NE], ALU.mult, ALU.add))
                step(v.tensor_tensor(ce[:, 0:NE], ce[:, 0:NE], dd[:, 0:NE], ALU.mult))
                step(v.tensor_reduce(chk[:, 2:3], ce[:, 0:NE], AX, ALU.add))
                step(v.tensor_scalar(chk[:, 3:4], C["kk"], float(W), chk[:, 2:3], ALU.mult, ALU.add))
                v.tensor_scalar(chk[:, 1:2], chk[:, 3:4], float(PAIRS), None, ALU.min).then_inc(chunk_cols.sem, 1)
                MR = MAX_ROUNDS
                step(v.tensor_scalar(rnd[:, 0:MR], C["rounds"], nchunks, None, ALU.is_lt))
                step(v.tensor_reduce(rnd[:, MR + 2:], rnd[:, 0:MR], AX, ALU.add))
                step(v.tensor_scalar(rnd[:, MR:MR + 1], rnd[:, MR + 2:], -1.0, None, ALU.add))
                step(v.scalar_tensor_tensor(rnd[:, MR + 1:MR + 2], rnd[:, MR:MR + 1], float(-RING), nchunks, ALU.mult, ALU.add))
                step(v.tensor_scalar(rnd[:, MR + 1:MR + 2], rnd[:, MR + 1:MR + 2], 2.0, 1.0, ALU.is_gt, ALU.add))
                counts = rnd[0:1, MR:MR + 2].unsqueeze(2)
                step(v.tensor_copy(rounds_tab[:, :, ds(l, 1)], counts))
                step(v.tensor_tensor(before_f[:, :, ds(l + 1, 1)], before_f[:, :, ds(l, 1)], counts, ALU.add))
                step(v.tensor_copy(before_tab[:, :, ds(l + 1, 1)], before_f[:, :, ds(l + 1, 1)]))
                wait(chunk_turned, l, 1)
                v.tensor_copy(chunk_tab[:], ps[0:1, 6, 0:2 * P].rearrange("p (i n) -> p i n", i=2)
                              [:, :, 0:LISTED]).then_inc(chunks_ready.sem, 1)
                wait(gexp, l, 1)
                step(v.tensor_reduce(gsum, gtmp, AX, ALU.add))
                step(v.reciprocal(gw, gsum))
                wait(eexp, l, 1)
                step(v.tensor_scalar(rq, q, 1.0, None, ALU.add))
                step(v.reciprocal(cm, rq))
                step(v.tensor_tensor(w1, gw, cm, ALU.mult))
                step(v.tensor_tensor(w2, w1, q, ALU.mult))

                def weighted(t):
                    if t >= 2:
                        wait(Pw_turned, l, 2 * (t - 1))
                    if t >= 1:
                        wait(Pw_ready, l, t)
                    tmp = tail[:, 0:PAIRS]
                    own.add(v.tensor_scalar(tmp, iota, s1[:, t:t + 1], w1[:, t:t + 1], ALU.is_equal, ALU.mult))
                    step(v.tensor_scalar(Pw[:, t % 2, :], iota, s2[:, t:t + 1], w2[:, t:t + 1], ALU.is_equal, ALU.mult))
                    v.tensor_tensor(Pw[:, t % 2, :], Pw[:, t % 2, :], tmp, ALU.add).then_inc(Pw_ready.sem, 1)

                own.add(v.memset(XsT[:, :, PAIRS:PADDED], 0.0))
                for k in range(KD):
                    wait(gath_ready, l, 2 * k + 2)
                    if k == 0:
                        after(own.n)
                    v.tensor_copy(XsT[:, k, 512:PAIRS], ps[:, (2 * k + 1) % 4, 0:PAIRS - 512]).then_inc(xs_dve.sem, 1)
                    if k in (1, 2, 4):
                        weighted((1, 2, 4).index(k))

                rounds, halves = rounds_now(dve, l)

                def copy_x(j, done, i, start=False):
                    off = dve.value_load(chunk_tab[0:1, 1, ds(j, 1)], min_val=0, max_val=PAIRS)
                    if start:
                        wait(xs_act, l, KD)
                        wait(xs_dve, l, KD)
                        wait(Pw_ready, l, NT)
                    dve.wait_ge(gu_ready.sem, (done + (i + 1)) * 2)
                    v.tensor_copy(xc[:, i % 2], XsT[:, :, ds(off, W)]).then_inc(xc_ready.sem, 1)

                def chunks(n, first, done, used):

                    def hidden(i):
                        dve.wait_ge(silu_ready.sem, done + (i + 1))
                        dve.wait_ge(h_turned.sem, done + (i + 1))
                        v.tensor_tensor(hrow[:, i % 2, :], sg[:, i % 2, :], ps[:, i % 2, P:2 * P], ALU.mult).then_inc(h_ready.sem, 1)
                        dve.wait_ge(h_turned.sem, done + (i + 3))
                        v.tensor_copy(hT[:, i % 2, :], ps[:, 2 + 5 * (i % 2), 0:P]).then_inc(hT_ready.sem, 1)

                    def place(i):
                        off = dve.value_load(chunk_tab[0:1, 1, ds(first + i, 1)], min_val=0, max_val=PAIRS)
                        dve.wait_ge(y_turned.sem, done + (i + 3))
                        dve.wait_ge(y_placed.sem, done + (i + 2))
                        v.tensor_copy(YsT[:, :, ds(off, W)].rearrange("p (h c) n -> p h c n", h=2),
                                      ps[:, 5 + i % 2, :].rearrange("p (c h n) -> p h c n", c=4, h=2)).then_inc(y_placed.sem, 1)

                    for i in range(n):
                        hidden(i)
                        copy_x(first + (i + 2), done, i + 2)
                        if i >= 1:
                            place(i - 1)
                    place(n - 1)

                for i in range(2):
                    copy_x(i, before * RING + halves_before * 2, i, start=(i == 0))
                with dve.Fori(0, rounds) as r:
                    chunks(RING, r * RING, (before + r) * RING + halves_before * 2, lambda i: slot_before(i) + r)
                with dve.Fori(0, halves) as r:
                    chunks(2, rounds * RING + r * 2, (before + rounds) * RING + (halves_before + r) * 2,
                           lambda i: slot_before(i) + rounds + r)

                for s in range(ST):
                    wait(ys_turned, l, 2 * s + 2)
                    v.tensor_copy(Ysr[:, s, 512:1024], ps[:, (2 * s + 1) % 4, :]).then_inc(ys_dve.sem, 1)
                residual_norm(1)
                own.check()


_INPUTS = ["x_prompt", "x_sample", "cache_k", "cache_v", "c", "c_ctx", "w_mod", "b_mod", "w_in", "w_out", "pool_w",
           "pool_scale", "diff_lambda", "subln_g", "conv_dw", "conv_ln_g", "conv_ln_b", "conv_pw", "ln1_g", "ln1_b",
           "ln2_g", "ln2_b", "router_grp", "router_grp_b", "router_exp", "router_exp_b", "w_gate", "w_up", "w_down"]
_OUTPUTS = [(1, SEQ, D), (1, LAT, D), (1, DEPTH, SEQ, HEADS, 2, HD), (1, DEPTH, SEQ, HEADS, VD)]


def kernel(**inputs):
    import concourse.bacc as bacc
    from concourse.bass_utils import run_bass_kernel_spmd as run

    nc = bacc.Bacc("TRN2", target_bir_lowering=False, num_devices=1)
    arrays, aps = {}, {}

    def add(name, a):
        a = np.ascontiguousarray(a)
        arrays[f"in_{name}"] = a
        aps[name] = nc.dram_tensor(f"in_{name}", a.shape, mybir.dt.from_np(a.dtype), kind="ExternalInput").ap()

    for name in _INPUTS:
        add(name, inputs[name])
    table, iota, lam = shape_constants()
    add("consts", table)
    add("iota", iota)
    add("lam", lam)
    outs = [nc.dram_tensor(f"out_{i}", s, F32, kind="ExternalOutput").ap() for i, s in enumerate(_OUTPUTS)]
    build(nc, aps, aps["consts"], aps["iota"], aps["lam"], *outs)
    r = run(nc, [arrays], core_ids=[0])
    return tuple(r.results[0][f"out_{i}"] for i in range(len(_OUTPUTS)))
```
